# Optimizing a Trainium2 kernel written in Bass

```python
import math
import jax, jax.numpy as jnp
from jax import lax
import numpy as np

D_MODEL = 1024
BATCH = 1
SEQ = 512
DEPTH = 1

GRID_W = 64
CTX_LEN = 256

SSD_EXPAND = 2
D_INNER = SSD_EXPAND * D_MODEL
SSD_HEADDIM = 64
SSD_HEADS = D_INNER // SSD_HEADDIM
SSD_GROUPS = 4
SSD_STATE = 128
SSD_CONV = 5
SSD_CHUNK = 128
D_BC = SSD_GROUPS * SSD_STATE
D_XBC = D_INNER + 2 * D_BC

POOL_WINDOWS = (2, 4, 8, 16)
POOL_WIDTH = D_MODEL
POOL_GROUPS = len(POOL_WINDOWS)
POOL_GROUP_DIM = POOL_WIDTH // POOL_GROUPS

IN_SPLITS = (D_INNER, D_INNER + D_XBC, D_INNER + D_XBC + 2 * SSD_HEADS,
             D_INNER + D_XBC + 2 * SSD_HEADS + POOL_WIDTH)
IN_COLS = IN_SPLITS[-1] + 2 * D_MODEL

MOE_GROUPS = 4
MOE_EXPERTS_PER_GROUP = 8
MOE_EXPERTS = MOE_GROUPS * MOE_EXPERTS_PER_GROUP
MOE_TOP_K = 2
D_EXPERT = 512
MOE_BLOCK = 256

DEEPNORM_ALPHA = (2.0 * DEPTH) ** 0.25
DEEPNORM_BETA = (8.0 * DEPTH) ** -0.25
NORM_EPS = 1e-5


def layer_norm(x, g, b):
    xf = x.astype(jnp.float32)
    mu = xf.mean(-1, keepdims=True)
    var = jnp.square(xf - mu).mean(-1, keepdims=True)
    return ((xf - mu) * lax.rsqrt(var + NORM_EPS) * g.astype(jnp.float32) + b.astype(jnp.float32)).astype(x.dtype)

def post_norm(x, y, g, b):
    return layer_norm(DEEPNORM_ALPHA * x + y, g, b)

def modulate(x, shift, scale):
    return x * (1 + scale) + shift

def rms_norm_gated(y, z, g):
    yz = y.astype(jnp.float32) * jax.nn.silu(z.astype(jnp.float32))
    return yz * lax.rsqrt(jnp.mean(yz * yz, -1, keepdims=True) + NORM_EPS) * g.astype(jnp.float32)

def flip_seq(t):
    return t[:, ::-1]

def conv_centred(u, w, b):
    ch = u.shape[-1]
    y = lax.conv_general_dilated(u, w[:, None, :].astype(u.dtype), window_strides=(1,),
                                 padding=((SSD_CONV // 2, SSD_CONV // 2),),
                                 dimension_numbers=('NWC', 'WIO', 'NWC'), feature_group_count=ch)
    return y + b

def ssd_decay(dt_raw, lp):
    b, l, _ = dt_raw.shape
    dt = jax.nn.softplus(dt_raw.reshape(b, l, 2, SSD_HEADS).astype(jnp.float32) + lp['dt_bias'].astype(jnp.float32))
    a = dt * -jnp.exp(lp['a_log'].astype(jnp.float32))
    return dt, a

def ssd_scan(xdt, a, bm, cm, h0):
    b, l = a.shape[:2]
    r = SSD_HEADS // SSD_GROUPS
    q = SSD_CHUNK
    nc = l // q

    def chunks(t):
        return jnp.moveaxis(t.reshape((b, nc, q) + t.shape[2:]), 1, 0)

    xs = (chunks(xdt.reshape(b, l, SSD_GROUPS, r, SSD_HEADDIM)), chunks(a.reshape(b, l, SSD_GROUPS, r)),
          chunks(bm), chunks(cm))
    lower = jnp.tril(jnp.ones((q, q), dtype=bool))[None, :, :, None, None]

    def step(state, inp):
        xc, ac, bc, cc = inp
        acs = jnp.cumsum(ac, axis=1)
        seg = acs[:, :, None] - acs[:, None, :]
        decay = jnp.exp(jnp.where(lower, seg, -jnp.inf))
        cb = jnp.einsum('bign,bjgn->bijg', cc, bc)
        y_diag = jnp.einsum('bijg,bijgr,bjgrp->bigrp', cb, decay, xc)
        y_off = jnp.einsum('bign,bgrpn->bigrp', cc, state) * jnp.exp(acs)[..., None]
        tail = jnp.exp(acs[:, -1:] - acs)
        state = state * jnp.exp(acs[:, -1])[..., None, None] + jnp.einsum('bjgn,bjgr,bjgrp->bgrpn', bc, tail, xc)
        return state, y_diag + y_off

    h_final, ys = lax.scan(step, h0.reshape(b, SSD_GROUPS, r, SSD_HEADDIM, SSD_STATE), xs)
    y = jnp.moveaxis(ys, 0, 1).reshape(b, l, SSD_HEADS, SSD_HEADDIM)
    return y, h_final.reshape(b, SSD_HEADS, SSD_HEADDIM, SSD_STATE)

def ssd_final_state(xdt, a, bm):
    b, l = a.shape[:2]
    r = SSD_HEADS // SSD_GROUPS
    acs = jnp.cumsum(a, axis=1)
    tail = jnp.exp(acs[:, -1:] - acs).reshape(b, l, SSD_GROUPS, r)
    st = jnp.einsum('blgn,blgr,blgrp->bgrpn', bm, tail, xdt.reshape(b, l, SSD_GROUPS, r, SSD_HEADDIM))
    return st.reshape(b, SSD_HEADS, SSD_HEADDIM, SSD_STATE)

def ssd_branch(z, xbc, dt_raw, lp, h0_f, h0_b):
    b, l, _ = z.shape
    xbc = jax.nn.silu(conv_centred(xbc, lp['conv_w'], lp['conv_b'])).astype(jnp.float32)
    xs, bm, cm = jnp.split(xbc, (D_INNER, D_INNER + D_BC), axis=-1)
    xs = xs.reshape(b, l, SSD_HEADS, SSD_HEADDIM)
    bm = bm.reshape(b, l, SSD_GROUPS, SSD_STATE)
    cm = cm.reshape(b, l, SSD_GROUPS, SSD_STATE)
    dt, a = ssd_decay(dt_raw, lp)
    y_f, s_f = ssd_scan(xs * dt[:, :, 0, :, None], a[:, :, 0], bm, cm, h0_f)
    y_b, s_b = ssd_scan(flip_seq(xs * dt[:, :, 1, :, None]), flip_seq(a[:, :, 1]), flip_seq(bm), flip_seq(cm), h0_b)
    y = y_f + flip_seq(y_b) + xs * lp['d_skip'].astype(jnp.float32)[:, None]
    y = rms_norm_gated(y.reshape(b, l, D_INNER), z, lp['ssd_norm_g'])
    return y.astype(z.dtype), s_f, s_b

def ssd_context_states(hc, lp):
    b, l, _ = hc.shape
    w = lp['w_in']
    xb = hc @ w[:, IN_SPLITS[0]:IN_SPLITS[0] + D_INNER + D_BC]
    dt_raw = hc @ w[:, IN_SPLITS[1]:IN_SPLITS[2]]
    xb = jax.nn.silu(conv_centred(xb, lp['conv_w'][:, :D_INNER + D_BC], lp['conv_b'][:D_INNER + D_BC])).astype(jnp.float32)
    xs, bm = jnp.split(xb, (D_INNER,), axis=-1)
    xs = xs.reshape(b, l, SSD_HEADS, SSD_HEADDIM)
    bm = bm.reshape(b, l, SSD_GROUPS, SSD_STATE)
    dt, a = ssd_decay(dt_raw, lp)
    s_f = ssd_final_state(xs * dt[:, :, 0, :, None], a[:, :, 0], bm)
    s_b = ssd_final_state(flip_seq(xs * dt[:, :, 1, :, None]), flip_seq(a[:, :, 1]), flip_seq(bm))
    return s_f, s_b

def window_sum(u, axis, k):
    n = u.shape[axis]
    pad = [(0, 0)] * u.ndim
    pad[axis] = (1, 0)
    cs = jnp.cumsum(jnp.pad(u, pad), axis=axis)
    pos = jnp.arange(n)
    lo = jnp.clip(pos - k // 2, 0, n)
    hi = jnp.clip(pos - k // 2 + k, 0, n)
    s = jnp.take(cs, hi, axis=axis) - jnp.take(cs, lo, axis=axis)
    return s, (hi - lo).astype(jnp.float32)

def pool_grid(uf):
    b, l = uf.shape[:2]
    rows = l // GRID_W
    ug_all = uf.reshape(b, rows, GRID_W, POOL_GROUPS, POOL_GROUP_DIM)
    outs = []
    for gi, k in enumerate(POOL_WINDOWS):
        ug = ug_all[:, :, :, gi]
        s, cnt_r = window_sum(ug, 1, k)
        s, cnt_c = window_sum(s, 2, k)
        outs.append(s / (cnt_r[:, None] * cnt_c[None, :])[None, :, :, None])
    return jnp.stack(outs, axis=3).reshape(b, l, POOL_GROUPS, POOL_GROUP_DIM)

def pool_seq(uf):
    outs = []
    for gi, k in enumerate(POOL_WINDOWS):
        s, cnt = window_sum(uf[:, :, gi], 1, k)
        outs.append(s / cnt[None, :, None])
    return jnp.stack(outs, axis=2)

def pool_branch(u, lp, on_grid):
    b, l, _ = u.shape
    uf = u.astype(jnp.float32).reshape(b, l, POOL_GROUPS, POOL_GROUP_DIM)
    mean = pool_grid(uf) if on_grid else pool_seq(uf)
    y = jnp.einsum('blgc,gcd->blgd', mean - uf, lp['pool_w'].astype(jnp.float32)).reshape(b, l, POOL_WIDTH)
    return (y * lp['pool_scale'].astype(jnp.float32)).astype(u.dtype)

def mix_stream(h, lp, on_grid, h0_f, h0_b):
    z, xbc, dt_raw, u, gates = jnp.split(h @ lp['w_in'], IN_SPLITS, axis=-1)
    y_a, s_f, s_b = ssd_branch(z, xbc, dt_raw, lp, h0_f, h0_b)
    y_p = pool_branch(u, lp, on_grid)
    g = jax.nn.sigmoid((gates + lp['b_gate']).astype(jnp.float32)).astype(h.dtype)
    g_a, g_p = jnp.split(g, 2, axis=-1)
    merged = g_a * (y_a @ lp['w_branch_a']) + g_p * (y_p @ lp['w_branch_b'])
    return merged @ lp['w_out'], s_f, s_b

def swiglu(xb, wg, wu, wd):
    return (jax.nn.silu(xb @ wg) * (xb @ wu)) @ wd

def hier_moe(h, lp):
    t, d = h.shape
    hf = h.astype(jnp.float32)
    lg = hf @ lp['w_rg'].astype(jnp.float32) + lp['b_rg'].astype(jnp.float32)
    grp = jnp.argmax(lg, axis=-1)
    p_grp = jnp.take_along_axis(jax.nn.softmax(lg, axis=-1), grp[:, None], axis=-1)
    le = jnp.einsum('td,gde->tge', hf, lp['w_re'].astype(jnp.float32)) + lp['b_re'].astype(jnp.float32)
    le = jnp.take_along_axis(le, grp[:, None, None], axis=1)[:, 0]
    top_v, top_i = lax.top_k(le, MOE_TOP_K)
    w = p_grp * jax.nn.softmax(top_v, axis=-1)
    eid = grp[:, None].astype(jnp.int32) * MOE_EXPERTS_PER_GROUP + top_i.astype(jnp.int32)
    n_assign = t * MOE_TOP_K
    flat_e = eid.reshape(-1)
    flat_t = jnp.repeat(jnp.arange(t, dtype=jnp.int32), MOE_TOP_K)
    order = jnp.argsort(flat_e)
    se, st, sw = flat_e[order], flat_t[order], w.reshape(-1)[order]
    counts = jnp.bincount(flat_e, length=MOE_EXPERTS)
    padded = (counts + MOE_BLOCK - 1) // MOE_BLOCK * MOE_BLOCK
    pad_end = jnp.cumsum(padded)
    pad_start = pad_end - padded
    start = jnp.cumsum(counts) - counts
    dest = pad_start[se] + jnp.arange(n_assign, dtype=jnp.int32) - start[se]
    n_blocks = -(-n_assign // MOE_BLOCK) + MOE_EXPERTS
    n_rows = n_blocks * MOE_BLOCK
    row_tok = jnp.full((n_rows,), t, jnp.int32).at[dest].set(st)
    block_e = jnp.minimum(jnp.searchsorted(pad_end, jnp.arange(n_blocks, dtype=jnp.int32) * MOE_BLOCK, side='right'),
                          MOE_EXPERTS - 1)
    h_pad = jnp.concatenate([h, jnp.zeros((1, d), h.dtype)], axis=0)
    xin = h_pad[row_tok].reshape(n_blocks, MOE_BLOCK, d)

    def expert_block(args):
        xb, e = args
        return swiglu(xb, lp['w_eg'][e], lp['w_eu'][e], lp['w_ed'][e])

    yb = lax.map(expert_block, (xin, block_e)).reshape(n_rows, d)
    return jax.ops.segment_sum(yb[dest] * sw[:, None].astype(h.dtype), st, num_segments=t)

def first_inputs(seed: int = 0) -> dict:
    key = jax.random.key(seed)
    ks = jax.random.split(key, 32)
    f32 = jnp.float32
    L, D = DEPTH, D_MODEL

    def nrm(k, shape, scale):
        return jax.random.normal(k, shape, f32) * scale

    dt0 = jnp.exp(jax.random.uniform(ks[8], (L, 2, SSD_HEADS), f32, math.log(1e-3), math.log(1e-1)))
    return {
        'x': nrm(ks[0], (BATCH, SEQ, D), 1.0),
        'c': nrm(ks[1], (BATCH, D), 1.0),
        'ctx': nrm(ks[2], (BATCH, CTX_LEN, D), 1.0),
        'c_ctx': nrm(ks[3], (D,), 1.0),
        'w_ada': nrm(ks[4], (L, D, 6 * D), D ** -0.5),
        'b_ada': nrm(ks[5], (L, 6 * D), 0.02),
        'w_in': nrm(ks[6], (L, D, IN_COLS), D ** -0.5),
        'b_gate': nrm(ks[7], (L, 2 * D), 0.1),
        'conv_w': nrm(ks[9], (L, SSD_CONV, D_XBC), SSD_CONV ** -0.5),
        'conv_b': nrm(ks[10], (L, D_XBC), 0.02),
        'dt_bias': dt0 + jnp.log(-jnp.expm1(-dt0)),
        'a_log': jnp.log(jax.random.uniform(ks[11], (L, 2, SSD_HEADS), f32, 1.0, 16.0)),
        'd_skip': 1.0 + nrm(ks[12], (L, SSD_HEADS), 0.1),
        'ssd_norm_g': 1.0 + nrm(ks[13], (L, D_INNER), 0.1),
        'pool_w': nrm(ks[14], (L, POOL_GROUPS, POOL_GROUP_DIM, POOL_GROUP_DIM), POOL_GROUP_DIM ** -0.5),
        'pool_scale': 1.0 + nrm(ks[15], (L, POOL_WIDTH), 0.1),
        'w_branch_a': nrm(ks[16], (L, D_INNER, D), D_INNER ** -0.5),
        'w_branch_b': nrm(ks[17], (L, POOL_WIDTH, D), POOL_WIDTH ** -0.5),
        'w_out': nrm(ks[18], (L, D, D), D ** -0.5 * DEEPNORM_BETA),
        'ln1_g': 1.0 + nrm(ks[19], (L, D), 0.1),
        'ln1_b': nrm(ks[20], (L, D), 0.02),
        'ln2_g': 1.0 + nrm(ks[21], (L, D), 0.1),
        'ln2_b': nrm(ks[22], (L, D), 0.02),
        'w_router_group': nrm(ks[23], (L, D, MOE_GROUPS), D ** -0.5),
        'b_router_group': nrm(ks[24], (L, MOE_GROUPS), 0.01),
        'w_router_expert': nrm(ks[25], (L, MOE_GROUPS, D, MOE_EXPERTS_PER_GROUP), D ** -0.5),
        'b_router_expert': nrm(ks[26], (L, MOE_GROUPS, MOE_EXPERTS_PER_GROUP), 0.01),
        'w_expert_gate': nrm(ks[27], (L, MOE_EXPERTS, D, D_EXPERT), D ** -0.5),
        'w_expert_up': nrm(ks[28], (L, MOE_EXPERTS, D, D_EXPERT), D ** -0.5),
        'w_expert_down': nrm(ks[29], (L, MOE_EXPERTS, D_EXPERT, D), D_EXPERT ** -0.5 * DEEPNORM_BETA),
    }

def first_block(x, c, ctx, c_ctx, w_ada, b_ada, w_in, b_gate, conv_w, conv_b, dt_bias, a_log, d_skip,
              ssd_norm_g, pool_w, pool_scale, w_branch_a, w_branch_b, w_out, ln1_g, ln1_b, ln2_g, ln2_b,
              w_router_group, b_router_group, w_router_expert, b_router_expert,
              w_expert_gate, w_expert_up, w_expert_down):
    b, l, d = x.shape
    lc = ctx.shape[1]
    xl, xc = x, ctx
    zero_state = jnp.zeros((b, SSD_HEADS, SSD_HEADDIM, SSD_STATE), jnp.float32)
    for i in range(DEPTH):
        last = i == DEPTH - 1
        lp = {'w_in': w_in[i], 'b_gate': b_gate[i], 'conv_w': conv_w[i], 'conv_b': conv_b[i],
              'dt_bias': dt_bias[i], 'a_log': a_log[i], 'd_skip': d_skip[i], 'ssd_norm_g': ssd_norm_g[i],
              'pool_w': pool_w[i], 'pool_scale': pool_scale[i], 'w_branch_a': w_branch_a[i],
              'w_branch_b': w_branch_b[i], 'w_out': w_out[i],
              'w_rg': w_router_group[i], 'b_rg': b_router_group[i],
              'w_re': w_router_expert[i], 'b_re': b_router_expert[i],
              'w_eg': w_expert_gate[i], 'w_eu': w_expert_up[i], 'w_ed': w_expert_down[i]}
        mod_l = jnp.split((jax.nn.silu(c) @ w_ada[i] + b_ada[i])[:, None, :], 6, axis=-1)
        mod_c = jnp.split((jax.nn.silu(c_ctx) @ w_ada[i] + b_ada[i])[None, None, :], 6, axis=-1)

        hc = modulate(xc, mod_c[0], mod_c[1])
        hl = modulate(xl, mod_l[0], mod_l[1])
        if last:
            s_f, s_b = ssd_context_states(hc, lp)
        else:
            out_c, s_f, s_b = mix_stream(hc, lp, False, zero_state, zero_state)
            xc = post_norm(xc, mod_c[2] * out_c, ln1_g[i], ln1_b[i])
        out_l, _, _ = mix_stream(hl, lp, True, s_f, s_b)
        xl = post_norm(xl, mod_l[2] * out_l, ln1_g[i], ln1_b[i])

        hl = modulate(xl, mod_l[3], mod_l[4]).reshape(b * l, d)
        if last:
            yl = hier_moe(hl, lp)
        else:
            hc = modulate(xc, mod_c[3], mod_c[4]).reshape(b * lc, d)
            y = hier_moe(jnp.concatenate([hl, hc], axis=0), lp)
            yl, yc = y[:b * l], y[b * l:]
            xc = post_norm(xc, mod_c[5] * yc.reshape(b, lc, d), ln2_g[i], ln2_b[i])
        xl = post_norm(xl, mod_l[5] * yl.reshape(b, l, d), ln2_g[i], ln2_b[i])
    return xl


HEAD_DIM = 64
ATTN_HEADS = 8
ATTN_WIDTH = ATTN_HEADS * HEAD_DIM
ROPE_DIM = HEAD_DIM // 4
ROPE_THETA = 500000.0
DILATED_PATTERNS = ((128, 1), (512, 4), (2048, 16))
HG_HEADS = 4
HG_EXPAND = 128
HG_VDIM = 128
HG_KDIM = HG_HEADS * HG_EXPAND
HG_WIDTH = HG_HEADS * HG_VDIM
HG_CHUNK = 64
MIX_WIDTH = ATTN_WIDTH + HG_WIDTH
IN_SIZES = (ATTN_WIDTH, ATTN_WIDTH, ATTN_WIDTH, HG_KDIM, HG_KDIM, HG_WIDTH, HG_WIDTH)
IN_COLS_2 = sum(IN_SIZES)
D_FF = 2816
EPS = 1e-6
NEG_INF = -1e30


def _rms_norm(x, w):
    xf = x.astype(jnp.float32)
    y = xf * lax.rsqrt(jnp.mean(xf * xf, axis=-1, keepdims=True) + EPS)
    return (y * w.astype(jnp.float32)).astype(x.dtype)

def _swiglu(h, w1, w3, w2):
    return (jax.nn.silu(h @ w1) * (h @ w3)) @ w2

def _rope_tables(s):
    inv = ROPE_THETA ** (-jnp.arange(0, ROPE_DIM, 2, dtype=jnp.float32) / ROPE_DIM)
    ang = jnp.arange(s, dtype=jnp.float32)[:, None] * inv[None, :]
    return jnp.cos(ang), jnp.sin(ang)

def _partial_rope(x, cos, sin):
    half = ROPE_DIM // 2
    xf = x.astype(jnp.float32)
    x1, x2, rest = xf[..., :half], xf[..., half:ROPE_DIM], xf[..., ROPE_DIM:]
    c, s_ = cos[None, :, None, :], sin[None, :, None, :]
    out = jnp.concatenate([x1 * c - x2 * s_, x1 * s_ + x2 * c, rest], axis=-1)
    return out.astype(x.dtype)

def _dilated_branch(q, k, v, window, dilation):
    b, s, h, dh = q.shape
    w = window // dilation
    l = s // dilation
    nb = -(-l // w)
    lp = nb * w
    bb = b * dilation

    def to_sub(t):
        t = t.reshape(b, l, dilation, h, dh).transpose(0, 2, 1, 3, 4).reshape(bb, l, h, dh)
        return jnp.pad(t, ((0, 0), (0, lp - l), (0, 0), (0, 0)))

    def windows(t):
        t = jnp.pad(t, ((0, 0), (w, 0), (0, 0), (0, 0))).reshape(bb, nb + 1, w, h, dh)
        return jnp.concatenate([t[:, :-1], t[:, 1:]], axis=2)

    qb = to_sub(q).reshape(bb, nb, w, h, dh)
    kw, vw = windows(to_sub(k)), windows(to_sub(v))
    scores = jnp.einsum('bnqhd,bnkhd->bnhqk', qb, kw,
                        preferred_element_type=jnp.float32) * (dh ** -0.5)
    qi = jnp.arange(w)[:, None]
    kj = jnp.arange(2 * w)[None, :]
    dist = qi + w - kj
    band = (dist >= 0) & (dist <= w)
    valid = band[None] & ((jnp.arange(nb)[:, None, None] > 0) | (kj >= w)[None])
    scores = jnp.where(valid[None, :, None], scores, NEG_INF)
    m = jnp.max(scores, axis=-1, keepdims=True)
    p = jnp.exp(scores - m)
    den = jnp.sum(p, axis=-1, keepdims=True)
    out = jnp.einsum('bnhqk,bnkhd->bnqhd', p / den, vw.astype(jnp.float32))
    lse = (m + jnp.log(den))[..., 0]
    out = (out.reshape(bb, lp, h, dh)[:, :l]
           .reshape(b, dilation, l, h, dh).transpose(0, 2, 1, 3, 4).reshape(b, s, h, dh))
    lse = (lse.transpose(0, 1, 3, 2).reshape(bb, lp, h)[:, :l]
           .reshape(b, dilation, l, h).transpose(0, 2, 1, 3).reshape(b, s, h))
    return out, lse

def _dilated_attention(q, k, v):
    outs, lses = [], []
    for window, dilation in DILATED_PATTERNS:
        o, lse = _dilated_branch(q, k, v, window, dilation)
        outs.append(o)
        lses.append(lse)
    wts = jax.nn.softmax(jnp.stack(lses), axis=0)
    return jnp.einsum('pbsh,pbshd->bshd', wts, jnp.stack(outs))

def _hgrn2(q, f_pre, inp, lb):
    b, s, h, n = q.shape
    dv = inp.shape[-1]
    c = HG_CHUNK
    nc = s // c
    lb = lb.reshape(h, n).astype(jnp.float32)
    f = lb + (1.0 - lb) * jax.nn.sigmoid(f_pre.astype(jnp.float32))
    g = jnp.log(f)
    k = 1.0 - f

    def chunks(t):
        return t.reshape(b, nc, c, h, t.shape[-1]).transpose(0, 3, 1, 2, 4)

    qc, kc, gc, vc = chunks(q.astype(jnp.float32)), chunks(k), chunks(g), chunks(inp.astype(jnp.float32))
    G = jnp.cumsum(gc, axis=3)
    G_last = G[:, :, :, -1:]
    q_dec = qc * jnp.exp(G)
    att = jnp.einsum('bhntk,bhnsk->bhnts', q_dec, kc * jnp.exp(-G))
    att = jnp.where(jnp.tril(jnp.ones((c, c), dtype=bool)), att, 0.0)
    intra = jnp.einsum('bhnts,bhnsv->bhntv', att, vc)
    chunk_state = jnp.einsum('bhnsk,bhnsv->bhnkv', kc * jnp.exp(G_last - G), vc)
    decay = jnp.exp(G_last[:, :, :, 0])

    def step(state, xs):
        dec, upd = xs
        return dec[..., None] * state + upd, state

    _, prev = lax.scan(step, jnp.zeros((b, h, n, dv), jnp.float32),
                       (jnp.moveaxis(decay, 2, 0), jnp.moveaxis(chunk_state, 2, 0)))
    prev = jnp.moveaxis(prev, 0, 2)
    inter = jnp.einsum('bhntk,bhnkv->bhntv', q_dec, prev)
    return (intra + inter).transpose(0, 2, 3, 1, 4).reshape(b, s, h, dv)

def second_inputs(seed: int = 0) -> dict:
    key = jax.random.key(seed)
    ks = jax.random.split(key, 20)
    f32 = jnp.float32

    def nrm(k, shape, fan_in):
        return jax.random.normal(k, shape, f32) * (fan_in ** -0.5)

    def gain(k, shape):
        return 1.0 + 0.02 * jax.random.normal(k, shape, f32)

    return {
        'x': jax.random.normal(ks[0], (BATCH, SEQ, D_MODEL), f32),
        'ffn1_norm': gain(ks[1], (DEPTH, D_MODEL)),
        'ffn1_w1': nrm(ks[2], (DEPTH, D_MODEL, D_FF), D_MODEL),
        'ffn1_w3': nrm(ks[3], (DEPTH, D_MODEL, D_FF), D_MODEL),
        'ffn1_w2': nrm(ks[4], (DEPTH, D_FF, D_MODEL), D_FF),
        'mix_norm': gain(ks[5], (DEPTH, D_MODEL)),
        'w_in': nrm(ks[6], (DEPTH, D_MODEL, IN_COLS_2), D_MODEL),
        'q_norm': gain(ks[7], (DEPTH, HEAD_DIM)),
        'k_norm': gain(ks[8], (DEPTH, HEAD_DIM)),
        'hg_lb_logits': 0.1 * jax.random.normal(ks[9], (DEPTH + 1, HG_KDIM), f32),
        'hg_out_norm': gain(ks[10], (DEPTH, HG_VDIM)),
        'w_out': nrm(ks[11], (DEPTH, MIX_WIDTH, D_MODEL), MIX_WIDTH),
        'ffn2_norm': gain(ks[12], (DEPTH, D_MODEL)),
        'ffn2_w1': nrm(ks[13], (DEPTH, D_MODEL, D_FF), D_MODEL),
        'ffn2_w3': nrm(ks[14], (DEPTH, D_MODEL, D_FF), D_MODEL),
        'ffn2_w2': nrm(ks[15], (DEPTH, D_FF, D_MODEL), D_FF),
    }

def second_block(x, ffn1_norm, ffn1_w1, ffn1_w3, ffn1_w2, mix_norm, w_in, q_norm, k_norm,
              hg_lb_logits, hg_out_norm, w_out, ffn2_norm, ffn2_w1, ffn2_w3, ffn2_w2):
    b, s, _ = x.shape
    cos, sin = _rope_tables(s)
    lower_bounds = jnp.cumsum(jax.nn.softmax(hg_lb_logits.astype(jnp.float32), axis=0), axis=0)
    split_at = list(np.cumsum(IN_SIZES)[:-1])
    for layer in range(DEPTH):
        x = x + 0.5 * _swiglu(_rms_norm(x, ffn1_norm[layer]),
                              ffn1_w1[layer], ffn1_w3[layer], ffn1_w2[layer])
        h = _rms_norm(x, mix_norm[layer])
        proj = h @ w_in[layer]
        aq, ak, av, hq, hf, hi, hg = jnp.split(proj, split_at, axis=-1)
        aq = _partial_rope(_rms_norm(aq.reshape(b, s, ATTN_HEADS, HEAD_DIM), q_norm[layer]), cos, sin)
        ak = _partial_rope(_rms_norm(ak.reshape(b, s, ATTN_HEADS, HEAD_DIM), k_norm[layer]), cos, sin)
        av = av.reshape(b, s, ATTN_HEADS, HEAD_DIM)
        attn_out = _dilated_attention(aq, ak, av).astype(x.dtype).reshape(b, s, ATTN_WIDTH)
        rec = _hgrn2(hq.reshape(b, s, HG_HEADS, HG_EXPAND), hf.reshape(b, s, HG_HEADS, HG_EXPAND),
                     hi.reshape(b, s, HG_HEADS, HG_VDIM), lower_bounds[layer]).astype(x.dtype)
        rec = _rms_norm(rec, hg_out_norm[layer]) * jax.nn.silu(hg.reshape(b, s, HG_HEADS, HG_VDIM))
        mixed = jnp.concatenate([attn_out, rec.reshape(b, s, HG_WIDTH)], axis=-1)
        x = x + mixed @ w_out[layer]
        x = x + 0.5 * _swiglu(_rms_norm(x, ffn2_norm[layer]),
                              ffn2_w1[layer], ffn2_w3[layer], ffn2_w2[layer])
    return x


def setup_inputs(seed=0):
    out = dict(first_inputs(seed))
    for name, value in second_inputs(seed + 1).items():
        if name != "x":
            out[name + "_2"] = value
    return out


def reference(
    x, c, ctx, c_ctx, w_ada, b_ada, w_in, b_gate, conv_w, conv_b, dt_bias, a_log, d_skip,
    ssd_norm_g, pool_w, pool_scale, w_branch_a, w_branch_b, w_out, ln1_g, ln1_b, ln2_g, ln2_b,
    w_router_group, b_router_group, w_router_expert, b_router_expert, w_expert_gate,
    w_expert_up, w_expert_down, ffn1_norm_2, ffn1_w1_2, ffn1_w3_2, ffn1_w2_2, mix_norm_2,
    w_in_2, q_norm_2, k_norm_2, hg_lb_logits_2, hg_out_norm_2, w_out_2, ffn2_norm_2, ffn2_w1_2,
    ffn2_w3_2, ffn2_w2_2,
):
    x = first_block(
        x, c, ctx, c_ctx, w_ada, b_ada, w_in, b_gate, conv_w, conv_b, dt_bias, a_log, d_skip,
        ssd_norm_g, pool_w, pool_scale, w_branch_a, w_branch_b, w_out, ln1_g, ln1_b, ln2_g,
        ln2_b, w_router_group, b_router_group, w_router_expert, b_router_expert, w_expert_gate,
        w_expert_up, w_expert_down,
    )
    return second_block(
        x, ffn1_norm_2, ffn1_w1_2, ffn1_w3_2, ffn1_w2_2, mix_norm_2, w_in_2, q_norm_2, k_norm_2,
        hg_lb_logits_2, hg_out_norm_2, w_out_2, ffn2_norm_2, ffn2_w1_2, ffn2_w3_2, ffn2_w2_2,
    )


_drawn_inputs = setup_inputs


def setup_inputs(seed=0):
    import zlib

    import numpy as np

    out = dict(_drawn_inputs(seed))
    spreads = {}
    factors = {'ctx': 3.192,
     'conv_b': 4.468,
     'd_skip': 3.529,
     'b_router_group': 4.961,
     'b_router_expert': 6.749,
     'ffn1_norm_2': 5.463,
     'mix_norm_2': 3.493,
     'q_norm_2': 8.0,
     'k_norm_2': 8.0,
     'hg_out_norm_2': 7.486,
     'ffn2_norm_2': 7.761}
    for name, (base, spread) in spreads.items():
        noise = np.random.default_rng([zlib.crc32(name.encode()), seed]).standard_normal(out[name].shape)
        drawn = base * np.exp(spread * noise) if base else spread * noise
        out[name] = __import__('jax').numpy.asarray(drawn.astype(out[name].dtype))
    for name, factor in factors.items():
        out[name] = (out[name] * factor).astype(out[name].dtype)
    return out
```

```python
from contextlib import ExitStack

import numpy as np

import concourse.bass as bass
from concourse import mybir

F32 = mybir.dt.float32
I32 = mybir.dt.int32
U32 = mybir.dt.uint32
ALU = mybir.AluOpType
ACT = mybir.ActivationFunctionType
AX = mybir.AxisListType

ALPHA = 2.0 ** 0.25
CAP = 128
NOV = 7
OVB = 3
NBLK = 32 + NOV
NR = 6
SLOT = 2048

PC = {}
_n = 0
for _name, _w in (("b_ada", 48), ("b_gate", 16), ("conv_w", 120), ("conv_b", 24), ("ssd_g", 16),
                  ("pool_scale", 8), ("ln1_g", 8), ("ln1_b", 8), ("ln2_g", 8), ("ln2_b", 8),
                  ("n1", 8), ("nm", 8), ("n2", 8), ("qn", 1), ("kn", 1), ("lb0", 4), ("lb1", 4),
                  ("hn", 1), ("cc", 16)):
    PC[_name] = _n
    _n += _w
NPC = _n
PR_DTB, PR_ALOG, PR_SKIP, PR_RB = 0, 64, 128, 160
NPR = 196
KM = {}
_n = 0
for _name in ("ident", "ones", "o1024", "o2048", "hb", "o128", "triU", "triL", "sU", "sL", "mF", "mB", "psw",
              "iota"):
    KM[_name] = _n
    _n += 128
KM["iotag"] = _n
_n += 32
KM["tok"] = _n
_n += 8
KM["aid"] = _n
_n += 8
KM["slot"] = _n
_n += 1
KM["hgm"] = _n
_n += 128
NKM = _n


class Eng:

    def __init__(self, e, sem):
        self.e, self.sem, self.n, self.seen = e, sem, 0, {}

    def wait(self, *toks):
        for t in toks:
            if t is None:
                continue
            sem, v = t
            if self.seen.get(id(sem), 0) < v:
                self.e.wait_ge(sem, v)
                self.seen[id(sem)] = v

    def inc(self, ins):
        ins.then_inc(self.sem, 1)
        self.n += 1
        return (self.sem, self.n)

    def now(self):
        return (self.sem, self.n) if self.n else None


class Dma:

    def __init__(self, sem):
        self.sem, self.n = sem, 0

    def inc(self, ins):
        ins.then_inc(self.sem, 16)
        self.n += 16
        return (self.sem, self.n)

    def now(self):
        return (self.sem, self.n) if self.n else None


class Banks:

    def __init__(self, banks):
        self.free = [(b, None) for b in banks]

    def get(self, eng):
        b, t = self.free.pop(0)
        eng.wait(t)
        return b

    def put(self, b, tok):
        self.free.append((b, tok))


class Ring:

    def __init__(self, buf, sp, dmas):
        self.buf, self.sp, self.dmas = buf, sp, dmas
        self.n, self.last = 0, [None] * NR

    def load(self, *srcs):
        s = self.n % NR
        self.n += 1
        self.sp.wait(self.last[s])
        self.last[s] = "held"
        at = 0
        for src in srcs:
            w = 1
            for d in src.shape[1:]:
                w *= d
            dst = self.buf[:, s, at:at + w]
            if len(src.shape) == 3:
                dst = dst.rearrange("p (a b) -> p a b", a=src.shape[1])
            t = self.dmas[s].inc(self.sp.e.dma_start(dst, src))
            at += w
        return s, t

    def view(self, slot, w, a=None):
        v = self.buf[:, slot[0], 0:w]
        return v if a is None else v.rearrange("p (a b) -> p a b", a=a)

    def done(self, slot, tok):
        self.last[slot[0]] = tok


def build(nc, I, outT):
    ctx = ExitStack()
    with ctx:
        def sb(name, shape, dt=F32):
            return ctx.enter_context(nc.sbuf_tensor(name, shape, dt))

        def sem(name):
            return ctx.enter_context(nc.semaphore(name))

        banks = Banks([ctx.enter_context(nc.psum_tensor(f"bank{i}", [128, 512], F32)) for i in range(8)])
        T = Eng(nc.tensor, sem("s_pe"))
        V = Eng(nc.vector, sem("s_dve"))
        A = Eng(nc.scalar, sem("s_act"))
        G = Eng(nc.gpsimd, sem("s_pool"))
        S = Eng(nc.sync, sem("s_sp"))
        ring = Ring(sb("ring", [128, NR, SLOT]), S, [Dma(sem(f"s_ring{i}")) for i in range(NR)])
        d_c = Dma(sem("d_c"))
        d_x = Dma(sem("d_x"))
        d_h = Dma(sem("d_h"))
        d_g = Dma(sem("d_g"))
        d_s = Dma(sem("d_s"))
        d_y = Dma(sem("d_y"))
        d_t = Dma(sem("d_t"))
        d_o = Dma(sem("d_o"))

        H2 = nc.dram_tensor("h2_scratch", (512, 1024), F32, kind="Internal").ap()
        YD = nc.dram_tensor("y_scratch", (1024, 1024), F32, kind="Internal").ap()

        km = sb("km", [128, NKM])
        pc = sb("pc", [128, NPC])
        pr = sb("pr", [128, NPR])
        XT = sb("XT", [128, 8, 512])
        HT = sb("HT", [128, 8, 512])
        BIG = sb("BIG", [128, 12288])
        WORK = sb("WORK", [128, 11776])
        mod = sb("mod", [128, 48, 2])
        sm = sb("sm", [128, 80])
        TMP = [sb(f"tmp{i}", [128, 512]) for i in range(6)]

        mm, act = nc.tensor.matmul, nc.scalar.activation

        def K(name, w=128, p=128):
            return km[0:p, KM[name]:KM[name] + w]

        def C(name, i, w=1):
            return pc[:, PC[name] + i:PC[name] + i + w]

        def tt(E, out, a, b, op, *waits):
            E.wait(*waits)
            return E.inc(E.e.tensor_tensor(out, a, b, op))

        def ts(E, out, a, s1, s2, op0, op1, *waits):
            E.wait(*waits)
            if s2 is None:
                return E.inc(E.e.tensor_scalar(out, a, s1, None, op0))
            return E.inc(E.e.tensor_scalar(out, a, s1, s2, op0, op1))

        def stt(out, a, s, b, op0, op1, *waits):
            V.wait(*waits)
            return V.inc(nc.vector.scalar_tensor_tensor(out=out, in0=a, scalar=s, in1=b, op0=op0, op1=op1))

        def recip(out, a, *waits):
            V.wait(*waits)
            return V.inc(nc.vector.reciprocal(out, a))

        def rsqrt(out, a, eps, *waits):
            t0 = ts(V, out, a, eps, None, ALU.add, None, *waits)
            return av(out, out, ACT.Sqrt, recip(out, out, t0)), t0

        def av(out, a, f, *waits, **kw):
            A.wait(*waits)
            return A.inc(act(out, a, f, **kw))

        def cp(E, out, a, *waits):
            if E is A:
                return av(out, a, ACT.Copy, *waits)
            E.wait(*waits)
            return E.inc(E.e.tensor_copy(out, a))

        def bc(ap, n):
            return ap.unsqueeze(2).to_broadcast([ap.shape[0], ap.shape[1], n])

        def chain(bank, pairs, *waits, m=128, inc=True):
            T.wait(*waits)
            for i, (l, r) in enumerate(pairs):
                ins = mm(bank, l, r, start=(i == 0), stop=(i == len(pairs) - 1))
            return T.inc(ins) if inc else None

        def pair_load(w, c):
            return ring.load(w[c:c + 2].rearrange("c p n -> p c n"))

        tc = d_c.inc(nc.scalar.dma_start(pc[:, :], I["pc"]))
        tc = d_c.inc(nc.scalar.dma_start(km[:, :], I["km"]))
        tc = d_c.inc(nc.scalar.dma_start(pr[:, :], I["pr"]))
        tx = d_x.inc(nc.scalar.dma_start(XT[:, :, :], I["xT"]))
        CT_IN = BIG[:, 0:8 * 256].rearrange("p (k n) -> p k n", k=8)
        tx = d_x.inc(nc.scalar.dma_start(CT_IN, I["ctxT"]))
        sc = sm[:, 64:80]
        t_sc = av(sc, C("cc", 0, 16), ACT.Silu, tc)

        def modulation(c0, c1):
            bank = banks.get(T)
            T.wait(t_sc)
            for c in range(c0, c1, 2):
                s = pair_load(I["wada"], c)
                T.wait(s[1])
                w = ring.view(s, 2048, 16)
                for j in range(2):
                    for k in range(8):
                        ins = mm(bank[:, 2 * (c + j - c0):2 * (c + j - c0) + 2], w[:, 8 * j + k, :],
                                 sc[:, 2 * k:2 * k + 2], start=(k == 0), stop=(k == 7))
                t = T.inc(ins)
                ring.done(s, t)
            n = c1 - c0
            V.wait(t)
            t = V.inc(nc.vector.tensor_tensor(mod[:, c0:c1, :], bank[:, 0:2 * n].rearrange("p (c j) -> p c j", j=2),
                                              bc(pc[:, PC["b_ada"] + c0:PC["b_ada"] + c1], 2), ALU.add))
            banks.put(bank, t)
            return t

        t = modulation(0, 16)
        t_mod01 = ts(V, mod[:, 8:16, :], mod[:, 8:16, :], 1.0, None, ALU.add, None, t)
        HC = WORK[:, 9728:11776].rearrange("p (k n) -> p k n", k=8)
        for k in range(8):
            t_h = ts(V, HT[:, k, :], XT[:, k, :], mod[:, 8 + k, 0:1], mod[:, k, 0:1], ALU.mult, ALU.add, t_mod01, tx)
            t_hc = ts(V, HC[:, k, :], CT_IN[:, k, :], mod[:, 8 + k, 1:2], mod[:, k, 1:2], ALU.mult, ALU.add)

        dec = sb("dec", [128, 6, 64])
        acs = sb("acs", [128, 4, 64])
        eacs = BIG[:, 11808:12064].rearrange("p (t h) -> p t h", t=4)
        tw = WORK[:, 9472:9728].rearrange("p (t h) -> p t h", t=4)
        etot = sb("etot", [128, 4, 64])
        cw = sb("cw", [128, 2, 64])
        ats = sb("ats", [64, 512])
        aa = TMP[5][:, 0:384].rearrange("p (t h) -> p t h", t=6)
        s = ring.load(I["wdt"])
        w = ring.view(s, 512, 8)
        bank = banks.get(T)
        T.wait(s[1], t_hc)
        for i in range(6):
            for k in range(8):
                l = HT[:, k, i * 128:(i + 1) * 128] if i < 4 else HC[:, k, (i - 4) * 128:(i - 3) * 128]
                ins = mm(bank[:, i * 64:(i + 1) * 64], l, w[:, k, :], start=(k == 0), stop=(k == 7))
        t = T.inc(ins)
        ring.done(s, t)
        raw, ab, e_, u_, l_ = (TMP[i][:, 0:384] for i in range(5))
        b3 = lambda o: pr[:, o:o + 64].unsqueeze(1).to_broadcast([128, 6, 64])
        r3 = lambda a: a.rearrange("p (t h) -> p t h", t=6)
        t = tt(V, r3(raw), r3(bank[:, 0:384]), b3(PR_DTB), ALU.add, t, tc)
        banks.put(bank, t)
        t = av(ab, raw, ACT.Abs, t)
        t = av(e_, ab, ACT.Exp, t, scale=-1.0)
        t_u = ts(V, u_, e_, 1.0, None, ALU.add, None, t)
        t_l = av(l_, u_, ACT.Ln, t_u)
        t_d = ts(V, ab, u_, -1.0, None, ALU.add, None, t_u)
        t_z = ts(V, u_, ab, 0.0, None, ALU.is_equal, None, t_d, t_l)
        t = tt(V, ab, ab, u_, ALU.add, t_z)
        t = recip(ab, ab, t)
        t = tt(V, ab, e_, ab, ALU.mult, t)
        t_q = tt(V, l_, l_, ab, ALU.mult, t, t_l)
        t = tt(V, u_, u_, e_, ALU.mult, t_z)
        t = tt(V, l_, l_, u_, ALU.add, t, t_q)
        dt2 = dec[:, :, :].rearrange("p t h -> p (t h)")
        t_dt = stt(dt2, raw, 0.0, l_, ALU.max, ALU.add, t)
        t = av(sm[:, 0:64], pr[:, PR_ALOG:PR_ALOG + 64], ACT.Exp, t_dt, T.now())
        t = tt(V, aa, dec[:, :, :], sm[:, 0:64].unsqueeze(1).to_broadcast([128, 6, 64]), ALU.mult, t)
        t = ts(V, aa, aa, -1.0, None, ALU.mult, None, t)
        t_a = t
        b1, b2 = banks.get(T), banks.get(T)
        T.wait(t_a)
        v1 = b1[:, 0:256].rearrange("p (t h) -> p t h", t=4)
        v2 = b2[:, 0:256].rearrange("p (t h) -> p t h", t=4)
        for i in range(4):
            mm(v1[:, i, 0:32], K("triU"), aa[:, i, 0:32], start=True, stop=True)
            mm(v1[:, i, 32:64], K("triL"), aa[:, i, 32:64], start=True, stop=True)
            mm(v2[:, i, :], K("ones"), aa[:, i, :], start=True, stop=True)
        v3 = b2[:, 256:384].rearrange("p (t h) -> p t h", t=2)
        mm(v3[:, 0, 0:32], K("sL"), aa[:, 4, 0:32], start=True, stop=False)
        mm(v3[:, 0, 0:32], K("ones"), aa[:, 5, 0:32], start=False, stop=True)
        mm(v3[:, 1, 0:32], K("sL"), aa[:, 5, 0:32], start=True, stop=True)
        mm(v3[:, 0, 32:64], K("sU"), aa[:, 4, 32:64], start=True, stop=True)
        mm(v3[:, 1, 32:64], K("sU"), aa[:, 5, 32:64], start=True, stop=False)
        t = T.inc(mm(v3[:, 1, 32:64], K("ones"), aa[:, 4, 32:64], start=False, stop=True))
        t_acs = cp(V, acs[:, :, :], v1, t)
        banks.put(b1, t_acs)
        t_tl = tt(V, tw[:, :, :], v2, acs[:, :, :], ALU.subtract, t_acs)
        t_e1 = av(etot[:, :, :], v2, ACT.Exp, t_tl)
        t_e2 = av(cw[:, :, :], v3, ACT.Exp, t)
        banks.put(b2, t_e2)
        t_b2 = t_tl
        t_e3 = av(tw[:, :, :], tw[:, :, :], ACT.Exp, t_tl)
        t_e4 = av(eacs[:, :, :], acs[:, :, :], ACT.Exp, t_acs)
        tt(V, tw[:, :, :], tw[:, :, :], dec[:, 0:4, :], ALU.mult, t_e3)
        t_co = tt(V, cw[:, :, :], cw[:, :, :], dec[:, 4:6, :], ALU.mult, t_e4)
        bank = banks.get(T)
        T.wait(t_acs, t_b2)
        for i in range(4):
            ins = nc.tensor.transpose(bank[0:64, i * 128:(i + 1) * 128], acs[:, i, :], K("ident"))
        t = T.inc(ins)
        t_ats = cp(V, ats[:, :], bank[0:64, :], t)
        banks.put(bank, t_ats)

        YZ = BIG[:, 0:16 * 512].rearrange("p (k n) -> p k n", k=16)
        o = [0]

        def carve(w, base=WORK):
            r = base[:, o[0]:o[0] + w]
            o[0] += w
            return r

        XS = carve(2048).rearrange("p (t n) -> p t n", t=4)
        BT = carve(512)
        CTt = carve(512)
        Bt = carve(512).rearrange("p (t n) -> p t n", t=4)
        CBT = carve(512)
        XC = carve(1024).rearrange("p (t n) -> p t n", t=2)
        Bc = carve(256).rearrange("p (t n) -> p t n", t=2)
        ST = [carve(512), carve(512)]
        Y = carve(2048).rearrange("p (t n) -> p t n", t=4)
        XCW = carve(1024).rearrange("p (t n) -> p t n", t=2)
        o2 = [8192]

        def carve2(w):
            r = BIG[:, o2[0]:o2[0] + w]
            o2[0] += w
            return r

        CB = [carve2(776) for _ in range(2)]
        CA = [carve2(776) for _ in range(2)]
        SQ = sb("SQ", [128, 512])
        M = [TMP[0], TMP[1]]
        V.wait(t_hc)
        for b in CB:
            t_pad = V.inc(nc.vector.memset(b[:, 0:776], 0.0))
        t_sq = V.inc(nc.vector.memset(SQ[:, :], 0.0))
        A.wait(t_pad)
        XD = carve2(512).rearrange("p (d t n) -> p d t n", d=2, t=4)
        SE = [TMP[2], TMP[3]]
        cb_free = [None, None]
        ca_free = [None, None]
        nconv = 0
        m_free = [None, None]
        se_free = [None, None]
        xd_free = None

        def conv_chunk(xc, w, ctx_too):
            nonlocal nconv
            i = nconv % 2
            nconv += 1
            bank = banks.get(T)
            t = chain(bank[:, :], [(w[:, k, :], HT[:, k, :]) for k in range(8)], t_h)
            t1 = cp(A, CB[i][:, 2:514], bank[:, :], t, cb_free[i])
            banks.put(bank, t1)
            n = 512
            if ctx_too:
                bank = banks.get(T)
                t = chain(bank[:, 0:256], [(w[:, k, :], HC[:, k, :]) for k in range(8)], t_hc)
                t1 = cp(A, CB[i][:, 516:772], bank[:, 0:256], t)
                banks.put(bank, t1)
                n = 770
            t_pe = t
            t = ts(V, CA[i][:, 0:n], CB[i][:, 0:n], C("conv_w", xc * 5), C("conv_b", xc), ALU.mult, ALU.add,
                   t1, ca_free[i])
            for j in range(1, 5):
                t = stt(CA[i][:, 0:n], CB[i][:, j:j + n], C("conv_w", xc * 5 + j), CA[i][:, 0:n], ALU.mult, ALU.add, t)
            cb_free[i] = t
            t = av(CA[i][:, 0:n], CA[i][:, 0:n], ACT.Silu, t)
            return i, t, t_pe

        def turn(E, dst, srcs, *waits):
            bank = banks.get(T)
            T.wait(*waits)
            n = len(srcs)
            for j, src in enumerate(srcs):
                ins = nc.tensor.transpose(bank[:, j * 128:(j + 1) * 128], src, K("ident"))
            t = T.inc(ins)
            v = bank[:, 0:n * 128]
            if len(dst.shape) == 3:
                v = v.rearrange("p (t n) -> p t n", t=n)
            t2 = cp(E, dst, v, t)
            banks.put(bank, t2)
            return t, t2

        for g in range(4):
            fr = (T.now(), V.now(), G.now())
            A.wait(*fr)
            V.wait(T.now(), G.now())
            t_xs = []
            order = [("x", 4 * g + j) for j in range(4)] + [("b", 16 + g), ("c", 20 + g)]
            for m in range(0, 6, 2):
                pairs = order[m:m + 2]
                sl = ring.load(I["wxbc"][pairs[0][1]], I["wxbc"][pairs[1][1]])
                wv = ring.view(sl, 2048, 16)
                T.wait(sl[1])
                for j, (kind, xc) in enumerate(pairs):
                    i, t, t_pe = conv_chunk(xc, wv[:, 8 * j:8 * j + 8, :], kind != "c")
                    if j == 1:
                        ring.done(sl, t_pe)
                    ca = CA[i]
                    if kind == "x":
                        q = xc - 4 * g
                        _a, ta = turn(A, XS[:, :, q * 128:(q + 1) * 128],
                                      [ca[:, c * 128:(c + 1) * 128] for c in range(4)], t)
                        _b, tb = turn(V, XC[:, :, q * 128:(q + 1) * 128],
                                      [ca[:, 514 + c * 128:514 + (c + 1) * 128] for c in range(2)])
                        ca_free[i] = _b
                        t_xs = [ta, tb]
                    elif kind == "b":
                        _a, ta = turn(A, Bt[:, :, :], [ca[:, c * 128:(c + 1) * 128] for c in range(4)], t)
                        _b, tb = turn(V, Bc[:, :, :], [ca[:, 514 + c * 128:514 + (c + 1) * 128] for c in range(2)])
                        t_B = [ta, tb]
                        t3 = cp(G, BT, ca[:, 0:512], t, fr[0])
                        ca_free[i] = t3
                        V.wait(_b)
                    else:
                        t4 = cp(G, CTt, ca[:, 0:512], t, fr[0])
                        ca_free[i] = t4
            bank = banks.get(T)
            T.wait(t3, t4)
            for c in range(4):
                sl_ = slice(c * 128, (c + 1) * 128)
                ins = mm(bank[:, sl_], BT[:, sl_], CTt[:, sl_], start=True, stop=True)
            t = T.inc(ins)
            t_cb = cp(A, CBT, bank[:, :], t)
            banks.put(bank, t_cb)

            def heads(ap, d):
                return ap[:, 32 * d + 8 * g:32 * d + 8 * g + 8]

            t_st = [None, None]
            for d in range(2):
                for i in range(2):
                    t = tt(V, XCW[:, i, :].rearrange("p (h n) -> p h n", h=8),
                           XC[:, i, :].rearrange("p (h n) -> p h n", h=8), bc(heads(cw[:, i, :], d), 64), ALU.mult,
                           t_xs[1], t_co, T.now())
                bank = banks.get(T)
                t = chain(bank[:, :], [(Bc[:, i, :], XCW[:, i, :]) for i in range(2)], t, t_B[1])
                t_st[d] = cp(A, ST[d], bank[:, :], t)
                banks.put(bank, t_st[d])
            for c in range(4):
                t_y = tt(V, Y[:, c, :].rearrange("p (h n) -> p h n", h=8), XS[:, c, :].rearrange("p (h n) -> p h n", h=8),
                         bc(pr[:, PR_SKIP + 8 * g:PR_SKIP + 8 * g + 8], 64), ALU.mult, t_xs[0])
            t_ty = None
            for step in range(4):
                for d in range(2):
                    c = step if d == 0 else 3 - step
                    bank = banks.get(T)
                    t_o = chain(bank[:, :], [(CTt[:, c * 128:(c + 1) * 128], ST[d])], t_st[d])
                    tq = TMP[4][:, :].rearrange("p (h n) -> p h n", h=8)
                    t = tt(V, tq, bank[:, :].rearrange("p (h n) -> p h n", h=8), bc(heads(eacs[:, c, :], d), 64),
                           ALU.mult, t_o, t_ty)
                    banks.put(bank, t)
                    t_ty = tt(G, Y[:, c, :], Y[:, c, :], TMP[4][:, :], ALU.add, t, t_y)
                    if step < 3:
                        t = tt(V, SE[d][:, :].rearrange("p (h n) -> p h n", h=8),
                               XS[:, c, :].rearrange("p (h n) -> p h n", h=8), bc(heads(tw[:, c, :], d), 64),
                               ALU.mult, T.now(), se_free[d])
                        bank = banks.get(T)
                        t_up = chain(bank[:, :], [(Bt[:, c, :], SE[d][:, :])], t, t_B[0])
                        t = tt(V, ST[d].rearrange("p (h n) -> p h n", h=8), ST[d].rearrange("p (h n) -> p h n", h=8),
                               bc(heads(etot[:, c, :], d), 64), ALU.mult, t_o, t_st[d])
                        t_st[d] = tt(V, ST[d], ST[d], bank[:, :], ALU.add, t, t_up)
                        banks.put(bank, t_st[d])
            for h in range(8):
                ms = []
                for d in range(2):
                    hh = 32 * d + 8 * g + h
                    bank = banks.get(T)
                    t = chain(bank[:, :], [(K("ident", p=64)[:, hh:hh + 1].to_broadcast([64, 128]), ats[0:64, :])], t_ats)
                    for c in range(4):
                        cs = slice(c * 128, (c + 1) * 128)
                        t2 = stt(SE[d][:, cs], bank[:, cs], acs[:, c, hh:hh + 1], K("mF" if d == 0 else "mB"),
                                 ALU.subtract, ALU.min, t, se_free[d], T.now() if h == 0 else None)
                    banks.put(bank, t2)
                    t = av(M[d][:, :], SE[d][:, :], ACT.Exp, t2, m_free[d])
                    se_free[d] = t
                    t = tt(V, M[d][:, :], M[d][:, :], CBT, ALU.mult, t, t_cb)
                    t3 = tt(G, XD[:, d, :, :], XS[:, :, h * 64:(h + 1) * 64],
                            dec[:, 0:4, hh:hh + 1].to_broadcast([128, 4, 64]), ALU.mult, xd_free, t_xs[0])
                    ms.append((t, t3))
                bank = banks.get(T)
                T.wait(ms[0][0], ms[1][0], ms[1][1])
                for c in range(4):
                    for d in range(2):
                        ins = mm(bank[:, c * 64:(c + 1) * 64], M[d][:, c * 128:(c + 1) * 128], XD[:, d, c, :],
                                 start=(d == 0), stop=(d == 1))
                t = T.inc(ins)
                m_free = [t, t]
                xd_free = t
                t_y = tt(V, Y[:, :, h * 64:(h + 1) * 64], Y[:, :, h * 64:(h + 1) * 64],
                         bank[:, 0:256].rearrange("p (t n) -> p t n", t=4), ALU.add, t, t_ty)
                banks.put(bank, t_y)
            for j in range(0, 4, 2):
                sl = pair_load(I["wz"], 4 * g + j)
                wv = ring.view(sl, 2048, 16)
                for jj in range(2):
                    q = 4 * g + j + jj
                    bz = banks.get(T)
                    t = chain(bz[:, :], [(wv[:, 8 * jj + k, :], HT[:, k, :]) for k in range(8)], sl[1])
                    if jj == 1:
                        ring.done(sl, t)
                    t_s = av(TMP[4][:, :], bz[:, :], ACT.Silu, t, V.now(), G.now())
                    banks.put(bz, t_s)
                    by = banks.get(T)
                    T.wait(t_y)
                    for c in range(4):
                        ins = nc.tensor.transpose(by[:, c * 128:(c + 1) * 128],
                                                  Y[:, c, (j + jj) * 128:(j + jj + 1) * 128], K("ident"))
                    t = T.inc(ins)
                    t_yz = tt(V, YZ[:, q, :], TMP[4][:, :], by[:, :], ALU.mult, t, t_s, t_hc)
                    banks.put(by, t_yz)
                    t = tt(G, TMP[5][:, :], YZ[:, q, :], YZ[:, q, :], ALU.mult, t_yz, t_sq, t_ats)
                    t_sq = tt(G, SQ[:, :], SQ[:, :], TMP[5][:, :], ALU.add, t)
                    t_yg = av(YZ[:, q, :], YZ[:, q, :], ACT.Copy, t, scale=C("ssd_g", q))

        t_mod = modulation(16, 48)
        t_mod = ts(V, mod[:, 32:40, :], mod[:, 32:40, :], 1.0, None, ALU.add, None, t_mod)
        U = WORK[:, 0:4096].rearrange("p (t n) -> p t n", t=4)
        DT = WORK[:, 4096:8192].rearrange("p (k n) -> p k n", k=8)
        MG = WORK[:, 4096:8192].rearrange("p (k n) -> p k n", k=8)
        YP = WORK[:, 0:4096].rearrange("p (k n) -> p k n", k=8)
        A.wait(T.now(), V.now(), G.now())
        V.wait(T.now(), G.now(), A.now())
        for n in range(2):
            sl = [ring.load(I["wu"][:, 4 * a:4 * a + 4, n * 512:(n + 1) * 512]) for a in range(2)]
            wv = [ring.view(x, 2048, 4) for x in sl]
            for i in range(4):
                bank = banks.get(T)
                t = chain(bank[:, :], [(HT[:, k, i * 128:(i + 1) * 128], wv[k // 4][:, k % 4, :]) for k in range(8)],
                          sl[0][1], sl[1][1])
                t_u = cp(A, U[:, i, n * 512:(n + 1) * 512], bank[:, :], t)
                banks.put(bank, t_u)
            for x in sl:
                ring.done(x, t)
        for g in range(4):
            sl = ring.load(I["pm"][g])
            wv = ring.view(sl, 2048, 4)
            for j in range(2):
                q = 2 * g + j
                bank = banks.get(T)
                t = chain(bank[:, :], [(U[:, i, q * 128:(q + 1) * 128], wv[:, i, :]) for i in range(4)], sl[1], t_u)
                t_dd = cp(V, DT[:, q, :], bank[:, :], t)
                banks.put(bank, t_dd)
            ring.done(sl, t)
        t_pd = t
        sl = ring.load(I["pw"])
        wv = ring.view(sl, 2048, 8)
        for g in range(4):
            for m in range(2):
                bank = banks.get(T)
                t = chain(bank[:, :], [(wv[:, 2 * g + k, m * 128:(m + 1) * 128], DT[:, 2 * g + k, :]) for k in range(2)],
                          sl[1], t_dd)
                t_yp = av(YP[:, 2 * g + m, :], bank[:, :], ACT.Copy, t, t_pd, scale=C("pool_scale", 2 * g + m))
                banks.put(bank, t_yp)
        ring.done(sl, t)
        t_py = t

        def rows_sum(acc, kname, *waits):
            bank = banks.get(T)
            return bank, chain(bank[:, :], [(K(kname), acc)], *waits)

        bank, t = rows_sum(SQ[:, :], "o2048", t_sq)
        RA = sb("RA", [128, 512])
        t_ra, t = rsqrt(RA[:, :], bank[:, :], 1e-5, t)
        banks.put(bank, t)
        tg = [None] * 6
        for c in range(8):
            sg = ring.load(I["wg"][c], I["wg"][8 + c])
            wv = ring.view(sg, 2048, 16)
            for j in range(2):
                bank = banks.get(T)
                t = chain(bank[:, :], [(wv[:, 8 * j + k, :], HT[:, k, :]) for k in range(8)], sg[1])
                tg[j] = av(TMP[j][:, :], bank[:, :], ACT.Sigmoid, t, tg[2], tg[3], bias=C("b_gate", 8 * j + c))
                banks.put(bank, tg[j])
            ring.done(sg, t)
            sa = ring.load(I["wa"][c])
            wv = ring.view(sa, 2048, 16)
            bank = banks.get(T)
            t = chain(bank[:, :], [(wv[:, k, :], YZ[:, k, :]) for k in range(16)], sa[1], t_yg)
            ring.done(sa, t)
            t = tt(V, TMP[2][:, :], bank[:, :], RA[:, :], ALU.mult, t, t_ra, tg[4])
            banks.put(bank, t)
            tg[2] = tt(V, TMP[2][:, :], TMP[0][:, :], TMP[2][:, :], ALU.mult, t, tg[0])
            if c % 2 == 0:
                s_b = pair_load(I["wb"], c)
            wv = ring.view(s_b, 2048, 16)
            bank = banks.get(T)
            t = chain(bank[:, :], [(wv[:, 8 * (c % 2) + k, :], YP[:, k, :]) for k in range(8)], s_b[1], t_yp)
            if c % 2:
                ring.done(s_b, t)
            tg[3] = tt(V, TMP[3][:, :], TMP[1][:, :], bank[:, :], ALU.mult, t, tg[1], tg[4])
            banks.put(bank, tg[3])
            tg[4] = tt(G, MG[:, c, :], TMP[2][:, :], TMP[3][:, :], ALU.add, tg[3], tg[2], t_py)
        t_mg = tg[4]

        def layer_norm(gname, bname, t_in):
            t = tt(V, SQ[:, :], XT[:, 0, :], XT[:, 1, :], ALU.add, t_in, T.now(), G.now(), A.now())
            for k in range(2, 8):
                t = tt(V, SQ[:, :], SQ[:, :], XT[:, k, :], ALU.add, t)
            bank, t = rows_sum(SQ[:, :], "o1024", t)
            t_c = [None] * 8
            for k in range(8):
                t_c[k] = tt(V, XT[:, k, :], XT[:, k, :], bank[:, :], ALU.subtract, t)
            banks.put(bank, t_c[7])
            tf = [None, None]
            for k in range(8):
                t = av(TMP[k % 2][:, :], XT[:, k, :], ACT.Square, t_c[k], tf[k % 2])
                if k == 0:
                    t = cp(G, SQ[:, :], TMP[0][:, :], t, t_c[7])
                else:
                    t = tt(G, SQ[:, :], SQ[:, :], TMP[k % 2][:, :], ALU.add, t, G.now())
                tf[k % 2] = t
            bank, t = rows_sum(SQ[:, :], "o1024", t)
            t, t0 = rsqrt(RA[:, :], bank[:, :], 1e-5, t)
            banks.put(bank, t0)
            for k in range(8):
                t2 = tt(V, XT[:, k, :], XT[:, k, :], RA[:, :], ALU.mult, t)
                t3 = ts(V, XT[:, k, :], XT[:, k, :], C(gname, k), C(bname, k), ALU.mult, ALU.add, t2)
            return t3

        for c in range(0, 8, 2):
            sl = pair_load(I["wo"], c)
            wv = ring.view(sl, 2048, 16)
            for j in range(2):
                q = c + j
                bank = banks.get(T)
                t = chain(bank[:, :], [(wv[:, 8 * j + k, :], MG[:, k, :]) for k in range(8)], sl[1], t_mg)
                t1 = ts(V, XT[:, q, :], XT[:, q, :], ALPHA, None, ALU.mult, None, t_h)
                t_r = stt(XT[:, q, :], bank[:, :], mod[:, 16 + q, 0:1], XT[:, q, :], ALU.mult, ALU.add, t, t1, t_mod)
                banks.put(bank, t_r)
            ring.done(sl, t)
        t_x = layer_norm("ln1_g", "ln1_b", t_r)

        for k in range(8):
            t_h2 = ts(V, HT[:, k, :], XT[:, k, :], mod[:, 32 + k, 0:1], mod[:, 24 + k, 0:1], ALU.mult, ALU.add, t_x)
        HR = WORK[:, 0:4096].rearrange("p (t n) -> p t n", t=4)
        A.wait(T.now(), V.now(), G.now())
        for i in range(4):
            for q in range(2):
                _t, t = turn(A, HR[:, i, q * 512:(q + 1) * 512].rearrange("p (t n) -> p t n", t=4),
                             [HT[:, 4 * q + k, i * 128:(i + 1) * 128] for k in range(4)], t_h2)
        A.wait(t)
        t_hd = d_h.inc(nc.scalar.dma_start(H2.rearrange("(t p) n -> p t n", p=128), HR[:, :, :]))
        sl = ring.load(I["wr"])
        wv = ring.view(sl, 288, 8)
        bank = banks.get(T)
        T.wait(sl[1], t_h2)
        for i in range(4):
            for k in range(8):
                ins = mm(bank[:, i * 36:(i + 1) * 36], HT[:, k, i * 128:(i + 1) * 128], wv[:, k, :],
                         start=(k == 0), stop=(k == 7))
        t = T.inc(ins)
        ring.done(sl, t)
        rt = BIG[:, 0:4096]
        ro = [0]

        def rc(w, t_=4):
            r = rt[:, ro[0]:ro[0] + w * t_]
            ro[0] += w * t_
            return r.rearrange("p (t n) -> p t n", t=t_)

        lg, g8, gm, m32, lm, vm, oh0, oh1, ohs, sc4, wk = (rc(n) for n in (36, 8, 8, 32, 32, 8, 32, 32, 32, 24, 2))
        gi = sb("gi", [128, 4, 8], U32)
        vi = sb("vi", [128, 4, 8], U32)
        t = tt(V, lg, bank[:, 0:144].rearrange("p (t n) -> p t n", t=4),
               pr[:, PR_RB:PR_RB + 36].unsqueeze(1).to_broadcast([128, 4, 36]), ALU.add, t, A.now(), G.now())
        banks.put(bank, t)
        V.inc(nc.vector.memset(g8, -1e30))
        V.wait(V.now())
        t = cp(V, g8[:, :, 0:4], lg[:, :, 0:4], t)
        for i in range(4):
            V.wait(t)
            t = V.inc(nc.vector.max(gm[:, i, :], g8[:, i, :]))
            V.wait(t)
            t = V.inc(nc.vector.max_index(gi[:, i, :], gm[:, i, :], g8[:, i, :]))
            t = cp(V, sc4[:, i, 0:1], gi[:, i, 0:1], t)
            t = ts(V, m32[:, i, :], K("iotag", 32), sc4[:, i, 0:1], None, ALU.is_equal, None, t)
            t1 = tt(V, lm[:, i, :], lg[:, i, 4:36], m32[:, i, :], ALU.mult, t)
            t2 = ts(V, m32[:, i, :], m32[:, i, :], 1e30, -1e30, ALU.mult, ALU.add, t1)
            t = tt(V, lm[:, i, :], lm[:, i, :], m32[:, i, :], ALU.add, t2)
            V.wait(t)
            t = V.inc(nc.vector.max(vm[:, i, :], lm[:, i, :]))
            V.wait(t)
            t = V.inc(nc.vector.max_index(vi[:, i, :], vm[:, i, :], lm[:, i, :]))
            t = cp(V, sc4[:, i, 2:4], vi[:, i, 0:2], t)
            t1 = ts(V, oh0[:, i, :], K("iota", 32), sc4[:, i, 2:3], None, ALU.is_equal, None, t)
            t2 = ts(V, oh1[:, i, :], K("iota", 32), sc4[:, i, 3:4], None, ALU.is_equal, None, t)
            t = tt(V, ohs[:, i, :], oh0[:, i, :], oh1[:, i, :], ALU.add, t2)
            t3 = ts(V, sc4[:, i, 4:5], gm[:, i, 0:1], -1.0, None, ALU.mult, None)
            t4 = tt(V, sc4[:, i, 5:6], vm[:, i, 1:2], vm[:, i, 0:1], ALU.subtract, t)
            A.wait(t4)
            A.inc(act(g8[:, i, 4:8], lg[:, i, 0:4], ACT.Exp, bias=sc4[:, i, 4:5], accum_out=sc4[:, i, 6:7]))
            t5 = av(sc4[:, i, 7:8], sc4[:, i, 5:6], ACT.Exp)
            t = ts(V, sc4[:, i, 8:9], sc4[:, i, 7:8], 1.0, None, ALU.add, None, t5)
            t = tt(V, sc4[:, i, 8:9], sc4[:, i, 8:9], sc4[:, i, 6:7], ALU.mult, t)
            V.wait(t)
            t = V.inc(nc.vector.reciprocal(wk[:, i, 0:1], sc4[:, i, 8:9]))
            t = tt(V, wk[:, i, 1:2], wk[:, i, 0:1], sc4[:, i, 7:8], ALU.mult, t)
        bank = banks.get(T)
        T.wait(t)
        for i in range(4):
            for j in range(i + 1):
                mm(bank[:, i * 32:(i + 1) * 32], K("sU") if j == i else K("ones"), ohs[:, j, :],
                   start=(j == 0), stop=(j == i))
        for j in range(4):
            ins = mm(bank[:, 128:160], K("ones"), ohs[:, j, :], start=(j == 0), stop=(j == 3))
        t = T.inc(ins)
        cnt = rc(32, 1)[:, 0, :]
        ove = rc(32, 1)[:, 0, :]
        send = rc(32, 1)[:, 0, :]
        sst = rc(32, 1)[:, 0, :]
        t32 = rc(32, 1)[:, 0, :]
        eid = rc(NOV + 1, 1)[:, 0, :]
        rk = rc(32)
        t0 = cp(V, cnt, bank[:, 128:160], t)
        t1 = cp(V, rk, bank[:, 0:128].rearrange("p (t n) -> p t n", t=4), t)
        banks.put(bank, t1)
        t = ts(V, ove, cnt, float(CAP), None, ALU.is_gt, None, t1)
        for b in range(2, OVB + 1):
            t = stt(ove, cnt, float(CAP * b), ove, ALU.is_gt, ALU.add, t)
        V.wait(t)
        V.inc(nc.vector.memset(t32, 0.0))
        V.wait(V.now())
        t = V.inc(nc.vector.tensor_tensor_scan(send, ove, t32, 0.0, ALU.add, ALU.add))
        t = tt(V, sst, send, ove, ALU.subtract, t)
        for j in range(NOV):
            V.wait(V.now())
            V.inc(nc.vector.tensor_scalar(t32, send, float(j), 0.0, ALU.is_le, ALU.add, accum_out=eid[:, j:j + 1]))
        V.wait(V.now())
        t = ts(V, eid[:, 0:NOV], eid[:, 0:NOV], 31.0, None, ALU.min, None)
        cp(V, eid[:, NOV:NOV + 1], send[:, 31:32], t)
        eidi = sb("eidi", [128, NOV + 1], I32)
        t_eid = cp(V, eidi[:, :], eid, V.now())
        SB_ = BIG[:, 4096:4096 + 128 + 2 * NBLK]
        bank = banks.get(T)
        tpe = None
        for i in range(4):
            for k in range(2):
                oh = (oh0, oh1)[k]
                x = sc4[:, i, 9:10]
                y = sc4[:, i, 10:11]
                q = sc4[:, i, 11:12]
                bl = sc4[:, i, 12:13]
                r1 = sc4[:, i, 13:14]
                V.wait(V.now())
                V.inc(nc.vector.tensor_tensor_reduce(out=t32, in0=rk[:, i, :], in1=oh[:, i, :], scale=1.0, scalar=0.0,
                                                     op0=ALU.mult, op1=ALU.add, accum_out=x))
                V.wait(V.now())
                V.inc(nc.vector.tensor_tensor_reduce(out=t32, in0=sst, in1=oh[:, i, :], scale=1.0, scalar=0.0,
                                                     op0=ALU.mult, op1=ALU.add, accum_out=y))
                ts(V, q, x, float(CAP), None, ALU.is_ge, None, V.now())
                for b in range(2, OVB + 1):
                    stt(q, x, float(CAP * b), q, ALU.is_ge, ALU.add, V.now())
                stt(r1, q, -float(CAP), x, ALU.mult, ALU.add, V.now())
                e = sc4[:, i, 2 + k:3 + k]
                stt(y, y, 31.0, q, ALU.add, ALU.add, V.now())
                tt(V, y, y, e, ALU.subtract, V.now())
                ts(V, x, q, 0.0, None, ALU.is_gt, None, V.now())
                tt(V, y, y, x, ALU.mult, V.now())
                tt(V, bl, y, e, ALU.add, V.now())
                V.wait(tpe)
                ts(V, SB_[:, 0:128], K("iota"), r1, None, ALU.is_equal, None, V.now())
                ts(V, SB_[:, 128:128 + NBLK], K("iota", NBLK), bl, km[:, KM["tok"] + 2 * i + k:KM["tok"] + 2 * i + k + 1],
                   ALU.is_equal, ALU.mult, V.now())
                t = ts(V, SB_[:, 128 + NBLK:128 + 2 * NBLK], K("iota", NBLK), bl,
                       km[:, KM["aid"] + 2 * i + k:KM["aid"] + 2 * i + k + 1], ALU.is_equal, ALU.mult, V.now())
                T.wait(t)
                n = 2 * i + k
                tpe = T.inc(mm(bank[:, 0:2 * NBLK], SB_[:, 0:128], SB_[:, 128:128 + 2 * NBLK], start=(n == 0),
                               stop=(n == 7)))
        fl = BIG[:, 4400:4400 + 2 * NBLK]
        ix = sb("ix", [128, 2, NBLK], U32)
        ts(V, fl[:, 0:NBLK], bank[:, 0:NBLK], -1.0, 0.0, ALU.add, ALU.max, tpe)
        t = ts(V, BIG[:, 4600:4600 + NBLK], bank[:, NBLK:2 * NBLK], 0.0, km[:, KM["slot"]:KM["slot"] + 1],
               ALU.is_equal, ALU.mult)
        t = stt(fl[:, NBLK:2 * NBLK], bank[:, NBLK:2 * NBLK], -1.0, BIG[:, 4600:4600 + NBLK], ALU.add, ALU.add, t)
        banks.put(bank, t)
        t_ix = cp(V, ix[:, :, :], fl.rearrange("p (a n) -> p a n", a=2), t)
        t_free = (T.now(), A.now())
        V.wait(t_ix)

        XG = [WORK[:, 4096 + 1024 * i:5120 + 1024 * i] for i in range(2)]
        XGT = [WORK[:, 6144 + 1024 * i:7168 + 1024 * i].rearrange("p (k n) -> p k n", k=8) for i in range(2)]
        YO = [WORK[:, 8192 + 1024 * i:9216 + 1024 * i] for i in range(2)]
        GT = [BIG[:, 5120 + 512 * i:5632 + 512 * i] for i in range(2)]
        GTT = [BIG[:, 6144 + 512 * i:6656 + 512 * i].rearrange("p (k n) -> p k n", k=4) for i in range(2)]
        d_gg = [Dma(sem(f"d_gg{i}")) for i in range(2)]

        def make_moe(T, V, A, G, S, ring, banks, d_gg, d_s, first):
            free = {}
            got = {}

            def w(name, i):
                return free.get((name, i))

            def gather(b):
                i = b % 2
                G.wait(t_ix if first else None, t_hd if first else None, t_free[0] if first else None,
                       w("xg", i))
                got[b] = d_gg[i].inc(nc.gpsimd.indirect_dma_start(
                    XG[i], None, H2, bass.IndirectOffsetOnAxis(ap=ix[:, 0, b:b + 1], axis=0)))

            def block(b, srcs):
                i = b % 2
                sg = [ring.load(s_) for s_ in srcs[0:2]]
                su = [ring.load(s_) for s_ in srcs[2:4]]
                sd = [ring.load(s_) for s_ in srcs[4:6]]
                for q in range(2):
                    bank = banks.get(T)
                    T.wait(got[b])
                    for k in range(4):
                        ins = nc.tensor.transpose(bank[:, k * 128:(k + 1) * 128],
                                                  XG[i][:, (4 * q + k) * 128:(4 * q + k + 1) * 128], K("ident"))
                    t = T.inc(ins)
                    A.wait(t, w("xgt", i))
                    t2 = A.inc(act(XGT[i][:, 4 * q:4 * q + 4, :], bank[:, :].rearrange("p (k n) -> p k n", k=4),
                                   ACT.Copy))
                    banks.put(bank, t2)
                free[("xg", i)] = t
                bk = []
                for sl in (sg, su):
                    bank = banks.get(T)
                    T.wait(t2, sl[0][1], sl[1][1])
                    for k in range(8):
                        ins = mm(bank[:, :], XGT[i][:, k, :], ring.view(sl[k // 4], 2048, 4)[:, k % 4, :],
                                 start=(k == 0), stop=(k == 7))
                    t = T.inc(ins)
                    ring.done(sl[0], t)
                    ring.done(sl[1], t)
                    bk.append((bank, t))
                free[("xgt", i)] = t
                A.wait(bk[0][1], w("gt", i))
                t = A.inc(act(GT[i], bk[0][0][:, :], ACT.Silu))
                banks.put(bk[0][0], t)
                V.wait(t, bk[1][1])
                t = V.inc(nc.vector.tensor_tensor(GT[i], GT[i], bk[1][0][:, :], ALU.mult))
                banks.put(bk[1][0], t)
                bank = banks.get(T)
                T.wait(t)
                for k in range(4):
                    ins = nc.tensor.transpose(bank[:, k * 128:(k + 1) * 128], GT[i][:, k * 128:(k + 1) * 128],
                                              K("ident"))
                t = T.inc(ins)
                free[("gt", i)] = t
                V.wait(t, w("gtt", i))
                t = V.inc(nc.vector.tensor_copy(GTT[i], bank[:, :].rearrange("p (k n) -> p k n", k=4)))
                banks.put(bank, t)
                T.wait(sd[0][1], sd[1][1], t)
                for n in range(2):
                    bank = banks.get(T)
                    for k in range(4):
                        ins = mm(bank[:, :], GTT[i][:, k, :],
                                 ring.view(sd[k // 2], 2048, 2)[:, k % 2, n * 512:(n + 1) * 512],
                                 start=(k == 0), stop=(k == 3))
                    t = T.inc(ins)
                    A.wait(t, w("yo", i))
                    t3 = A.inc(act(YO[i][:, n * 512:(n + 1) * 512], bank[:, :], ACT.Copy))
                    banks.put(bank, t3)
                free[("gtt", i)] = t
                ring.done(sd[0], t)
                ring.done(sd[1], t)
                G.wait(t3, d_s.now())
                free[("yo", i)] = d_s.inc(nc.gpsimd.indirect_dma_start(
                    YD, bass.IndirectOffsetOnAxis(ap=ix[:, 1, b:b + 1], axis=0), YO[i], None,
                    bounds_check=1023, oob_is_err=False))

            return gather, block

        def expert(e):
            r = []
            for w_ in ("eg", "eu"):
                v = I[w_].rearrange("e (k p) n -> e p k n", p=128)
                r += [v[e, :, 0:4, :], v[e, :, 4:8, :]]
            v = I["ed"].rearrange("e (k p) n -> e p k n", p=128)
            return r + [v[e, :, 0:2, :], v[e, :, 2:4, :]]

        A.wait(V.now())
        gather, block = make_moe(T, V, A, G, S, ring, banks, d_gg, d_s, True)
        gather(0)
        for e in range(32):
            if e + 1 < 32:
                gather(e + 1)
            block(e, expert(e))

        everything = (T.now(), V.now(), A.now(), d_s.now(), t_eid)
        for E_ in (T, V, A, G, S):
            E_.wait(*everything)
        nov = nc.values_load(eidi[0:1, NOV:NOV + 1], min_val=0, max_val=NOV)
        with nc.If(nov > 0):
            T2, V2, A2, G2, S2 = (Eng(e_.e, sem(f"o_{n}")) for n, e_ in enumerate((T, V, A, G, S)))
            ring2 = Ring(ring.buf, S2, [Dma(sem(f"o_r{i}")) for i in range(NR)])
            banks2 = Banks([b for b, _t in banks.free])
            dg2 = [Dma(sem(f"o_g{i}")) for i in range(2)]
            ds2 = Dma(sem("o_s"))
            gather2, block2 = make_moe(T2, V2, A2, G2, S2, ring2, banks2, dg2, ds2, False)
            for j in range(NOV):
                ev = nc.sync.value_load(eidi[0:1, j:j + 1], min_val=0, max_val=31)
                srcs = []
                for w_ in ("eg", "eu"):
                    v = I[w_].rearrange("e (k p) n -> p e k n", p=128)[:, bass.ds(ev, 1), :, :]
                    v = v.rearrange("p e k n -> p (e k) n")
                    srcs += [v[:, 0:4, :], v[:, 4:8, :]]
                v = I["ed"].rearrange("e (k p) n -> p e k n", p=128)[:, bass.ds(ev, 1), :, :]
                v = v.rearrange("p e k n -> p (e k) n")
                srcs += [v[:, 0:2, :], v[:, 2:4, :]]
                gather2(32 + j)
                block2(32 + j, srcs)
            for E_ in (T2, V2, A2, G2, S2):
                E_.wait(T2.now(), V2.now(), A2.now(), ds2.now())
        nc.end_ifs()

        YV = YD.rearrange("(t p k) n -> t p k n", p=128, k=2)
        YI = BIG[:, 8192:12288].rearrange("p (i k n) -> p i k n", i=2, k=2)
        YL = WORK[:, 0:4096].rearrange("p (t n) -> p t n", t=4)
        G.wait(d_s.now())
        d_yy = [Dma(sem(f"d_yy{i}")) for i in range(2)]
        tw_ = [None, None]
        A.wait(t_hd)
        for i in range(4):
            G.wait(tw_[i % 2])
            t_ld = d_yy[i % 2].inc(nc.gpsimd.dma_start(YI[:, i % 2, :, :], YV[i]))
            t1 = ts(V, YL[:, i, :], YI[:, i % 2, 0, :], wk[:, i, 0:1], None, ALU.mult, None, t_ld, t_hd)
            t_yl = stt(YL[:, i, :], YI[:, i % 2, 1, :], wk[:, i, 1:2], YL[:, i, :], ALU.mult, ALU.add, t1)
            tw_[i % 2] = t_yl
        for k in range(8):
            bank = banks.get(T)
            T.wait(t_yl)
            for i in range(4):
                ins = nc.tensor.transpose(bank[:, i * 128:(i + 1) * 128], YL[:, i, k * 128:(k + 1) * 128], K("ident"))
            t = T.inc(ins)
            t1 = ts(V, XT[:, k, :], XT[:, k, :], ALPHA, None, ALU.mult, None)
            t_r = stt(XT[:, k, :], bank[:, :], mod[:, 40 + k, 0:1], XT[:, k, :], ALU.mult, ALU.add, t, t1)
            banks.put(bank, t_r)
        t_x = layer_norm("ln2_g", "ln2_b", t_r)

        def sum_squares(t_in):
            tf = [None, None]
            for k in range(8):
                t = av(TMP[k % 2][:, :], XT[:, k, :], ACT.Square, t_in, V.now(), tf[k % 2])
                if k == 0:
                    t = cp(G, SQ[:, :], TMP[0][:, :], t, V.now(), T.now())
                else:
                    t = tt(G, SQ[:, :], SQ[:, :], TMP[k % 2][:, :], ALU.add, t, G.now())
                tf[k % 2] = t
            return t

        def rms_norm(name, t_in):
            t = sum_squares(t_in)
            bank, t = rows_sum(SQ[:, :], "o1024", t)
            t, t0 = rsqrt(RA[:, :], bank[:, :], 1e-6, t, T.now())
            banks.put(bank, t0)
            V.wait(T.now())
            for k in range(8):
                t2 = stt(HT[:, k, :], XT[:, k, :], C(name, k), RA[:, :], ALU.mult, ALU.mult, t)
            return t2

        def ffn(name, w1, w3, w2, t_in):
            t_n = rms_norm(name, t_in)
            FA = BIG[:, 0:22 * 512].rearrange("p (k n) -> p k n", k=22)
            tfree = [None, None]
            V.wait(A.now(), T.now(), G.now())
            for f in range(0, 22, 2):
                s1, s3 = pair_load(w1, f), pair_load(w3, f)
                for j in range(2):
                    bk = []
                    for sl in (s1, s3):
                        wv = ring.view(sl, 2048, 16)
                        bank = banks.get(T)
                        t = chain(bank[:, :], [(wv[:, 8 * j + k, :], HT[:, k, :]) for k in range(8)], sl[1], t_n)
                        if j:
                            ring.done(sl, t)
                        bk.append((bank, t))
                    i = j
                    t = av(TMP[i][:, :], bk[0][0][:, :], ACT.Silu, bk[0][1], tfree[i])
                    banks.put(bk[0][0], t)
                    t_f = tt(V, FA[:, f + j, :], TMP[i][:, :], bk[1][0][:, :], ALU.mult, t, bk[1][1])
                    tfree[i] = t_f
                    banks.put(bk[1][0], t_f)
            for c in range(8):
                sl = [ring.load(w2[c][:, 0:11 * 128]), ring.load(w2[c][:, 11 * 128:22 * 128])]
                wv = [ring.view(x, 11 * 128, 11) for x in sl]
                bank = banks.get(T)
                t = chain(bank[:, :], [(wv[k // 11][:, k % 11, :], FA[:, k, :]) for k in range(22)], sl[0][1], sl[1][1],
                          t_f)
                for x in sl:
                    ring.done(x, t)
                t_o = stt(XT[:, c, :], bank[:, :], 0.5, XT[:, c, :], ALU.mult, ALU.add, t)
                banks.put(bank, t_o)
            return t_o

        t_x = ffn("n1", I["f11"], I["f13"], I["f12"], t_x)
        t_n = rms_norm("nm", t_x)
        fr = (T.now(), V.now(), G.now(), A.now())
        for E_ in (V, A, G):
            E_.wait(*fr)
        o[0] = 0
        QT = carve(2048).rearrange("p (k n) -> p k n", k=4)
        KT = carve(2048).rearrange("p (k n) -> p k n", k=4)
        VV = carve(2048).rearrange("p (t n) -> p t n", t=4)
        HV = carve(2048).rearrange("p (t n) -> p t n", t=4)
        AL = carve(2048).rearrange("p (t n) -> p t n", t=4)
        CS = carve(1024).rearrange("p (t n) -> p t n", t=2)
        RST = carve(512)
        o2[0] = 0
        MX = carve2(4096).rearrange("p (k n) -> p k n", k=8)
        S.wait(*fr)
        t_tab = d_t.inc(nc.sync.dma_start(AL, I["al"]))
        t_tab = d_t.inc(nc.sync.dma_start(CS, I["cs"]))
        t_tab = d_t.inc(nc.sync.dma_start(RST, I["rst"]))
        tq_ = [None] * 6
        for n, (dst, nm) in enumerate(((QT, "qn"), (KT, "kn"))):
            for c in range(0, 4, 2):
                sl = pair_load(I["w2in"], 4 * n + c)
                wv = ring.view(sl, 2048, 16)
                for j in range(2):
                    bank = banks.get(T)
                    t = chain(bank[:, :], [(wv[:, 8 * j + k, :], HT[:, k, :]) for k in range(8)], sl[1], t_n)
                    if j:
                        ring.done(sl, t)
                    t_s = av(TMP[0][:, :], bank[:, :], ACT.Square, t, tq_[0])
                    b2, t = rows_sum(TMP[0][:, :], "hb", t_s)
                    tq_[0] = t
                    t, t0 = rsqrt(TMP[1][:, :], b2[:, :], 1e-6, t)
                    banks.put(b2, t0)
                    t = stt(TMP[2][:, :], bank[:, :], C(nm, 0), TMP[1][:, :], ALU.mult, ALU.mult, t, tq_[2])
                    banks.put(bank, t)
                    t_q = t
                    b3_, t = rows_sum(TMP[2][:, :], "psw", t)
                    t1 = tt(G, TMP[3][:, :], TMP[2][:, :], CS[:, 0, :], ALU.mult, t_q, t_tab, tq_[3])
                    t2 = tt(V, TMP[4][:, :], b3_[:, :], CS[:, 1, :], ALU.mult, t, t_tab, tq_[3])
                    banks.put(b3_, t2)
                    tq_[3] = t_qk = tt(G, dst[:, c + j, :], TMP[3][:, :], TMP[4][:, :], ALU.add, t1, t2)
                    tq_[2] = t_qk
        for nm, dst in (("w2v", VV), ("w2i", HV)):
            sl = [ring.load(I[nm][:, 4 * a:4 * a + 4, :]) for a in range(2)]
            wv = [ring.view(x, 2048, 4) for x in sl]
            for i in range(4):
                bank = banks.get(T)
                t = chain(bank[:, :], [(HT[:, k, i * 128:(i + 1) * 128], wv[k // 4][:, k % 4, :]) for k in range(8)],
                          sl[0][1], sl[1][1])
                t_v = cp(A, dst[:, i, :], bank[:, :], t)
                banks.put(bank, t_v)
            for x in sl:
                ring.done(x, t)

        PB = [carve2(512) for _ in range(2)]
        PT = [carve2(512).rearrange("p (k n) -> p k n", k=4) for _ in range(2)]
        ms_ = [carve2(8) for _ in range(2)]
        f_pb, f_pt, f_ms = [None] * 2, [None] * 2, [None] * 2
        n = 0
        for h in range(8):
            ps = slice(64 * (h % 2), 64 * (h % 2) + 64)
            bo = banks.get(T)
            for qt in range(4):
                i = n % 2
                n += 1
                nk = (qt + 1) * 128
                bank = banks.get(T)
                t = chain(bank[:, 0:nk], [(QT[ps, h // 2, qt * 128:(qt + 1) * 128], KT[ps, h // 2, 0:nk])], t_qk)
                t = stt(PB[i][:, 0:nk], bank[:, 0:nk], 0.125, AL[:, qt, 0:nk], ALU.mult, ALU.add, t, f_pb[i], t_tab)
                banks.put(bank, t)
                V.wait(t)
                t = V.inc(nc.vector.tensor_reduce(ms_[i][:, 0:1], PB[i][:, 0:nk], AX.X, ALU.max))
                t = ts(V, ms_[i][:, 1:2], ms_[i][:, 0:1], -1.0, None, ALU.mult, None, t)
                A.wait(t)
                t = A.inc(act(PB[i][:, 0:nk], PB[i][:, 0:nk], ACT.Exp, bias=ms_[i][:, 1:2], accum_out=ms_[i][:, 2:3]))
                V.wait(t)
                t = V.inc(nc.vector.reciprocal(ms_[i][:, 3:4], ms_[i][:, 2:3]))
                t = ts(V, PB[i][:, 0:nk], PB[i][:, 0:nk], ms_[i][:, 3:4], None, ALU.mult, None, t)
                bank = banks.get(T)
                T.wait(t)
                for k in range(qt + 1):
                    ins = nc.tensor.transpose(bank[:, k * 128:(k + 1) * 128], PB[i][:, k * 128:(k + 1) * 128],
                                              K("ident"))
                t = T.inc(ins)
                f_pb[i] = t
                t = cp(A, PT[i][:, 0:qt + 1, :], bank[:, 0:nk].rearrange("p (k n) -> p k n", k=qt + 1), t, f_pt[i])
                banks.put(bank, t)
                T.wait(t, t_v)
                for k in range(qt + 1):
                    ins = mm(bo[ps, qt * 128:(qt + 1) * 128], VV[:, k, h * 64:(h + 1) * 64], PT[i][:, k, :],
                             start=(k == 0), stop=(k == qt))
                t = T.inc(ins)
                f_pt[i] = t
            t_mx = cp(V, MX[ps, h // 2, :], bo[ps, :], t)
            banks.put(bo, t_mx)

        lw = sm[:, 16:40]
        t = tt(V, lw[:, 0:4], C("lb0", 0, 4), C("lb1", 0, 4), ALU.max)
        tt(V, lw[:, 4:8], C("lb0", 0, 4), lw[:, 0:4], ALU.subtract, t)
        t = tt(V, lw[:, 8:12], C("lb1", 0, 4), lw[:, 0:4], ALU.subtract, t)
        t = av(lw[:, 4:12], lw[:, 4:12], ACT.Exp, t)
        t = tt(V, lw[:, 0:4], lw[:, 4:8], lw[:, 8:12], ALU.add, t)
        t = recip(lw[:, 0:4], lw[:, 0:4], t)
        t = tt(V, lw[:, 12:16], lw[:, 4:8], lw[:, 0:4], ALU.mult, t)
        t_lb = ts(V, lw[:, 16:20], lw[:, 12:16], -1.0, 1.0, ALU.mult, ALU.add, t)
        names = [carve2(512) for _ in range(9)]
        QD, KD, KW, FF, GG, EX, ATT, REC, HGB = names
        KWT = TMP[5][:, :].rearrange("p (t n) -> p t n", t=4)
        SS = [carve2(128) for _ in range(8)]
        V.wait(T.now(), A.now(), G.now())
        V.inc(nc.vector.memset(ATT, 0.0))
        t_at0 = V.inc(nc.vector.memset(SS[0], 0.0))
        V.wait(t_at0)
        hgm = K("hgm").bitcast(U32)
        for h in range(4):
            prev = (T.now(), V.now(), G.now(), A.now())
            if h % 2 == 0:
                sl3 = [pair_load(I["w2in"], b_ + h) for b_ in (8, 12, 16)]
            wv3 = [ring.view(x, 2048, 16) for x in sl3]
            bks = []
            for x, wv in zip(sl3, wv3):
                bank = banks.get(T)
                t = chain(bank[:, :], [(wv[:, 8 * (h % 2) + k, :], HT[:, k, :]) for k in range(8)], x[1])
                if h % 2:
                    ring.done(x, t)
                bks.append((bank, t))
            (bq, t_bq), (bf, t_bf), (bg, t_bg) = bks
            t = av(FF, bf[:, :], ACT.Sigmoid, t_bf, *prev)
            banks.put(bf, t)
            t_f = ts(V, FF, FF, lw[:, 16 + h:17 + h], lw[:, 12 + h:13 + h], ALU.mult, ALU.add, t, t_lb)
            t = av(GG, FF, ACT.Ln, t_f)
            t_k = ts(V, FF, FF, -1.0, 1.0, ALU.mult, ALU.add, t)
            V.wait(t, t_tab, t_k)
            t_g = V.inc(nc.vector.tensor_tensor_scan(GG, RST, GG, 0.0, ALU.mult, ALU.add))
            t = av(EX, GG, ACT.Exp, t_g)
            t_qd = tt(V, QD, bq[:, :], EX, ALU.mult, t, t_bq)
            banks.put(bq, t_qd)
            ev = EX.rearrange("p (c n) -> p c n", c=8)
            dc = sm[:, 40:48]
            t_dc = cp(V, dc, ev[:, :, 63], t, *prev)
            t = av(KD, GG, ACT.Exp, t_g, scale=-1.0)
            t_kd = tt(V, KD, KD, FF, ALU.mult, t, t_k)
            gv = GG.rearrange("p (c n) -> p c n", c=8)
            t = tt(V, KW.rearrange("p (c n) -> p c n", c=8), gv[:, :, 63:64].to_broadcast([128, 8, 64]), gv,
                   ALU.subtract, t_kd)
            t = av(KW, KW, ACT.Exp, t)
            t_kw = tt(V, KW, KW, FF, ALU.mult, t)
            t_hg = av(HGB, bg[:, :], ACT.Silu, t_bg)
            banks.put(bg, t_hg)
            bank = banks.get(T)
            T.wait(t_qd, t_kd)
            for c in range(4):
                cs = slice(c * 128, (c + 1) * 128)
                ins = mm(bank[:, cs], KD[:, cs], QD[:, cs], start=True, stop=True)
            t = T.inc(ins)
            V.wait(t)
            t_att = V.inc(nc.vector.copy_predicated(ATT.rearrange("p (c n) -> p c n", c=4),
                                                    hgm.unsqueeze(1).to_broadcast([128, 4, 128]),
                                                    bank[:, :].rearrange("p (c n) -> p c n", c=4)))
            banks.put(bank, t_att)
            _t, t_kwt = turn(A, KWT, [KW[:, c * 128:(c + 1) * 128] for c in range(4)], t_kw)
            bo = banks.get(T)
            T.wait(t_kwt)
            b4 = [banks.get(T), banks.get(T)]
            for c in range(8):
                pp = slice(64 * (c % 2), 64 * (c % 2) + 64)
                t_u = T.inc(mm(b4[c % 2][:, (c // 2) * 128:(c // 2 + 1) * 128], KWT[pp, c // 2, :],
                               HV[pp, c // 2, h * 128:(h + 1) * 128], start=True, stop=True))
            t_s = t_at0
            tss = [t_at0]
            for c in range(7):
                t_s = stt(SS[c + 1], SS[c], dc[:, c:c + 1], b4[c % 2][:, (c // 2) * 128:(c // 2 + 1) * 128],
                          ALU.mult, ALU.add, t_u, t_s, t_dc)
                tss.append(t_s)
            for b_ in b4:
                banks.put(b_, t_s)
            T.wait(t_att)
            for c in range(4):
                for j in range(2):
                    cj = 2 * c + j
                    cs = slice(cj * 64, (cj + 1) * 64)
                    T.wait(tss[cj])
                    mm(bo[:, cs], HV[:, c, h * 128:(h + 1) * 128], ATT[:, cs], start=True, stop=False)
                    ins = mm(bo[:, cs], SS[cj], QD[:, cs], start=False, stop=True)
            t_o = T.inc(ins)
            t = av(REC, bo[:, :], ACT.Square, t_o)
            b5, t = rows_sum(REC, "o128", t)
            t, t0 = rsqrt(EX, b5[:, :], 1e-6, t)
            banks.put(b5, t0)
            t = stt(EX, bo[:, :], C("hn", 0), EX, ALU.mult, ALU.mult, t)
            banks.put(bo, t)
            t_mx2 = tt(V, MX[:, 4 + h, :], EX, HGB, ALU.mult, t, t_hg)
        for c in range(0, 8, 2):
            sl = pair_load(I["wo2"], c)
            wv = ring.view(sl, 2048, 16)
            for j in range(2):
                bank = banks.get(T)
                t = chain(bank[:, :], [(wv[:, 8 * j + k, :], MX[:, k, :]) for k in range(8)], sl[1], t_mx2, t_mx)
                t_x = tt(V, XT[:, c + j, :], bank[:, :], XT[:, c + j, :], ALU.add, t)
                banks.put(bank, t_x)
            ring.done(sl, t)
        t_x = ffn("n2", I["f21"], I["f23"], I["f22"], t_x)
        S.wait(t_x)
        t = d_o.inc(nc.sync.dma_start(outT, XT[:, :, :]))
        S.wait(t)


def _chunks(w, kc=None):
    k, n = w.shape
    return np.ascontiguousarray(w.reshape(k // 128, 128, n // 128, 128).transpose(2, 1, 0, 3)).reshape(
        n // 128, 128, k)


def _rows(w):
    k, n = w.shape
    return np.ascontiguousarray(w.reshape(k // 128, 128, n).transpose(1, 0, 2))


def _cols(v):
    return v.reshape(-1, 128).T


def _constants():
    f = np.float32
    i = np.arange(128)
    m, n = i[:, None], i[None, :]
    km = np.zeros((128, NKM), f)

    def put(name, a):
        a = np.asarray(a, f)
        km[:, KM[name]:KM[name] + a.shape[1]] = a

    put("ident", m == n)
    put("ones", np.ones((128, 128)))
    put("o1024", np.full((128, 128), 1 / 1024))
    put("o2048", np.full((128, 128), 1 / 2048))
    put("hb", (m // 64 == n // 64) / 64)
    put("o128", np.full((128, 128), 1 / 128))
    put("triU", m <= n)
    put("triL", m >= n)
    put("sU", m < n)
    put("sL", m > n)
    put("mF", np.where(n >= m, 0, -1e30))
    put("mB", np.where(n <= m, 0, -1e30))
    md = n % 64
    put("psw", ((md < 8) & (m == n + 8)) | ((md >= 8) & (md < 16) & (m == n - 8)))
    put("iota", np.broadcast_to(n, (128, 128)))
    put("iotag", np.broadcast_to(np.arange(32)[None] // 8, (128, 32)))
    t, k = np.arange(8)[None] // 2, np.arange(8)[None] % 2
    put("tok", t * 128 + m + 1)
    put("aid", (t * 128 + m) * 2 + k + 1)
    put("slot", 1025.0 + m)
    km[:, KM["hgm"]:KM["hgm"] + 128] = np.where((m // 64 == n // 64) & (m <= n), 1, 0).astype(np.uint32).view(f)
    pos = np.arange(512)
    inv = (f(500000.0) ** (-np.arange(0, 16, 2, dtype=f) / f(16))).astype(f)
    ang = pos.astype(f)[:, None] * inv[None]
    cs = np.zeros((128, 2, 512), f)
    cs[:, 0] = 1
    for p in range(128):
        d = p % 64
        if d < 16:
            cs[p, 0] = np.cos(ang[:, d % 8])
            cs[p, 1] = np.sin(ang[:, d % 8]) * (-1 if d < 8 else 1)
    q, s = pos[:, None], pos[None, :]
    df = q - s
    cnt = ((df >= 0) & (df <= 128)).astype(int) + ((df >= 0) & (df % 4 == 0)) + ((df >= 0) & (df % 16 == 0))
    al = np.where(cnt > 0, np.log(np.maximum(cnt, 1)), -1e30).astype(f).reshape(4, 128, 512).transpose(1, 0, 2)
    rst = np.broadcast_to((pos % 64 != 0).astype(f)[None], (128, 512))
    pm = np.zeros((4, 512, 512), f)
    for g, w in enumerate((2, 4, 8, 16)):
        def win(n_):
            a = np.arange(n_)
            lo, hi = np.clip(a - w // 2, 0, n_), np.clip(a - w // 2 + w, 0, n_)
            return ((a[None] >= lo[:, None]) & (a[None] < hi[:, None])) / (hi - lo)[:, None].astype(np.float64)
        pm[g] = (np.kron(win(8), win(64)) - np.eye(512)).T
    pm = pm.reshape(4, 4, 128, 512).transpose(0, 2, 1, 3)
    c = np.ascontiguousarray
    return {"km": km, "cs": cs, "al": c(al), "rst": c(rst), "pm": c(pm)}


def _lay_out(x):
    a = {k: np.asarray(v) for k, v in x.items()}
    w_in = a["w_in"][0]
    w2 = a["w_in_2"][0]
    pc = [_cols(a["b_ada"][0]), _cols(a["b_gate"][0]),
          a["conv_w"][0].reshape(5, 24, 128).transpose(2, 1, 0).reshape(128, 120), _cols(a["conv_b"][0]),
          _cols(a["ssd_norm_g"][0]), _cols(a["pool_scale"][0]), _cols(a["ln1_g"][0]), _cols(a["ln1_b"][0]),
          _cols(a["ln2_g"][0]), _cols(a["ln2_b"][0]), _cols(a["ffn1_norm_2"][0]), _cols(a["mix_norm_2"][0]),
          _cols(a["ffn2_norm_2"][0]), np.tile(a["q_norm_2"][0], 2)[:, None], np.tile(a["k_norm_2"][0], 2)[:, None],
          _cols(a["hg_lb_logits_2"][0]), _cols(a["hg_lb_logits_2"][1]), a["hg_out_norm_2"][0][:, None],
          np.stack([_cols(a["c"][0]), _cols(a["c_ctx"])], axis=2).reshape(128, 16)]
    pr = np.concatenate([a["dt_bias"].reshape(-1), a["a_log"].reshape(-1), a["d_skip"].reshape(-1),
                         a["b_router_group"].reshape(-1), a["b_router_expert"].reshape(-1)])
    wre = a["w_router_expert"][0].transpose(1, 0, 2).reshape(1024, 32)
    ab = w2
    r = {
        "pc": np.ascontiguousarray(np.concatenate(pc, axis=1)),
        "pr": np.ascontiguousarray(np.broadcast_to(pr[None], (128, NPR))),
        "xT": _rows(np.ascontiguousarray(a["x"][0].T)), "ctxT": _rows(np.ascontiguousarray(a["ctx"][0].T)),
        "wada": _chunks(a["w_ada"][0]), "wdt": _rows(w_in[:, 5120:5184]),
        "wz": _chunks(w_in[:, 0:2048]), "wxbc": _chunks(w_in[:, 2048:5120]),
        "wu": _rows(w_in[:, 5184:6208]), "wg": _chunks(w_in[:, 6208:8256]),
        "pw": _rows(a["pool_w"][0].reshape(1024, 256)),
        "wa": _chunks(a["w_branch_a"][0]), "wb": _chunks(a["w_branch_b"][0]), "wo": _chunks(a["w_out"][0]),
        "wr": _rows(np.concatenate([a["w_router_group"][0], wre], axis=1)),
        "eg": a["w_expert_gate"][0], "eu": a["w_expert_up"][0], "ed": a["w_expert_down"][0],
        "w2in": _chunks(np.concatenate([ab[:, 0:1024], ab[:, 1536:2560], ab[:, 3072:3584]], axis=1)),
        "w2v": _rows(ab[:, 1024:1536]), "w2i": _rows(ab[:, 2560:3072]), "wo2": _chunks(a["w_out_2"][0]),
        "f11": _chunks(a["ffn1_w1_2"][0]), "f13": _chunks(a["ffn1_w3_2"][0]), "f12": _chunks(a["ffn1_w2_2"][0]),
        "f21": _chunks(a["ffn2_w1_2"][0]), "f23": _chunks(a["ffn2_w3_2"][0]), "f22": _chunks(a["ffn2_w2_2"][0]),
    }
    r.update(_constants())
    return r


def kernel(**inputs):
    import concourse.bacc as _bacc
    from concourse.bass_utils import run_bass_kernel_spmd as _run

    arrays = _lay_out(inputs)
    nc = _bacc.Bacc("TRN2", target_bir_lowering=False, num_devices=1)
    aps = {}
    for name, a in arrays.items():
        aps[name] = nc.dram_tensor("in_" + name, a.shape, F32, kind="ExternalInput").ap()
    out = nc.dram_tensor("out_x", (128, 8, 512), F32, kind="ExternalOutput").ap()
    build(nc, aps, out)
    r = _run(nc, [{"in_" + k: v for k, v in arrays.items()}], core_ids=[0])
    y = r.results[0]["out_x"]
    return np.ascontiguousarray(y.transpose(2, 1, 0).reshape(1, 512, 1024))
```

```python
from contextlib import ExitStack

import numpy as np

import concourse.bass as bass
from concourse import mybir

F32 = mybir.dt.float32
FR = mybir.dt.float32r
I32 = mybir.dt.int32
U32 = mybir.dt.uint32
ALU = mybir.AluOpType
ACT = mybir.ActivationFunctionType
AX = mybir.AxisListType

ALPHA = 2.0 ** 0.25
CAP = 128
NOV = 7
POOL_SPLITS = False
OVB = 3
NBLK = 32 + NOV
NRAW = 4
NHL = 5
WORDS = 53200
AHEAD = 4

PC = {}
_n = 0
for _name, _w in (("b_ada", 48), ("b_gate", 16), ("conv_w", 120), ("conv_b", 24), ("ssd_g", 16),
                  ("pool_scale", 8), ("ln1_g", 8), ("ln1_b", 8), ("ln2_g", 8), ("ln2_b", 8),
                  ("n1", 8), ("nm", 8), ("n2", 8), ("qn", 1), ("kn", 1), ("lb0", 4), ("lb1", 4),
                  ("hn", 1), ("cc", 16)):
    PC[_name] = _n
    _n += _w
NPC = _n
PR_DTB, PR_ALOG, PR_SKIP, PR_RB = 0, 64, 128, 160
NPR = 196
KM = {}
_n = 0
for _name in ("ident", "ones", "o1024", "o2048", "hb", "o128", "triU", "triL", "sU", "sL", "mF", "mB", "psw",
              "iota"):
    KM[_name] = _n
    _n += 128
KM["iotag"] = _n
_n += 32
KM["tok"] = _n
_n += 8
KM["aid"] = _n
_n += 8
KM["slot"] = _n
_n += 1
KM["hgm"] = _n
_n += 128
KM["eps5"] = _n
KM["eps6"] = _n + 1
_n += 8
NKM = _n


class Eng:

    def __init__(self, e, sem):
        self.e, self.sem, self.n, self.seen = e, sem, 0, {}

    def wait(self, *toks):
        for t in toks:
            if t is None:
                continue
            sem, v = t
            if self.seen.get(id(sem), 0) < v:
                self.e.wait_ge(sem, v)
                self.seen[id(sem)] = v

    def inc(self, ins):
        ins.then_inc(self.sem, 1)
        self.n += 1
        return (self.sem, self.n)

    def now(self):
        return (self.sem, self.n) if self.n else None


class Dma:

    def __init__(self, sem):
        self.sem, self.n = sem, 0

    def inc(self, ins):
        ins.then_inc(self.sem, 16)
        self.n += 16
        return (self.sem, self.n)

    def now(self):
        return (self.sem, self.n) if self.n else None


class Banks:

    def __init__(self, banks):
        self.free = [(b, None) for b in banks]

    def get(self, eng):
        b, t = self.free.pop(0)
        eng.wait(t)
        return b

    def put(self, b, tok):
        self.free.append((b, tok))


def resolve(I, key):
    name, c = key[0], key[1]
    w = I[name]
    if name in ("eg", "eu"):
        return w[c].rearrange("(k p) n -> p k n", p=128)[:, 2 * key[2]:2 * key[2] + 2, :]
    if name == "ed":
        return w[c].rearrange("(k p) n -> p k n", p=128)[:, key[2]:key[2] + 1, :]
    if name in ("wu", "w2v", "w2i"):
        return w[:, 4 * key[2]:4 * key[2] + 4, c * 256:(c + 1) * 256]
    if name == "pm":
        return w[c][:, 2 * key[2]:2 * key[2] + 2, :]
    if name in ("pw", "wdt", "wr"):
        return w[:, c:c + 4, :] if name == "pw" else w[:, :, :]
    k0 = key[2] if len(key) > 2 else 0
    k1 = min(k0 + 1024, w.shape[2])
    if name in ("f12", "f22") and k0 < 1408:
        k1 = min(k1, 1408)
    return w[c][:, k0:k1].rearrange("p (a b) -> p a b", b=128)


class Ring:

    def __init__(self, plan, src, raw, hl, S, A, V, G, dmas, inc_free):
        self.plan, self.src, self.raw, self.hl = plan, src, raw, hl
        self.S, self.A, self.V, self.G, self.dmas = S, A, V, G, dmas
        self.i = 0
        self.nl = self.ns = 0
        self.raw_free = [None] * NRAW
        self.hl_free = [(h, None) for h in range(NHL)]
        self.slot = {}
        self.loaded = {}
        self.ready = {}
        self.inc_free = inc_free
        self.stop = None
        self.keys = []

    def advance(self):
        while self.nl < self.limit() and self.raw_free[self.nl % NRAW] != "held":
            n, r = self.nl, self.nl % NRAW
            key = self.plan[n][0]
            s = self.src(key)
            self.S.wait(self.raw_free[r])
            self.raw_free[r] = "held"
            a, b = s.shape[1], s.shape[2]
            dst = self.raw[:, r, 0:a * b].rearrange("p (a b) -> p a b", a=a)
            self.loaded[n] = (self.dmas[r].inc(self.S.e.dma_start(dst, s)), a, b)
            self.nl += 1
        while self.ns < min(self.nl, self.i + AHEAD) and self.split_one():
            pass

    def limit(self):
        if self.stop:
            for n, (key, _kind) in enumerate(self.plan):
                if key[0] == self.stop:
                    return n
        return len(self.plan)

    def split_one(self):
        n = self.ns
        key, kind = self.plan[n]
        r = n % NRAW
        tok, a, b = self.loaded[n]
        w = a * b
        if kind == "raw":
            self.ready[n] = (self.raw[:, r, 0:w].rearrange("p (a b) -> p a b", a=a), None, tok, ("raw", r))
            self.ns += 1
            return True
        if not self.hl_free:
            return False
        h, freed = self.hl_free.pop(0)
        hi, lo = self.hl[:, h, 0, 0:w], self.hl[:, h, 1, 0:w]
        rw = self.raw[:, r, 0:w]
        self.A.wait(tok, freed)
        t = self.A.inc(self.A.e.activation(hi, rw, ACT.Copy))
        L = self.G if kind == "pool" else self.V
        L.wait(tok, freed, t)
        t = L.inc(L.e.tensor_tensor(lo, rw, hi.bitcast(F32), ALU.subtract))
        self.raw_free[r] = t
        self.ready[n] = (hi.rearrange("p (a b) -> p a b", a=a), lo.rearrange("p (a b) -> p a b", a=a), t, ("hl", h))
        self.ns += 1
        return True

    def get(self, *key, kind="split"):
        if self.inc_free:
            self.keys.append((key, kind))
            self.plan.append((key, kind))
        assert self.plan[self.i] == (key, kind), (self.plan[self.i], key, kind)
        self.advance()
        n = self.i
        self.i += 1
        assert n in self.ready, ("a slot is held too long", key)
        self.advance()
        return self.ready.pop(n)

    def done(self, e, tok):
        kind, i = e[3]
        if kind == "raw":
            self.raw_free[i] = tok
        else:
            self.hl_free.append((i, tok))
        self.advance()


def build(nc, I, outT, plans=None):
    ctx = ExitStack()
    with ctx:
        def sb(name, shape, dt=F32):
            return ctx.enter_context(nc.sbuf_tensor(name, shape, dt))

        def sem(name):
            return ctx.enter_context(nc.semaphore(name))

        banks = Banks([ctx.enter_context(nc.psum_tensor(f"bank{i}", [128, 512], F32)) for i in range(8)])
        T = Eng(nc.tensor, sem("s_pe"))
        V = Eng(nc.vector, sem("s_dve"))
        A = Eng(nc.scalar, sem("s_act"))
        G = Eng(nc.gpsimd, sem("s_pool"))
        S = Eng(nc.sync, sem("s_sp"))
        arena = sb("arena", [128, WORDS])
        base = nc.sbuf_base - 4 * WORDS
        at = [0]

        def place(name, shape, dt=F32, off=None):
            w = 1
            for x in shape[1:]:
                w *= x
            o_ = at[0] if off is None else off
            w = (w + 7) // 8 * 8
            if off is None:
                at[0] += w
            assert o_ + w <= WORDS, (name, o_ + w)
            return nc.alloc_sbuf_tensor_at(name, shape, dt, offset=base + 4 * o_)

        raw = place("raw", [128, NRAW, 1024])
        HLB = place("HLB", [128, NHL, 2, 1024], FR)
        dry = plans is None
        ring = Ring([] if dry else plans[0], lambda k: resolve(I, k), raw, HLB, S, A, V, G,
                    [Dma(sem(f"s_ring{i}")) for i in range(NRAW)], dry)
        d_c = Dma(sem("d_c"))
        d_x = Dma(sem("d_x"))
        d_h = Dma(sem("d_h"))
        d_g = Dma(sem("d_g"))
        d_s = Dma(sem("d_s"))
        d_y = Dma(sem("d_y"))
        d_t = Dma(sem("d_t"))
        d_o = Dma(sem("d_o"))

        ZD = nc.dram_tensor("z_scratch", (16, 128, 512), F32, kind="Internal").ap()
        GD = nc.dram_tensor("g_scratch", (16, 128, 512), F32, kind="Internal").ap()
        UD = nc.dram_tensor("u_scratch", (4, 128, 4, 256), F32, kind="Internal").ap()
        YZD = nc.dram_tensor("yz_scratch", (16, 128, 512), F32, kind="Internal").ap()
        H2 = nc.dram_tensor("h2_scratch", (512, 1024), F32, kind="Internal").ap()
        YD = nc.dram_tensor("y_scratch", (1024, 1024), F32, kind="Internal").ap()

        km = place("km", [128, NKM])
        pc = place("pc", [128, NPC])
        pr = place("pr", [128, NPR])
        HTh = place("HTh", [128, 8, 512], FR)
        HTl = place("HTl", [128, 8, 512], FR)
        mod = place("mod", [128, 48, 2])
        sm = place("sm", [128, 80])
        wk = place("wk", [128, 4, 2])
        gi = place("gi", [128, 4, 8], U32)
        vi = place("vi", [128, 4, 8], U32)
        eidi = place("eidi", [128, NOV + 1], I32)
        ix = place("ix", [128, 2, NBLK], U32)
        SQ = place("SQ", [128, 512])
        RA = place("RA", [128, 512])
        TMP = [place(f"tmp{i}", [128, 512]) for i in range(6)]
        DEC = at[0]
        dec = place("dec", [128, 6, 64])
        acs = place("acs", [128, 4, 64])
        eacs = place("eacs", [128, 4, 64])
        tw = place("tw", [128, 4, 64])
        etot = place("etot", [128, 4, 64])
        cw = place("cw", [128, 2, 64])
        ats = place("ats", [64, 512])
        DEC_END = at[0]
        W0 = at[0]
        XT = place("XT", [128, 8, 512])
        W1 = at[0]
        cur = [0]

        def here(name, shape, dt=F32):
            w = 1
            for x in shape[1:]:
                w *= x
            t_ = place(name, shape, dt, off=cur[0])
            cur[0] += (w + 7) // 8 * 8
            return t_

        def phase(start):
            cur[0] = start

        mm, act = nc.tensor.matmul, nc.scalar.activation

        def K(name, w=128, p=128):
            return km[0:p, KM[name]:KM[name] + w]

        def C(name, i, w=1):
            return pc[:, PC[name] + i:PC[name] + i + w]

        def tt(E, out, a, b, op, *waits):
            E.wait(*waits)
            return E.inc(E.e.tensor_tensor(out, a, b, op))

        def ts(E, out, a, s1, s2, op0, op1, *waits):
            E.wait(*waits)
            if s2 is None:
                return E.inc(E.e.tensor_scalar(out, a, s1, None, op0))
            return E.inc(E.e.tensor_scalar(out, a, s1, s2, op0, op1))

        def stt(out, a, s, b, op0, op1, *waits):
            V.wait(*waits)
            return V.inc(nc.vector.scalar_tensor_tensor(out=out, in0=a, scalar=s, in1=b, op0=op0, op1=op1))

        def recip(out, a, *waits):
            V.wait(*waits)
            return V.inc(nc.vector.reciprocal(out, a))

        def rsqrt(out, a, eps, *waits):
            t0 = av(out, a, ACT.Ln, *waits, bias=K(eps, 1))
            return av(out, out, ACT.Exp, t0, scale=-0.5), t0

        def av(out, a, f, *waits, **kw):
            A.wait(*waits)
            return A.inc(act(out, a, f, **kw))

        def cp(E, out, a, *waits):
            if E is A:
                return av(out, a, ACT.Copy, *waits)
            E.wait(*waits)
            return E.inc(E.e.tensor_copy(out, a))

        def bc(ap, n):
            return ap.unsqueeze(2).to_broadcast([ap.shape[0], ap.shape[1], n])

        def split(hi, lo, src, *waits):
            t1 = cp(A, hi, src, *waits)
            return tt(V, lo, src, hi.bitcast(F32), ALU.subtract, t1, *waits)

        def prod(bank, parts, *waits, start=True, stop=True, xt=None):
            T.wait(*waits)
            n = len(parts)
            for i, (ah, al, bh, bl) in enumerate(parts):
                if xt:
                    T.wait(xt[i])
                mm(bank, ah, bh, start=(start and i == 0), stop=False)
                mm(bank, ah, bl, start=False, stop=False)
                ins = mm(bank, al, bh, start=False, stop=(stop and i == n - 1))
            return T.inc(ins)

        def feature(bank, e, xh, xl, *waits, k0=0, n=8, **kw):
            return prod(bank, [(e[0][:, k, :], e[1][:, k, :], xh[:, k0 + k, :], xl[:, k0 + k, :]) for k in range(n)],
                        e[2], *waits, **kw)

        def chain(bank, pairs, *waits, m=128, inc=True):
            T.wait(*waits)
            for i, (l, r) in enumerate(pairs):
                ins = mm(bank, l, r, start=(i == 0), stop=(i == len(pairs) - 1))
            return T.inc(ins) if inc else None

        def rows_sum(acc, kname, *waits):
            bank = banks.get(T)
            return bank, chain(bank[:, :], [(K(kname), acc)], *waits)

        tc = d_c.inc(nc.scalar.dma_start(pc[:, :], I["pc"]))
        tc = d_c.inc(nc.scalar.dma_start(km[:, :], I["km"]))
        tc = d_c.inc(nc.scalar.dma_start(pr[:, :], I["pr"]))
        phase(W1)
        CTX = here("CTX", [128, 8, 256])
        tx = d_x.inc(nc.scalar.dma_start(XT[:, :, :], I["xT"]))
        tx = d_x.inc(nc.scalar.dma_start(CTX[:, :, :], I["ctxT"]))
        sc = sm[:, 64:80]
        t_sc = av(sc, C("cc", 0, 16), ACT.Silu, tc)

        def modulation(c0, c1):
            bank = banks.get(T)
            T.wait(t_sc)
            for c in range(c0, c1):
                e = ring.get("wada", c, kind="raw")
                T.wait(e[2])
                for k in range(8):
                    ins = mm(bank[:, 2 * (c - c0):2 * (c - c0) + 2], e[0][:, k, :], sc[:, 2 * k:2 * k + 2],
                             start=(k == 0), stop=(k == 7))
                t = T.inc(ins)
                ring.done(e, t)
            n = c1 - c0
            V.wait(t)
            t = V.inc(nc.vector.tensor_tensor(mod[:, c0:c1, :], bank[:, 0:2 * n].rearrange("p (c j) -> p c j", j=2),
                                              bc(pc[:, PC["b_ada"] + c0:PC["b_ada"] + c1], 2), ALU.add))
            banks.put(bank, t)
            return t

        t = modulation(0, 16)
        t_mod01 = ts(V, mod[:, 8:16, :], mod[:, 8:16, :], 1.0, None, ALU.add, None, t)
        phase(W0 + 4096 + 8192)
        HCh = here("HCh", [128, 8, 256], FR)
        HCl = here("HCl", [128, 8, 256], FR)
        for k in range(8):
            t1 = ts(V, XT[:, k, :], XT[:, k, :], mod[:, 8 + k, 0:1], mod[:, k, 0:1], ALU.mult, ALU.add, t_mod01, tx)
            t2 = ts(V, CTX[:, k, :], CTX[:, k, :], mod[:, 8 + k, 1:2], mod[:, k, 1:2], ALU.mult, ALU.add)
            t_h = split(HTh[:, k, :], HTl[:, k, :], XT[:, k, :], t1)
            t_hc = split(HCh[:, k, :], HCl[:, k, :], CTX[:, k, :], t2)

        phase(W0)
        XS = here("XS", [128, 4, 512])
        BT = here("BT", [128, 512])
        CTt = here("CTt", [128, 512])
        Bt = here("Bt", [128, 4, 128])
        CBT = here("CBT", [128, 512])
        XC = here("XC", [128, 2, 512])
        Bc = here("Bc", [128, 2, 128])
        ST = [here(f"ST{d}", [128, 512]) for d in range(2)]
        Y = here("Y", [128, 4, 512])
        XCW = here("XCW", [128, 2, 512])
        XD = [here(f"XD{i}", [128, 2, 4, 64]) for i in range(2)]
        FB = [here(f"FB{i}", [128, 512]) for i in range(2)]
        assert cur[0] <= W0 + 4096 + 8192
        phase(W0 + 4096 + 8192 + 4096)
        CB = [here(f"CB{i}", [128, 776]) for i in range(2)]
        CA = [here(f"CA{i}", [128, 776]) for i in range(2)]
        YZT = [here(f"YZT{i}", [128, 512]) for i in range(2)]
        SQ2, SQ3 = here("SQ2", [128, 512]), here("SQ3", [128, 512])
        E4 = [[TMP[0], TMP[1]], [TMP[2], TMP[3]]]
        V.wait(t_hc)
        for b in CB:
            t_pad = V.inc(nc.vector.memset(b[:, :], 0.0))
        t_sq = V.inc(nc.vector.memset(SQ[:, :], 0.0))
        A.wait(t_pad)
        G.wait(t_sq, t_hc)
        SE = [TMP[2], TMP[3]]
        cb_free = [None, None]
        ca_free = [None, None]
        nconv = 0
        yz_z = [None, None]
        d_z = [Dma(sem(f"d_z{i}")) for i in range(2)]
        d_yz = [Dma(sem(f"d_yz{i}")) for i in range(2)]
        ZB = [SQ2, RA]

        d_fb = [Dma(sem(f"d_fb{i}")) for i in range(2)]
        spilled = {}
        nf = [0]

        def spill(bank, dst, t):
            i = nf[0] % 2
            nf[0] += 1
            w = bank.shape[1]
            t = cp(A, FB[i][:, 0:w], bank, t, d_fb[i].now())
            A.wait(t)
            tok = d_fb[i].inc(nc.scalar.dma_start(dst, FB[i][:, 0:w]))
            return t, tok

        def fill():
            for q in range(16):
                e = ring.get("wz", q)
                bank = banks.get(T)
                t = feature(bank[:, :], e, HTh, HTl)
                ring.done(e, t)
                t, spilled[("z", q)] = spill(bank[:, :], ZD[q], t)
                banks.put(bank, t)
                yield
            for q in range(16):
                e = ring.get("wg", q)
                bank = banks.get(T)
                t = feature(bank[:, :], e, HTh, HTl)
                ring.done(e, t)
                t, spilled[("g", q)] = spill(bank[:, :], GD[q], t)
                banks.put(bank, t)
                yield
            for c in range(4):
                es = [ring.get("wu", c, a) for a in range(2)]
                for i in range(4):
                    cs = slice(i * 128, (i + 1) * 128)
                    bank = banks.get(T)
                    t = prod(bank[:, 0:256], [(HTh[:, k, cs], HTl[:, k, cs], es[k // 4][0][:, k % 4, :],
                                               es[k // 4][1][:, k % 4, :]) for k in range(8)], es[0][2], es[1][2])
                    if i == 3:
                        for e in es:
                            ring.done(e, t)
                    t, spilled[("u", c, i)] = spill(bank[:, 0:256], UD[c, :, i, :], t)
                    banks.put(bank, t)
                    yield
            bank = banks.get(T)
            for c in range(16, 48):
                e = ring.get("wada", c, kind="raw")
                T.wait(e[2])
                for k in range(8):
                    ins = mm(bank[:, 2 * (c - 16):2 * (c - 16) + 2], e[0][:, k, :], sc[:, 2 * k:2 * k + 2],
                             start=(k == 0), stop=(k == 7))
                t = T.inc(ins)
                ring.done(e, t)
                if c % 2:
                    yield
            V.wait(t)
            t = V.inc(nc.vector.tensor_tensor(mod[:, 16:48, :], bank[:, 0:64].rearrange("p (c j) -> p c j", j=2),
                                              bc(pc[:, PC["b_ada"] + 16:PC["b_ada"] + 48], 2), ALU.add))
            banks.put(bank, t)
            spilled["mod"] = ts(V, mod[:, 32:40, :], mod[:, 32:40, :], 1.0, None, ALU.add, None, t)

        filler = fill()

        def gap(n=1):
            for _i in range(n):
                next(filler, None)

        aa = TMP[5][:, 0:384].rearrange("p (t h) -> p t h", t=6)
        e = ring.get("wdt", 0)
        bank = banks.get(T)
        T.wait(e[2], t_hc)
        for i in range(6):
            xh, xl, c = (HTh, HTl, i) if i < 4 else (HCh, HCl, i - 4)
            cs = slice(c * 128, (c + 1) * 128)
            t = prod(bank[:, i * 64:(i + 1) * 64],
                     [(xh[:, k, cs], xl[:, k, cs], e[0][:, k, :], e[1][:, k, :]) for k in range(8)])
        ring.done(e, t)
        gap(2)
        dtr, ab, e_, u_, l_ = (TMP[i][:, 0:384] for i in range(5))
        b3 = lambda o: pr[:, o:o + 64].unsqueeze(1).to_broadcast([128, 6, 64])
        r3 = lambda a: a.rearrange("p (t h) -> p t h", t=6)
        t = tt(V, r3(dtr), r3(bank[:, 0:384]), b3(PR_DTB), ALU.add, t, tc)
        banks.put(bank, t)
        t = av(ab, dtr, ACT.Abs, t)
        t = av(e_, ab, ACT.Exp, t, scale=-1.0)
        t_u = ts(V, u_, e_, 1.0, None, ALU.add, None, t)
        t_l = av(l_, u_, ACT.Ln, t_u)
        t_d = ts(V, ab, u_, -1.0, None, ALU.add, None, t_u)
        t_z = ts(V, u_, ab, 0.0, None, ALU.is_equal, None, t_d, t_l)
        t = tt(V, ab, ab, u_, ALU.add, t_z)
        t = recip(ab, ab, t)
        t = tt(V, ab, e_, ab, ALU.mult, t)
        t_q = tt(V, l_, l_, ab, ALU.mult, t, t_l)
        t = tt(V, u_, u_, e_, ALU.mult, t_z)
        t = tt(V, l_, l_, u_, ALU.add, t, t_q)
        dt2 = dec[:, :, :].rearrange("p t h -> p (t h)")
        t_dt = stt(dt2, dtr, 0.0, l_, ALU.max, ALU.add, t)
        t = av(sm[:, 0:64], pr[:, PR_ALOG:PR_ALOG + 64], ACT.Exp, t_dt)
        t = tt(V, aa, dec[:, :, :], sm[:, 0:64].unsqueeze(1).to_broadcast([128, 6, 64]), ALU.mult, t)
        t = ts(V, aa, aa, -1.0, None, ALU.mult, None, t)
        t_a = t
        gap(2)
        b1, b2 = banks.get(T), banks.get(T)
        T.wait(t_a)
        v1 = b1[:, 0:256].rearrange("p (t h) -> p t h", t=4)
        v2 = b2[:, 0:256].rearrange("p (t h) -> p t h", t=4)
        for i in range(4):
            mm(v1[:, i, 0:32], K("triU"), aa[:, i, 0:32], start=True, stop=True)
            mm(v1[:, i, 32:64], K("triL"), aa[:, i, 32:64], start=True, stop=True)
            mm(v2[:, i, :], K("ones"), aa[:, i, :], start=True, stop=True)
        v3 = b2[:, 256:384].rearrange("p (t h) -> p t h", t=2)
        mm(v3[:, 0, 0:32], K("sL"), aa[:, 4, 0:32], start=True, stop=False)
        mm(v3[:, 0, 0:32], K("ones"), aa[:, 5, 0:32], start=False, stop=True)
        mm(v3[:, 1, 0:32], K("sL"), aa[:, 5, 0:32], start=True, stop=True)
        mm(v3[:, 0, 32:64], K("sU"), aa[:, 4, 32:64], start=True, stop=True)
        mm(v3[:, 1, 32:64], K("sU"), aa[:, 5, 32:64], start=True, stop=False)
        t = T.inc(mm(v3[:, 1, 32:64], K("ones"), aa[:, 4, 32:64], start=False, stop=True))
        t_acs = cp(V, acs[:, :, :], v1, t)
        banks.put(b1, t_acs)
        t_tl = tt(V, tw[:, :, :], v2, acs[:, :, :], ALU.subtract, t_acs)
        t_e1 = av(etot[:, :, :], v2, ACT.Exp, t_tl)
        t_e2 = av(cw[:, :, :], v3, ACT.Exp, t)
        banks.put(b2, t_e2)
        t_b2 = t_tl
        t_e3 = av(tw[:, :, :], tw[:, :, :], ACT.Exp, t_tl)
        t_e4 = av(eacs[:, :, :], acs[:, :, :], ACT.Exp, t_acs)
        tt(V, tw[:, :, :], tw[:, :, :], dec[:, 0:4, :], ALU.mult, t_e3)
        t_co = tt(V, cw[:, :, :], cw[:, :, :], dec[:, 4:6, :], ALU.mult, t_e4)
        gap()
        bank = banks.get(T)
        T.wait(t_acs, t_b2)
        for i in range(4):
            ins = nc.tensor.transpose(bank[0:64, i * 128:(i + 1) * 128], acs[:, i, :], K("ident"))
        t = T.inc(ins)
        t_ats = cp(V, ats[:, :], bank[0:64, :], t)
        banks.put(bank, t_ats)

        def conv_chunk(xc, e, ctx_too):
            nonlocal nconv
            i = nconv % 2
            nconv += 1
            bank = banks.get(T)
            t = feature(bank[:, :], e, HTh, HTl, t_h)
            t1 = cp(A, CB[i][:, 2:514], bank[:, :], t, cb_free[i])
            banks.put(bank, t1)
            n = 512
            if ctx_too:
                bank = banks.get(T)
                t = feature(bank[:, 0:256], e, HCh, HCl, t_hc)
                t1 = cp(A, CB[i][:, 516:772], bank[:, 0:256], t)
                banks.put(bank, t1)
                n = 770
            t_pe = t
            t = ts(V, CA[i][:, 0:n], CB[i][:, 0:n], C("conv_w", xc * 5), C("conv_b", xc), ALU.mult, ALU.add,
                   t1, ca_free[i])
            for j in range(1, 5):
                t = stt(CA[i][:, 0:n], CB[i][:, j:j + n], C("conv_w", xc * 5 + j), CA[i][:, 0:n], ALU.mult, ALU.add, t)
            cb_free[i] = t
            t = av(CA[i][:, 0:n], CA[i][:, 0:n], ACT.Silu, t)
            return i, t, t_pe

        def turn(E, dst, srcs, *waits):
            bank = banks.get(T)
            T.wait(*waits)
            n = len(srcs)
            for j, src in enumerate(srcs):
                ins = nc.tensor.transpose(bank[:, j * 128:(j + 1) * 128], src, K("ident"))
            t = T.inc(ins)
            v = bank[:, 0:n * 128]
            if len(dst.shape) == 3:
                v = v.rearrange("p (t n) -> p t n", t=n)
            t2 = cp(E, dst, v, t)
            banks.put(bank, t2)
            return t, t2

        def gate(g, t_y):
            nonlocal t_sq, t_yg
            for j in range(4):
                q = 4 * g + j
                A.wait(spilled[("z", q)], yz_z[j % 2])
                t = d_z[j % 2].inc(nc.scalar.dma_start(ZB[j % 2][:, :], ZD[q]))
                by = banks.get(T)
                T.wait(t_y)
                for c in range(4):
                    ins = nc.tensor.transpose(by[:, c * 128:(c + 1) * 128], Y[:, c, j * 128:(j + 1) * 128], K("ident"))
                t_yg = T.inc(ins)
                yield
                t_s = av(ZB[j % 2][:, :], ZB[j % 2][:, :], ACT.Silu, t)
                yz = YZT[j % 2]
                t_yz = tt(V, yz[:, :], ZB[j % 2][:, :], by[:, :], ALU.mult, t_yg, t_s, d_yz[j % 2].now())
                yz_z[j % 2] = t_yz
                banks.put(by, t_yz)
                t = tt(G, SQ3[:, :], yz[:, :], yz[:, :], ALU.mult, t_yz, t_sq)
                t_sq = tt(G, SQ[:, :], SQ[:, :], SQ3[:, :], ALU.add, t)
                t = av(yz[:, :], yz[:, :], ACT.Copy, t, scale=C("ssd_g", q))
                A.wait(t)
                d_yz[j % 2].inc(nc.scalar.dma_start(YZD[q], yz[:, :]))

        t_yg = None
        gating = None
        pe_end = v_end = g_end = None
        for g in range(4):
            order = [("b", 16 + g), ("c", 20 + g)] + [("x", 4 * g + j) for j in range(4)]

            def place_chunk(kind, xc, i, t):
                nonlocal t_xs, t_B, t_bt, t_ct
                ca = CA[i]
                blocks = [ca[:, c * 128:(c + 1) * 128] for c in range(4)]
                cblocks = [ca[:, 514 + c * 128:514 + (c + 1) * 128] for c in range(2)]
                A.wait(pe_end, v_end, g_end)
                V.wait(pe_end)
                if kind == "x":
                    q = xc - 4 * g
                    _a, ta = turn(A, XS[:, :, q * 128:(q + 1) * 128], blocks, t)
                    ca_free[i], tb = turn(V, XC[:, :, q * 128:(q + 1) * 128], cblocks)
                    t_xs = [ta, tb]
                elif kind == "b":
                    _a, ta = turn(A, Bt[:, :, :], blocks, t)
                    _b, tb = turn(V, Bc[:, :, :], cblocks)
                    t_B = [ta, tb]
                    t_bt = ca_free[i] = cp(G, BT[:, :], ca[:, 0:512], t, pe_end)
                    V.wait(_b)
                else:
                    t_ct = ca_free[i] = cp(G, CTt[:, :], ca[:, 0:512], t, pe_end)

            t_xs = t_B = t_bt = t_ct = None
            made = None
            for kind, xc in order:
                e = ring.get("wxbc", xc)
                i, t, t_pe = conv_chunk(xc, e, kind != "c")
                ring.done(e, t_pe)
                if gating:
                    next(gating, None)
                if made:
                    place_chunk(*made)
                made = (kind, xc, i, t)
            if gating:
                for _g in gating:
                    pass
            bank = banks.get(T)
            T.wait(t_bt, t_ct)
            for c in range(4):
                sl_ = slice(c * 128, (c + 1) * 128)
                ins = mm(bank[:, sl_], BT[:, sl_], CTt[:, sl_], start=True, stop=True)
            t = T.inc(ins)
            t_cb = cp(A, CBT[:, :], bank[:, :], t)
            banks.put(bank, t_cb)
            gap()
            place_chunk(*made)

            def heads(ap, d):
                return ap[:, 32 * d + 8 * g:32 * d + 8 * g + 8]

            def r8(ap):
                return ap.rearrange("p (h n) -> p h n", h=8)

            t_st, t_xw = [None, None], [None, None]
            xcw = [[XCW[:, i, :] for i in range(2)], [TMP[i][:, :] for i in range(2)]]
            for d in range(2):
                for i in range(2):
                    t_xw[d] = tt(V, r8(xcw[d][i]), r8(XC[:, i, :]), bc(heads(cw[:, i, :], d), 64), ALU.mult,
                                 t_xs[1], t_co, pe_end)
            gap()
            for d in range(2):
                bank = banks.get(T)
                t = chain(bank[:, :], [(Bc[:, i, :], xcw[d][i]) for i in range(2)], t_xw[d], t_B[1])
                t_st[d] = cp(A, ST[d][:, :], bank[:, :], t)
                banks.put(bank, t_st[d])
            t_ctx = t
            for c in range(4):
                t_y = tt(V, r8(Y[:, c, :]), r8(XS[:, c, :]), bc(pr[:, PR_SKIP + 8 * g:PR_SKIP + 8 * g + 8], 64),
                         ALU.mult, t_xs[0], t_yg)

            def decayed(h):
                out = []
                for d in range(2):
                    hh = 32 * d + 8 * g + h
                    E_ = E4[h % 2][d]
                    bank = banks.get(T)
                    t = chain(bank[:, :], [(K("ident", p=64)[:, hh:hh + 1].to_broadcast([64, 128]), ats[0:64, :])], t_ats)
                    for c in range(4):
                        cs = slice(c * 128, (c + 1) * 128)
                        t2 = stt(E_[:, cs], bank[:, cs], acs[:, c, hh:hh + 1], K("mF" if d == 0 else "mB"),
                                 ALU.subtract, ALU.min, t, e_free[h % 2])
                    banks.put(bank, t2)
                    t = av(E_[:, :], E_[:, :], ACT.Exp, t2)
                    t3 = tt(G, XD[h % 2][:, d, :, :], XS[:, :, h * 64:(h + 1) * 64],
                            dec[:, 0:4, hh:hh + 1].to_broadcast([128, 4, 64]), ALU.mult, e_free[h % 2], t_xs[0])
                    out.append((t, t3))
                return out

            t_ty = [None, None]
            tq = [TMP[4], TMP[5]]
            t_up = [None, None]
            e_free = [t_ctx, None]
            for step in range(4):
                cs_ = (step, 3 - step)
                t_se, b_o, b_u, t_o = [None] * 2, [None] * 2, [None] * 2, [None] * 2
                for d in range(2):
                    if step < 3:
                        t_se[d] = tt(V, r8(SE[d][:, :]), r8(XS[:, cs_[d], :]), bc(heads(tw[:, cs_[d], :], d), 64),
                                     ALU.mult, t_up[d], t_xs[0], pe_end)
                for d in range(2):
                    b_o[d] = banks.get(T)
                    t_o[d] = chain(b_o[d][:, :], [(CTt[:, cs_[d] * 128:(cs_[d] + 1) * 128], ST[d][:, :])], t_st[d])
                if step < 3:
                    for d in range(2):
                        b_u[d] = banks.get(T)
                        t_up[d] = chain(b_u[d][:, :], [(Bt[:, cs_[d], :], SE[d][:, :])], t_se[d], t_B[0])
                else:
                    next_e = decayed(0)
                for d in range(2):
                    c = cs_[d]
                    if step < 3:
                        t = tt(V, r8(ST[d][:, :]), r8(ST[d][:, :]), bc(heads(etot[:, c, :], d), 64), ALU.mult,
                               t_o[d], t_st[d])
                        t_st[d] = tt(V, ST[d][:, :], ST[d][:, :], b_u[d][:, :], ALU.add, t, t_up[d])
                        banks.put(b_u[d], t_st[d])
                for d in range(2):
                    c = cs_[d]
                    t = tt(V, r8(tq[d][:, :]), r8(b_o[d][:, :]), bc(heads(eacs[:, c, :], d), 64), ALU.mult,
                           t_o[d], t_ty[d])
                    banks.put(b_o[d], t)
                    t_ty[d] = tt(G, Y[:, c, :], Y[:, c, :], tq[d][:, :], ALU.add, t, t_y, *t_ty)
                gap()
            e_free[1] = t_up[1]
            late = None

            def add_y(h, bank, t):
                t_y = tt(V, Y[:, :, h * 64:(h + 1) * 64], Y[:, :, h * 64:(h + 1) * 64],
                         bank[:, 0:256].rearrange("p (t n) -> p t n", t=4), ALU.add, t, *t_ty)
                banks.put(bank, t_y)
                return t_y

            for h in range(8):
                this = next_e
                ts_ = []
                for d in range(2):
                    E_ = E4[h % 2][d]
                    ts_.append(tt(V, E_[:, :], E_[:, :], CBT[:, :], ALU.mult, this[d][0], t_cb))
                if h < 7:
                    next_e = decayed(h + 1)
                if late:
                    add_y(*late)
                gap()
                bank = banks.get(T)
                T.wait(*ts_, this[0][1], this[1][1])
                for c in range(4):
                    for d in range(2):
                        ins = mm(bank[:, c * 64:(c + 1) * 64], E4[h % 2][d][:, c * 128:(c + 1) * 128],
                                 XD[h % 2][:, d, c, :], start=(d == 0), stop=(d == 1))
                t = e_free[h % 2] = T.inc(ins)
                late = (h, bank, t)
            t_y = add_y(*late)
            pe_end, v_end, g_end = T.now(), V.now(), G.now()
            gating = gate(g, t_y)
        for _g in gating:
            pass
        for _f in filler:
            pass

        ends = (T.now(), V.now(), A.now(), G.now(), d_yz[0].now(), d_yz[1].now(), d_z[0].now(), d_z[1].now(),
                d_fb[0].now(), d_fb[1].now())
        t_mod = spilled["mod"]
        for E_ in (A, V, G, T):
            E_.wait(*ends)
        d_ld = [Dma(sem(f"d_ld{i}")) for i in range(4)]
        G.wait(*ends)
        tx = Dma(sem("d_x2")).inc(nc.gpsimd.dma_start(XT[:, :, :], I["xT"]))
        phase(W1)
        ACC = here("ACC", [128, 8, 512])
        at_ = cur[0]
        YH = here("YH", [128, 8, 512], FR)
        YL_ = here("YL_", [128, 8, 512], FR)
        n_ld = [0]
        ld_free = [None] * 4

        def fetch(src, w=512):
            i = n_ld[0] % 4
            n_ld[0] += 1
            G.wait(ld_free[i])
            v = TMP[i][:, 0:w]
            return i, d_ld[i].inc(nc.gpsimd.dma_start(v if len(src.shape) == 2 else
                                                      v.rearrange("p (a b) -> p a b", a=src.shape[1]), src))

        bank, t = rows_sum(SQ[:, :], "o2048", t_sq)
        t_ra, t = rsqrt(RA[:, :], bank[:, :], "eps5", t)
        banks.put(bank, t)
        t_a = [None] * 8
        half_done = None
        for n in range(2):
            for k in range(8):
                i, t = fetch(YZD[8 * n + k])
                t_y = split(YH[:, k, :], YL_[:, k, :], TMP[i][:, :], t, half_done)
                ld_free[i] = t_y
            for c in range(8):
                e = ring.get("wa", c, 1024 * n)
                bank = banks.get(T)
                t = feature(bank[:, :], e, YH, YL_, t_y)
                ring.done(e, t)
                half_done = t
                if n == 0:
                    t_a[c] = cp(A, ACC[:, c, :], bank[:, :], t)
                else:
                    t = tt(V, ACC[:, c, :], bank[:, :], ACC[:, c, :], ALU.add, t, t_a[c])
                    t_a[c] = tt(G, ACC[:, c, :], ACC[:, c, :], RA[:, :], ALU.mult, t, t_ra)
                banks.put(bank, t_a[c] if n == 0 else t)

        phase(at_)
        YPh = here("YPh", [128, 8, 512], FR)
        YPl = here("YPl", [128, 8, 512], FR)
        Uh = here("Uh", [128, 4, 256], FR)
        Ul = here("Ul", [128, 4, 256], FR)
        Dh = here("Dh", [128, 2, 512], FR)
        Dl = here("Dl", [128, 2, 512], FR)
        V.wait(half_done)
        A.wait(half_done)
        t_d = t_p = None
        for g in range(4):
            for m in range(2):
                i, t = fetch(UD[g, :, 2 * m:2 * m + 2, :])
                t_u = split(Uh[:, 2 * m:2 * m + 2, :], Ul[:, 2 * m:2 * m + 2, :],
                            TMP[i][:, :].rearrange("p (a b) -> p a b", a=2), t, t_d)
                ld_free[i] = t_u
            es = [ring.get("pm", g, a) for a in range(2)]
            for j in range(2):
                bank = banks.get(T)
                cs = slice(j * 128, (j + 1) * 128)
                t = prod(bank[:, :], [(Uh[:, i, cs], Ul[:, i, cs], es[i // 2][0][:, i % 2, :],
                                       es[i // 2][1][:, i % 2, :]) for i in range(4)], es[0][2], es[1][2], t_u)
                t_dd = split(Dh[:, j, :], Dl[:, j, :], bank[:, :], t, t_p)
                banks.put(bank, t_dd)
            t_d = t
            for e in es:
                ring.done(e, t)
            if g % 2 == 0:
                ew = ring.get("pw", 2 * g)
            for m in range(2):
                bank = banks.get(T)
                ms_ = slice(m * 128, (m + 1) * 128)
                kk = 2 * (g % 2)
                t = prod(bank[:, :], [(ew[0][:, kk + k, ms_], ew[1][:, kk + k, ms_], Dh[:, k, :], Dl[:, k, :])
                                      for k in range(2)], ew[2], t_dd)
                t1 = av(TMP[4 + m][:, :], bank[:, :], ACT.Copy, t, *([t_yp] if g else []), scale=C("pool_scale", 2 * g + m))
                banks.put(bank, t1)
                t_yp = split(YPh[:, 2 * g + m, :], YPl[:, 2 * g + m, :], TMP[4 + m][:, :], t1)
            t_p = t
            if g % 2:
                ring.done(ew, t)
        for c in range(8):
            ia, t1 = fetch(GD[c])
            ip, t2 = fetch(GD[8 + c])
            t1 = av(TMP[ia][:, :], TMP[ia][:, :], ACT.Sigmoid, t1, bias=C("b_gate", c))
            t2 = av(TMP[ip][:, :], TMP[ip][:, :], ACT.Sigmoid, t2, bias=C("b_gate", 8 + c))
            t3 = tt(G, ACC[:, c, :], ACC[:, c, :], TMP[ia][:, :], ALU.mult, t1, t_a[c])
            ld_free[ia] = t3
            e = ring.get("wb", c)
            bank = banks.get(T)
            t = feature(bank[:, :], e, YPh, YPl, t_yp)
            ring.done(e, t)
            t = tt(V, TMP[ip][:, :], TMP[ip][:, :], bank[:, :], ALU.mult, t, t2)
            banks.put(bank, t)
            t_mg = tt(V, ACC[:, c, :], ACC[:, c, :], TMP[ip][:, :], ALU.add, t, t3)
            ld_free[ip] = t_mg
        phase(at_)
        MGh = here("MGh", [128, 8, 512], FR)
        MGl = here("MGl", [128, 8, 512], FR)
        V.wait(T.now())
        A.wait(T.now())
        t_mgs = [split(MGh[:, c, :], MGl[:, c, :], ACC[:, c, :], t_mg) for c in range(8)]

        class Squares:

            def __init__(self):
                self.bank = banks.get(T)
                self.free = [None, None]
                self.pend = None
                self.v = V.now()

            def flush(self):
                if self.pend is not None:
                    i, t = self.pend
                    T.wait(t)
                    self.t = self.free[i % 2] = T.inc(mm(self.bank[:, :], K("o1024"), TMP[2 + i % 2][:, :],
                                                         start=(i == 0), stop=(i == 3)))
                    self.pend = None

            def add(self, k, t):
                x, i = XT[:, k, :], k // 2
                if k % 2 == 0:
                    self.a = av(TMP[2 + i % 2][:, :], x, ACT.Square, t, self.free[i % 2])
                else:
                    t = tt(V, SQ[:, :], x, x, ALU.mult, t, self.v)
                    t = self.v = tt(V, TMP[2 + i % 2][:, :], TMP[2 + i % 2][:, :], SQ[:, :], ALU.add, t, self.a)
                    self.flush()
                    self.pend = (i, t)

            def rsqrt(self, eps):
                self.flush()
                t, t0 = rsqrt(RA[:, :], self.bank[:, :], eps, self.t)
                banks.put(self.bank, t0)
                return t

        def layer_norm(gname, bname, sums):
            bank, t = sums
            sq = Squares()
            for k in range(8):
                t_c = tt(V, XT[:, k, :], XT[:, k, :], bank[:, :], ALU.subtract, t)
                sq.add(k, t_c)
            banks.put(bank, t_c)
            t = sq.rsqrt("eps5")
            out = []
            for k in range(8):
                t2 = tt(V, XT[:, k, :], XT[:, k, :], RA[:, :], ALU.mult, t)
                out.append(av(XT[:, k, :], XT[:, k, :], ACT.Identity, t2, scale=C(gname, k), bias=C(bname, k)))
            return out

        class Mean:

            def add(self, k, t):
                if k == 0:
                    self.first = t
                else:
                    self.t = tt(V, SQ[:, :], XT[:, 0, :] if k == 1 else SQ[:, :], XT[:, k, :], ALU.add,
                                t, self.first if k == 1 else self.t)

            def sums(self):
                return rows_sum(SQ[:, :], "o1024", self.t)

        V.wait(G.now(), T.now())
        mean = Mean()
        t_al = [ts(V, XT[:, c, :], XT[:, c, :], ALPHA, None, ALU.mult, None, tx) for c in range(8)]
        for c in range(8):
            e = ring.get("wo", c)
            bank = banks.get(T)
            t = feature(bank[:, :], e, MGh, MGl, xt=t_mgs)
            ring.done(e, t)
            t_r = stt(XT[:, c, :], bank[:, :], mod[:, 16 + c, 0:1], XT[:, c, :], ALU.mult, ALU.add, t, t_al[c], t_mod)
            banks.put(bank, t_r)
            mean.add(c, t_r)
        t_xs = layer_norm("ln1_g", "ln1_b", mean.sums())

        phase(W1)
        HF = here("HF", [128, 8, 512])
        HR = here("HR", [128, 4, 1024])
        rt = here("rt", [128, 3072])
        V.wait(T.now(), G.now())
        t_h2s = []
        for k in range(8):
            t = ts(V, HF[:, k, :], XT[:, k, :], mod[:, 32 + k, 0:1], mod[:, 24 + k, 0:1], ALU.mult, ALU.add, t_xs[k])
            t_h2 = split(HTh[:, k, :], HTl[:, k, :], HF[:, k, :], t)
            t_h2s.append(t_h2)
        for i in range(4):
            for q in range(2):
                _t, t = turn(A, HR[:, i, q * 512:(q + 1) * 512].rearrange("p (t n) -> p t n", t=4),
                             [HF[:, 4 * q + k, i * 128:(i + 1) * 128] for k in range(4)], t_h2)
        A.wait(t)
        t_hd = d_h.inc(nc.scalar.dma_start(H2.rearrange("(t p) n -> p t n", p=128), HR[:, :, :]))
        e = ring.get("wr", 0)
        bank = banks.get(T)
        for i in range(4):
            cs = slice(i * 128, (i + 1) * 128)
            t = prod(bank[:, i * 36:(i + 1) * 36], [(HTh[:, k, cs], HTl[:, k, cs], e[0][:, k, :], e[1][:, k, :])
                                                    for k in range(8)], e[2], xt=t_h2s)
        ring.done(e, t)
        ro = [0]

        def rc(w, t_=4):
            r = rt[:, ro[0]:ro[0] + w * t_]
            ro[0] += w * t_
            return r.rearrange("p (t n) -> p t n", t=t_)

        lg, g8, gm, m32, lm, vm, oh0, oh1, ohs, sc4 = (rc(n) for n in (36, 8, 8, 32, 32, 8, 32, 32, 32, 24))
        t = tt(V, lg, bank[:, 0:144].rearrange("p (t n) -> p t n", t=4),
               pr[:, PR_RB:PR_RB + 36].unsqueeze(1).to_broadcast([128, 4, 36]), ALU.add, t, A.now(), G.now())
        banks.put(bank, t)
        V.inc(nc.vector.memset(g8, -1e30))
        V.wait(V.now())
        t = cp(V, g8[:, :, 0:4], lg[:, :, 0:4], t)
        for i in range(4):
            V.wait(t)
            t = V.inc(nc.vector.max(gm[:, i, :], g8[:, i, :]))
            V.wait(t)
            t = V.inc(nc.vector.max_index(gi[:, i, :], gm[:, i, :], g8[:, i, :]))
            t = cp(V, sc4[:, i, 0:1], gi[:, i, 0:1], t)
            t = ts(V, m32[:, i, :], K("iotag", 32), sc4[:, i, 0:1], None, ALU.is_equal, None, t)
            t1 = tt(V, lm[:, i, :], lg[:, i, 4:36], m32[:, i, :], ALU.mult, t)
            t2 = ts(V, m32[:, i, :], m32[:, i, :], 1e30, -1e30, ALU.mult, ALU.add, t1)
            t = tt(V, lm[:, i, :], lm[:, i, :], m32[:, i, :], ALU.add, t2)
            V.wait(t)
            t = V.inc(nc.vector.max(vm[:, i, :], lm[:, i, :]))
            V.wait(t)
            t = V.inc(nc.vector.max_index(vi[:, i, :], vm[:, i, :], lm[:, i, :]))
            t = cp(V, sc4[:, i, 2:4], vi[:, i, 0:2], t)
            t1 = ts(V, oh0[:, i, :], K("iota", 32), sc4[:, i, 2:3], None, ALU.is_equal, None, t)
            t2 = ts(V, oh1[:, i, :], K("iota", 32), sc4[:, i, 3:4], None, ALU.is_equal, None, t)
            t = tt(V, ohs[:, i, :], oh0[:, i, :], oh1[:, i, :], ALU.add, t2)
            t3 = ts(V, sc4[:, i, 4:5], gm[:, i, 0:1], -1.0, None, ALU.mult, None)
            t4 = tt(V, sc4[:, i, 5:6], vm[:, i, 1:2], vm[:, i, 0:1], ALU.subtract, t)
            A.wait(t4)
            A.inc(act(g8[:, i, 4:8], lg[:, i, 0:4], ACT.Exp, bias=sc4[:, i, 4:5], accum_out=sc4[:, i, 6:7]))
            t5 = av(sc4[:, i, 7:8], sc4[:, i, 5:6], ACT.Exp)
            t = ts(V, sc4[:, i, 8:9], sc4[:, i, 7:8], 1.0, None, ALU.add, None, t5)
            t = tt(V, sc4[:, i, 8:9], sc4[:, i, 8:9], sc4[:, i, 6:7], ALU.mult, t)
            V.wait(t)
            t = V.inc(nc.vector.reciprocal(wk[:, i, 0:1], sc4[:, i, 8:9]))
            t = tt(V, wk[:, i, 1:2], wk[:, i, 0:1], sc4[:, i, 7:8], ALU.mult, t)
        bank = banks.get(T)
        T.wait(t)
        for i in range(4):
            for j in range(i + 1):
                mm(bank[:, i * 32:(i + 1) * 32], K("sU") if j == i else K("ones"), ohs[:, j, :],
                   start=(j == 0), stop=(j == i))
        for j in range(4):
            ins = mm(bank[:, 128:160], K("ones"), ohs[:, j, :], start=(j == 0), stop=(j == 3))
        t = T.inc(ins)
        cnt = rc(32, 1)[:, 0, :]
        ove = rc(32, 1)[:, 0, :]
        send = rc(32, 1)[:, 0, :]
        sst = rc(32, 1)[:, 0, :]
        t32 = rc(32, 1)[:, 0, :]
        eid = rc(NOV + 1, 1)[:, 0, :]
        rk = rc(32)
        t0 = cp(V, cnt, bank[:, 128:160], t)
        t1 = cp(V, rk, bank[:, 0:128].rearrange("p (t n) -> p t n", t=4), t)
        banks.put(bank, t1)
        t = ts(V, ove, cnt, float(CAP), None, ALU.is_gt, None, t1)
        for b in range(2, OVB + 1):
            t = stt(ove, cnt, float(CAP * b), ove, ALU.is_gt, ALU.add, t)
        V.wait(t)
        V.inc(nc.vector.memset(t32, 0.0))
        V.wait(V.now())
        t = V.inc(nc.vector.tensor_tensor_scan(send, ove, t32, 0.0, ALU.add, ALU.add))
        t = tt(V, sst, send, ove, ALU.subtract, t)
        for j in range(NOV):
            V.wait(V.now())
            V.inc(nc.vector.tensor_scalar(t32, send, float(j), 0.0, ALU.is_le, ALU.add, accum_out=eid[:, j:j + 1]))
        V.wait(V.now())
        t = ts(V, eid[:, 0:NOV], eid[:, 0:NOV], 31.0, None, ALU.min, None)
        cp(V, eid[:, NOV:NOV + 1], send[:, 31:32], t)
        t_eid = cp(V, eidi[:, :], eid, V.now())
        SB_ = rt[:, 1700:1700 + 128 + 2 * NBLK]
        bank = banks.get(T)
        tpe = None
        for i in range(4):
            for k in range(2):
                oh = (oh0, oh1)[k]
                x = sc4[:, i, 9:10]
                y = sc4[:, i, 10:11]
                q = sc4[:, i, 11:12]
                bl = sc4[:, i, 12:13]
                r1 = sc4[:, i, 13:14]
                V.wait(V.now())
                V.inc(nc.vector.tensor_tensor_reduce(out=t32, in0=rk[:, i, :], in1=oh[:, i, :], scale=1.0, scalar=0.0,
                                                     op0=ALU.mult, op1=ALU.add, accum_out=x))
                V.wait(V.now())
                V.inc(nc.vector.tensor_tensor_reduce(out=t32, in0=sst, in1=oh[:, i, :], scale=1.0, scalar=0.0,
                                                     op0=ALU.mult, op1=ALU.add, accum_out=y))
                ts(V, q, x, float(CAP), None, ALU.is_ge, None, V.now())
                for b in range(2, OVB + 1):
                    stt(q, x, float(CAP * b), q, ALU.is_ge, ALU.add, V.now())
                stt(r1, q, -float(CAP), x, ALU.mult, ALU.add, V.now())
                e = sc4[:, i, 2 + k:3 + k]
                stt(y, y, 31.0, q, ALU.add, ALU.add, V.now())
                tt(V, y, y, e, ALU.subtract, V.now())
                ts(V, x, q, 0.0, None, ALU.is_gt, None, V.now())
                tt(V, y, y, x, ALU.mult, V.now())
                tt(V, bl, y, e, ALU.add, V.now())
                V.wait(tpe)
                ts(V, SB_[:, 0:128], K("iota"), r1, None, ALU.is_equal, None, V.now())
                ts(V, SB_[:, 128:128 + NBLK], K("iota", NBLK), bl, km[:, KM["tok"] + 2 * i + k:KM["tok"] + 2 * i + k + 1],
                   ALU.is_equal, ALU.mult, V.now())
                t = ts(V, SB_[:, 128 + NBLK:128 + 2 * NBLK], K("iota", NBLK), bl,
                       km[:, KM["aid"] + 2 * i + k:KM["aid"] + 2 * i + k + 1], ALU.is_equal, ALU.mult, V.now())
                T.wait(t)
                n = 2 * i + k
                tpe = T.inc(mm(bank[:, 0:2 * NBLK], SB_[:, 0:128], SB_[:, 128:128 + 2 * NBLK], start=(n == 0),
                               stop=(n == 7)))
        fl = rt[:, 2100:2100 + 2 * NBLK]
        ts(V, fl[:, 0:NBLK], bank[:, 0:NBLK], -1.0, 0.0, ALU.add, ALU.max, tpe)
        t = ts(V, rt[:, 2400:2400 + NBLK], bank[:, NBLK:2 * NBLK], 0.0, km[:, KM["slot"]:KM["slot"] + 1],
               ALU.is_equal, ALU.mult)
        t = stt(fl[:, NBLK:2 * NBLK], bank[:, NBLK:2 * NBLK], -1.0, rt[:, 2400:2400 + NBLK], ALU.add, ALU.add, t)
        banks.put(bank, t)
        t_ix = cp(V, ix[:, :, :], fl.rearrange("p (a n) -> p a n", a=2), t)
        t_free = (T.now(), A.now())
        V.wait(t_ix)

        phase(W1)
        XG = [here(f"XG{i}", [128, 1024]) for i in range(2)]
        XGh = [here(f"XGh{i}", [128, 8, 128], FR) for i in range(2)]
        XGl = [here(f"XGl{i}", [128, 8, 128], FR) for i in range(2)]
        YO = [here(f"YO{i}", [128, 1024]) for i in range(2)]
        GT = [here(f"GT{i}", [128, 512]) for i in range(2)]
        GTh = [here(f"GTh{i}", [128, 4, 128], FR) for i in range(2)]
        GTl = [here(f"GTl{i}", [128, 4, 128], FR) for i in range(2)]
        d_gg = [Dma(sem(f"d_gg{i}")) for i in range(2)]

        def experts(T, V, A, G, ring, banks, d_gg, d_s, blocks, before):
            free, got, xt, act_ = {}, {}, {}, {}

            def w(name, i):
                return free.get((name, i))

            def gather(b):
                i = b % 2
                G.wait(w("xg", i), *before)
                got[b] = d_gg[i].inc(nc.gpsimd.indirect_dma_start(
                    XG[i][:, :], None, H2, bass.IndirectOffsetOnAxis(ap=ix[:, 0, b:b + 1], axis=0)))

            def turn_in(b):
                i = b % 2
                for q in range(2):
                    bank = banks.get(T)
                    T.wait(got[b])
                    for k in range(4):
                        ins = nc.tensor.transpose(bank[:, k * 128:(k + 1) * 128],
                                                  XG[i][:, (4 * q + k) * 128:(4 * q + k + 1) * 128], K("ident"))
                    t = T.inc(ins)
                    v = bank[:, :].rearrange("p (k n) -> p k n", k=4)
                    h_, l_ = XGh[i][:, 4 * q:4 * q + 4, :], XGl[i][:, 4 * q:4 * q + 4, :]
                    A.wait(t, w("xgt", i))
                    t1 = A.inc(act(h_, v, ACT.Copy))
                    V.wait(t1)
                    t2 = V.inc(nc.vector.tensor_tensor(l_, v, h_.bitcast(F32), ALU.subtract))
                    banks.put(bank, t2)
                free[("xg", i)] = t
                xt[b] = t2

            def first(b, e):
                i = b % 2
                bk = []
                T.wait(xt[b])
                for name in ("eg", "eu"):
                    bank = banks.get(T)
                    for a in range(4):
                        en = ring.get(name, e, a, kind="pool" if a == 3 and POOL_SPLITS else "split")
                        T.wait(en[2])
                        for kk in range(2):
                            k = 2 * a + kk
                            mm(bank[:, :], XGh[i][:, k, :], en[0][:, kk, :], start=(k == 0), stop=False)
                            mm(bank[:, :], XGl[i][:, k, :], en[0][:, kk, :], start=False, stop=False)
                            ins = mm(bank[:, :], XGh[i][:, k, :], en[1][:, kk, :], start=False, stop=(k == 7))
                        t = T.inc(ins)
                        ring.done(en, t)
                    bk.append((bank, t))
                free[("xgt", i)] = t
                A.wait(bk[0][1], w("gt", i))
                t = A.inc(act(GT[i][:, :], bk[0][0][:, :], ACT.Silu))
                banks.put(bk[0][0], t)
                V.wait(t, bk[1][1])
                act_[b] = V.inc(nc.vector.tensor_tensor(GT[i][:, :], GT[i][:, :], bk[1][0][:, :], ALU.mult))
                banks.put(bk[1][0], act_[b])

            def turn_mid(b):
                i = b % 2
                bank = banks.get(T)
                T.wait(act_[b])
                for k in range(4):
                    ins = nc.tensor.transpose(bank[:, k * 128:(k + 1) * 128], GT[i][:, k * 128:(k + 1) * 128],
                                              K("ident"))
                t = T.inc(ins)
                free[("gt", i)] = t
                v = bank[:, :].rearrange("p (k n) -> p k n", k=4)
                A.wait(t, w("gtt", i))
                t = A.inc(act(GTh[i][:, :, :], v, ACT.Copy))
                V.wait(t)
                t = V.inc(nc.vector.tensor_tensor(GTl[i][:, :, :], v, GTh[i][:, :, :].bitcast(F32), ALU.subtract))
                banks.put(bank, t)
                act_[b] = t

            def last(b, e):
                i = b % 2
                T.wait(act_[b])
                bs = [banks.get(T), banks.get(T)]
                for k in range(4):
                    en = ring.get("ed", e, k, kind="pool" if k == 3 and POOL_SPLITS else "split")
                    T.wait(en[2])
                    for n in range(2):
                        ns = slice(n * 512, (n + 1) * 512)
                        mm(bs[n][:, :], GTh[i][:, k, :], en[0][:, 0, ns], start=(k == 0), stop=False)
                        mm(bs[n][:, :], GTl[i][:, k, :], en[0][:, 0, ns], start=False, stop=False)
                        ins = mm(bs[n][:, :], GTh[i][:, k, :], en[1][:, 0, ns], start=False, stop=(k == 3))
                    t = T.inc(ins)
                    ring.done(en, t)
                free[("gtt", i)] = t
                for n in range(2):
                    A.wait(t, w("yo", i))
                    t3 = A.inc(act(YO[i][:, n * 512:(n + 1) * 512], bs[n][:, :], ACT.Copy))
                    banks.put(bs[n], t3)
                G.wait(t3, d_s.now())
                free[("yo", i)] = d_s.inc(nc.gpsimd.indirect_dma_start(
                    YD, bass.IndirectOffsetOnAxis(ap=ix[:, 1, b:b + 1], axis=0), YO[i][:, :], None,
                    bounds_check=1023, oob_is_err=False))

            n = len(blocks)
            gather(blocks[0][0])
            if n > 1:
                gather(blocks[1][0])
            turn_in(blocks[0][0])
            for j, (b, e) in enumerate(blocks):
                first(b, e)
                if j + 1 < n:
                    turn_in(blocks[j + 1][0])
                if j + 2 < n:
                    gather(blocks[j + 2][0])
                if j:
                    last(*blocks[j - 1])
                turn_mid(b)
            last(*blocks[-1])

        A.wait(V.now(), G.now())
        V.wait(A.now(), G.now())
        for k in range(8):
            ts(V, XT[:, k, :], XT[:, k, :], ALPHA, None, ALU.mult, None, t_h2s[7])
        ring.stop = "f11"
        experts(T, V, A, G, ring, banks, d_gg, d_s, [(e, e) for e in range(32)], (t_ix, t_hd, *t_free, V.now()))

        everything = (T.now(), V.now(), A.now(), G.now(), d_s.now(), t_eid)
        for E_ in (T, V, A, G, S):
            E_.wait(*everything)
        nov = nc.values_load(eidi[0:1, NOV:NOV + 1], min_val=0, max_val=NOV)
        with nc.If(nov > 0):
            T2, V2, A2, G2, S2 = (Eng(e_.e, sem(f"o_{n}")) for n, e_ in enumerate((T, V, A, G, S)))
            loaded = {}

            def theirs(key):
                j = key[1]
                if j not in loaded:
                    loaded[j] = nc.sync.value_load(eidi[0:1, j:j + 1], min_val=0, max_val=31)
                v = I[key[0]].rearrange("e (k p) n -> e p k n", p=128)[bass.ds(loaded[j], 1)]
                v = v.rearrange("e p k n -> p (e k) n")
                if key[0] == "ed":
                    return v[:, key[2]:key[2] + 1, :]
                return v[:, 2 * key[2]:2 * key[2] + 2, :]

            ring2 = Ring([] if dry else plans[1], theirs, raw, HLB, S2, A2, V2, G2,
                         [Dma(sem(f"o_r{i}")) for i in range(NRAW)], dry)
            banks2 = Banks([b for b, _t in banks.free])
            ds2 = Dma(sem("o_s"))
            experts(T2, V2, A2, G2, ring2, banks2, [Dma(sem(f"o_g{i}")) for i in range(2)], ds2,
                    [(32 + j, j) for j in range(NOV)], ())
            for E_ in (T2, V2, A2, G2, S2):
                E_.wait(T2.now(), V2.now(), A2.now(), G2.now(), ds2.now())
        nc.end_ifs()
        ring.stop = None
        ring.advance()

        YV = YD.rearrange("(t p k) n -> t p k n", p=128, k=2)
        phase(W1)
        YI = here("YI", [128, 2, 2, 1024])
        YL = here("YL", [128, 4, 1024])
        V.wait(A.now(), G.now(), T.now())
        G.wait(d_s.now())
        d_yy = [Dma(sem(f"d_yy{i}")) for i in range(2)]
        tw_ = [None, None]
        G.wait(T.now(), V.now(), A.now())
        for i in range(4):
            G.wait(tw_[i % 2])
            t_ld = d_yy[i % 2].inc(nc.gpsimd.dma_start(YI[:, i % 2, :, :], YV[i]))
            t1 = ts(V, YL[:, i, :], YI[:, i % 2, 0, :], wk[:, i, 0:1], None, ALU.mult, None, t_ld, t_hd)
            t_yl = stt(YL[:, i, :], YI[:, i % 2, 1, :], wk[:, i, 1:2], YL[:, i, :], ALU.mult, ALU.add, t1)
            tw_[i % 2] = t_yl
        for k in range(8):
            bank = banks.get(T)
            T.wait(t_yl)
            for i in range(4):
                ins = nc.tensor.transpose(bank[:, i * 128:(i + 1) * 128], YL[:, i, k * 128:(k + 1) * 128], K("ident"))
            t = T.inc(ins)
            t_r = stt(XT[:, k, :], bank[:, :], mod[:, 40 + k, 0:1], XT[:, k, :], ALU.mult, ALU.add, t)
            banks.put(bank, t_r)
            mean.add(k, t_r)
        t_xs = layer_norm("ln2_g", "ln2_b", mean.sums())

        def rms_norm(name, sq):
            t = sq.rsqrt("eps6")
            V.wait(T.now())
            A.wait(T.now())
            tf, out = [None, None], []
            for k in range(8):
                t2 = stt(TMP[4 + k % 2][:, :], XT[:, k, :], C(name, k), RA[:, :], ALU.mult, ALU.mult, t, tf[k % 2])
                tf[k % 2] = split(HTh[:, k, :], HTl[:, k, :], TMP[4 + k % 2][:, :], t2)
                out.append(tf[k % 2])
            return out

        def ffn(name, w1, w3, w2, sq, last=None):
            t_n = rms_norm(name, sq)
            phase(W1)
            FAh = here(name + "FAh", [128, 11, 512], FR)
            FAl = here(name + "FAl", [128, 11, 512], FR)
            tfree = [None, None]
            V.wait(A.now(), T.now(), G.now())
            A.wait(T.now(), G.now())
            for half in range(2):
                t_d = T.now() if half else None
                t_f = []
                for f in range(11):
                    bk = []
                    for w in (w1, w3):
                        e = ring.get(w, 11 * half + f)
                        bank = banks.get(T)
                        t = feature(bank[:, :], e, HTh, HTl, xt=t_n)
                        ring.done(e, t)
                        bk.append((bank, t))
                    i = f % 2
                    t = av(TMP[i][:, :], bk[0][0][:, :], ACT.Silu, bk[0][1], tfree[i])
                    banks.put(bk[0][0], t)
                    t = tt(V, TMP[i][:, :], TMP[i][:, :], bk[1][0][:, :], ALU.mult, t, bk[1][1])
                    banks.put(bk[1][0], t)
                    tfree[i] = split(FAh[:, f, :], FAl[:, f, :], TMP[i][:, :], t, t_d)
                    t_f.append(tfree[i])
                if half and last is None:
                    sq = Squares()
                for c in range(8):
                    bank = banks.get(T)
                    e = ring.get(w2, c, 1408 * half)
                    t = feature(bank[:, :], e, FAh, FAl, xt=t_f, n=8, stop=False)
                    ring.done(e, t)
                    e = ring.get(w2, c, 1408 * half + 1024)
                    t = feature(bank[:, :], e, FAh, FAl, xt=t_f[8:], k0=8, n=3, start=False)
                    ring.done(e, t)
                    t_o = stt(XT[:, c, :], bank[:, :], 0.5, XT[:, c, :], ALU.mult, ALU.add, t)
                    banks.put(bank, t_o)
                    if half and last is None:
                        sq.add(c, t_o)
                    elif half:
                        last(c, t_o)
            return sq

        sq = Squares()
        for k in range(8):
            sq.add(k, t_xs[k])
        sq = ffn("n1", "f11", "f13", "f12", sq)
        t_n = rms_norm("nm", sq)
        fr = (T.now(), V.now(), G.now(), A.now())
        V.wait(T.now())
        A.wait(T.now())
        G.wait(*fr)
        phase(W1)
        HV = here("HV", [128, 4, 512])
        MX = here("MX", [128, 8, 512])
        RST = here("RST", [128, 512])
        at_ = cur[0]
        QT = here("QT", [128, 4, 512])
        KT = here("KT", [128, 4, 512])
        VV = here("VV", [128, 4, 512])
        AL = here("AL", [128, 1280])
        CS = here("CS", [128, 2, 512])
        PT = [here(f"PT{i}", [128, 4, 128]) for i in range(2)]
        ms_ = [here(f"ms{i}", [128, 8]) for i in range(3)]
        PB = [TMP[0], TMP[1], here("PB2", [128, 512])]
        al_at = [0, 128, 384, 768]
        t_tab = d_t.inc(nc.gpsimd.dma_start(CS[:, :, :], I["cs"]))
        t_tab = d_t.inc(nc.gpsimd.dma_start(AL[:, :], I["al"]))
        t_tab = d_t.inc(nc.gpsimd.dma_start(RST[:, :], I["rst"]))

        def qk():
            f_n = [None] * 2
            st = {}
            for n in range(10):
                if n < 8:
                    e = ring.get("w2in", n)
                    bank = banks.get(T)
                    t = feature(bank[:, :], e, HTh, HTl, xt=t_n)
                    ring.done(e, t)
                    t_s = av(TMP[n % 2][:, :], bank[:, :], ACT.Square, t, st[n - 2][2] if n > 1 else None)
                    st[n] = [bank, t_s, None, None]
                if 0 <= n - 1 < 8:
                    m = n - 1
                    b2, t = rows_sum(TMP[m % 2][:, :], "hb", st[m][1])
                    st[m][2] = t
                    t, t0 = rsqrt(RA[:, :], b2[:, :], "eps6", t, V.now())
                    banks.put(b2, t0)
                    t = stt(TMP[2 + m % 2][:, :], st[m][0][:, :], C("qn" if m < 4 else "kn", 0), RA[:, :], ALU.mult,
                            ALU.mult, t, f_n[m % 2])
                    banks.put(st[m][0], t)
                    st[m][3] = t
                if 0 <= n - 2 < 8:
                    m = n - 2
                    b3_, t = rows_sum(TMP[2 + m % 2][:, :], "psw", st[m][3])
                    nm_ = TMP[2 + m % 2][:, :]
                    t1 = tt(G, TMP[4][:, :], nm_, CS[:, 0, :], ALU.mult, st[m][3], t_tab, G.now())
                    t2 = tt(V, nm_, b3_[:, :], CS[:, 1, :], ALU.mult, t, t1, t_tab)
                    banks.put(b3_, t2)
                    f_n[m % 2] = tt(G, (QT if m < 4 else KT)[:, m % 4, :], TMP[4][:, :], nm_, ALU.add, t1, t2)
                yield f_n[1]

        def vi():
            for nm, dst in (("w2v", VV), ("w2i", HV)):
                for c in range(2):
                    es = [ring.get(nm, c, a) for a in range(2)]
                    for i in range(4):
                        cs = slice(i * 128, (i + 1) * 128)
                        bank = banks.get(T)
                        t = prod(bank[:, 0:256], [(HTh[:, k, cs], HTl[:, k, cs], es[k // 4][0][:, k % 4, :],
                                                   es[k // 4][1][:, k % 4, :]) for k in range(8)], es[0][2], es[1][2])
                        if i == 3:
                            for e in es:
                                ring.done(e, t)
                        t_v = cp(A, dst[:, i, c * 256:(c + 1) * 256], bank[:, 0:256], t)
                        banks.put(bank, t_v)
                        if i % 2:
                            yield t_v

        turns = [qk(), vi()]
        t_qk = t_v = None
        for i in range(10):
            t_qk = next(turns[0])
            if i in (2, 5):
                t_v = next(turns[1])
                t_v = next(turns[1])
        t_v = [t_v] + list(turns[1])
        t_v = t_v[-1]

        lw = sm[:, 16:40]
        t = tt(V, lw[:, 0:4], C("lb0", 0, 4), C("lb1", 0, 4), ALU.max)
        tt(V, lw[:, 4:8], C("lb0", 0, 4), lw[:, 0:4], ALU.subtract, t)
        t = tt(V, lw[:, 8:12], C("lb1", 0, 4), lw[:, 0:4], ALU.subtract, t)
        t = av(lw[:, 4:12], lw[:, 4:12], ACT.Exp, t)
        t = tt(V, lw[:, 0:4], lw[:, 4:8], lw[:, 8:12], ALU.add, t)
        t = recip(lw[:, 0:4], lw[:, 0:4], t)
        t = tt(V, lw[:, 12:16], lw[:, 4:8], lw[:, 0:4], ALU.mult, t)
        t_lb = ts(V, lw[:, 16:20], lw[:, 12:16], -1.0, 1.0, ALU.mult, ALU.add, t)
        phase(DEC)
        GG, EX, ATT, HGB = (here("hg" + n_, [128, 512])[:, :] for n_ in "abcd")
        assert cur[0] <= DEC_END
        QD, KD, KW, FF = TMP[2][:, :], TMP[3][:, :], TMP[4][:, :], TMP[5][:, :]
        KWT = RA[:, :].rearrange("p (t n) -> p t n", t=4)
        REC = SQ[:, :]
        SS = [CS[:, i // 4, (i % 4) * 128:(i % 4 + 1) * 128] for i in range(8)]
        V.wait(t_qk, t_v)
        A.wait(V.now(), t_qk)
        V.inc(nc.vector.memset(ATT, 0.0))
        t_at0 = V.inc(nc.vector.memset(SS[0], 0.0))
        V.wait(t_at0)
        hgm = K("hgm").bitcast(U32)
        t_mx2 = None

        def recurrence():
            nonlocal t_mx2
            t_o = t_s = t_mm = None
            for h in range(4):
                bks = []
                e = ring.get("w2in", 12 + h)
                bf = banks.get(T)
                t_bf = feature(bf[:, :], e, HTh, HTl)
                ring.done(e, t_bf)
                t = av(FF, bf[:, :], ACT.Sigmoid, t_bf, V.now())
                banks.put(bf, t)
                t_f = ts(V, FF, FF, lw[:, 16 + h:17 + h], lw[:, 12 + h:13 + h], ALU.mult, ALU.add, t, t_lb)
                yield
                t = av(GG, FF, ACT.Ln, t_f)
                t_k = ts(V, FF, FF, -1.0, 1.0, ALU.mult, ALU.add, t)
                V.wait(t, t_tab, t_k)
                t_g = V.inc(nc.vector.tensor_tensor_scan(GG, RST[:, :], GG, 0.0, ALU.mult, ALU.add))
                t_ex = av(EX, GG, ACT.Exp, t_g, t_mx2)
                e = ring.get("w2in", 8 + h)
                bq = banks.get(T)
                t_bq = feature(bq[:, :], e, HTh, HTl)
                ring.done(e, t_bq)
                yield
                t_qd = tt(V, QD, bq[:, :], EX, ALU.mult, t_ex, t_bq, t_o)
                banks.put(bq, t_qd)
                ev = EX.rearrange("p (c n) -> p c n", c=8)
                dc = sm[:, 40:48]
                t_dc = cp(V, dc, ev[:, :, 63], t_ex, t_s)
                t = av(KD, GG, ACT.Exp, t_g, t_mm, scale=-1.0)
                t_kd = tt(V, KD, KD, FF, ALU.mult, t, t_k)
                gv = GG.rearrange("p (c n) -> p c n", c=8)
                t = tt(V, KW.rearrange("p (c n) -> p c n", c=8), gv[:, :, 63:64].to_broadcast([128, 8, 64]), gv,
                       ALU.subtract, t_kd)
                t = av(KW, KW, ACT.Exp, t)
                t_kw = tt(V, KW, KW, FF, ALU.mult, t)
                e = ring.get("w2in", 16 + h)
                bg = banks.get(T)
                t_bg = feature(bg[:, :], e, HTh, HTl)
                ring.done(e, t_bg)
                t_hg = av(HGB, bg[:, :], ACT.Silu, t_bg, t_mx2)
                banks.put(bg, t_hg)
                yield
                bank = banks.get(T)
                T.wait(t_qd, t_kd)
                for c in range(4):
                    cs = slice(c * 128, (c + 1) * 128)
                    ins = mm(bank[:, cs], KD[:, cs], QD[:, cs], start=True, stop=True)
                t_mm = T.inc(ins)
                V.wait(t_mm, t_o)
                t_att = V.inc(nc.vector.copy_predicated(ATT.rearrange("p (c n) -> p c n", c=4),
                                                        hgm.unsqueeze(1).to_broadcast([128, 4, 128]),
                                                        bank[:, :].rearrange("p (c n) -> p c n", c=4)))
                banks.put(bank, t_att)
                _t, t_kwt = turn(A, KWT, [KW[:, c * 128:(c + 1) * 128] for c in range(4)], t_kw)
                t_mm = _t
                yield
                T.wait(t_kwt)
                b4 = [banks.get(T), banks.get(T)]
                for c in range(8):
                    pp = slice(64 * (c % 2), 64 * (c % 2) + 64)
                    t_u = T.inc(mm(b4[c % 2][:, (c // 2) * 128:(c // 2 + 1) * 128], KWT[pp, c // 2, :],
                                   HV[pp, c // 2, h * 128:(h + 1) * 128], start=True, stop=True))
                t_s = t_at0
                tss = [t_at0]
                for c in range(7):
                    t_s = stt(SS[c + 1], SS[c], dc[:, c:c + 1], b4[c % 2][:, (c // 2) * 128:(c // 2 + 1) * 128],
                              ALU.mult, ALU.add, t_u, t_s, t_dc)
                    tss.append(t_s)
                for b_ in b4:
                    banks.put(b_, t_s)
                yield
                bo = banks.get(T)
                T.wait(t_att)
                for c in range(4):
                    for j in range(2):
                        cj = 2 * c + j
                        cs = slice(cj * 64, (cj + 1) * 64)
                        T.wait(tss[cj])
                        mm(bo[:, cs], HV[:, c, h * 128:(h + 1) * 128], ATT[:, cs], start=True, stop=False)
                        ins = mm(bo[:, cs], SS[cj], QD[:, cs], start=False, stop=True)
                t_o = T.inc(ins)
                t = av(REC, bo[:, :], ACT.Square, t_o)
                yield
                b5, t = rows_sum(REC, "o128", t)
                t, t0 = rsqrt(EX, b5[:, :], "eps6", t, V.now())
                banks.put(b5, t0)
                t = stt(EX, bo[:, :], C("hn", 0), EX, ALU.mult, ALU.mult, t)
                banks.put(bo, t)
                t_mx2 = tt(V, MX[:, 4 + h, :], EX, HGB, ALU.mult, t, t_hg)
                yield

        rec = recurrence()
        f_pb, f_pt = [None] * 3, [None] * 2
        st = {}
        t_mx = None
        for n in range(34):
            if n < 32:
                h, qt, i = n // 4, n % 4, n % 3
                ps = slice(64 * (h % 2), 64 * (h % 2) + 64)
                nk = (qt + 1) * 128
                bank = banks.get(T)
                t = chain(bank[:, 0:nk], [(QT[ps, h // 2, qt * 128:(qt + 1) * 128], KT[ps, h // 2, 0:nk])], t_qk)
                t = stt(PB[i][:, 0:nk], bank[:, 0:nk], 0.125, AL[:, al_at[qt]:al_at[qt] + nk], ALU.mult, ALU.add, t,
                        f_pb[i], t_tab)
                banks.put(bank, t)
                V.wait(t)
                t = V.inc(nc.vector.tensor_reduce(ms_[i][:, 0:1], PB[i][:, 0:nk], AX.X, ALU.max))
                t = ts(V, ms_[i][:, 1:2], ms_[i][:, 0:1], -1.0, None, ALU.mult, None, t)
                A.wait(t)
                t_e = A.inc(act(PB[i][:, 0:nk], PB[i][:, 0:nk], ACT.Exp, bias=ms_[i][:, 1:2], accum_out=ms_[i][:, 2:3]))
                st[n] = [t_e, None]
            if 0 <= n - 1 < 32:
                m = n - 1
                qt, i, j = m % 4, m % 3, m % 2
                nk = (qt + 1) * 128
                V.wait(st[m][0])
                t = V.inc(nc.vector.reciprocal(ms_[i][:, 3:4], ms_[i][:, 2:3]))
                t = ts(V, PB[i][:, 0:nk], PB[i][:, 0:nk], ms_[i][:, 3:4], None, ALU.mult, None, t)
                next(rec, None)
                bank = banks.get(T)
                T.wait(t)
                for k in range(qt + 1):
                    ins = nc.tensor.transpose(bank[:, k * 128:(k + 1) * 128], PB[i][:, k * 128:(k + 1) * 128],
                                              K("ident"))
                t = T.inc(ins)
                f_pb[i] = t
                t = cp(A, PT[j][:, 0:qt + 1, :], bank[:, 0:nk].rearrange("p (k n) -> p k n", k=qt + 1), t, f_pt[j])
                banks.put(bank, t)
                st[m][1] = t
            if 0 <= n - 2:
                m = n - 2
                h, qt, j = m // 4, m % 4, m % 2
                ps = slice(64 * (h % 2), 64 * (h % 2) + 64)
                if qt == 0:
                    bo = banks.get(T)
                T.wait(st[m][1], t_v)
                for k in range(qt + 1):
                    ins = mm(bo[ps, qt * 128:(qt + 1) * 128], VV[:, k, h * 64:(h + 1) * 64], PT[j][:, k, :],
                             start=(k == 0), stop=(k == qt))
                t = T.inc(ins)
                f_pt[j] = t
                if qt == 3:
                    t_mx = cp(V, MX[ps, h // 2, :], bo[ps, :], t)
                    banks.put(bo, t_mx)
        for _r in rec:
            pass
        phase(at_)
        MXh = here("MXh", [128, 8, 512], FR)
        MXl = here("MXl", [128, 8, 512], FR)
        A.wait(T.now())
        V.wait(T.now())
        t_m = [split(MXh[:, c, :], MXl[:, c, :], MX[:, c, :], t_mx if c < 4 else t_mx2) for c in range(8)]
        sq = Squares()
        for c in range(8):
            e = ring.get("wo2", c)
            bank = banks.get(T)
            t = feature(bank[:, :], e, MXh, MXl, xt=t_m)
            ring.done(e, t)
            t_x = tt(V, XT[:, c, :], bank[:, :], XT[:, c, :], ALU.add, t)
            banks.put(bank, t_x)
            sq.add(c, t_x)

        def store(c, t):
            S.wait(t)
            d_o.inc(nc.sync.dma_start(outT[:, c, :], XT[:, c, :]))

        ffn("n2", "f21", "f23", "f22", sq, store)
        S.wait(d_o.now())
        return ring.keys, ring2.keys


def program(nc, arrays, plans):
    aps = {n: nc.dram_tensor("in_" + n, a.shape, F32, kind="ExternalInput").ap() for n, a in arrays.items()}
    out = nc.dram_tensor("out_x", (128, 8, 512), F32, kind="ExternalOutput").ap()
    return build(nc, aps, out, plans)


def _chunks(w, kc=None):
    k, n = w.shape
    return np.ascontiguousarray(w.reshape(k // 128, 128, n // 128, 128).transpose(2, 1, 0, 3)).reshape(
        n // 128, 128, k)


def _rows(w):
    k, n = w.shape
    return np.ascontiguousarray(w.reshape(k // 128, 128, n).transpose(1, 0, 2))


def _cols(v):
    return v.reshape(-1, 128).T


def _constants():
    f = np.float32
    i = np.arange(128)
    m, n = i[:, None], i[None, :]
    km = np.zeros((128, NKM), f)

    def put(name, a):
        a = np.asarray(a, f)
        km[:, KM[name]:KM[name] + a.shape[1]] = a

    put("ident", m == n)
    put("ones", np.ones((128, 128)))
    put("o1024", np.full((128, 128), 1 / 1024))
    put("o2048", np.full((128, 128), 1 / 2048))
    put("hb", (m // 64 == n // 64) / 64)
    put("o128", np.full((128, 128), 1 / 128))
    put("triU", m <= n)
    put("triL", m >= n)
    put("sU", m < n)
    put("sL", m > n)
    put("mF", np.where(n >= m, 0, -1e30))
    put("mB", np.where(n <= m, 0, -1e30))
    md = n % 64
    put("psw", ((md < 8) & (m == n + 8)) | ((md >= 8) & (md < 16) & (m == n - 8)))
    put("iota", np.broadcast_to(n, (128, 128)))
    put("iotag", np.broadcast_to(np.arange(32)[None] // 8, (128, 32)))
    t, k = np.arange(8)[None] // 2, np.arange(8)[None] % 2
    put("tok", t * 128 + m + 1)
    put("aid", (t * 128 + m) * 2 + k + 1)
    put("slot", 1025.0 + m)
    put("eps5", np.full((128, 1), 1e-5))
    put("eps6", np.full((128, 1), 1e-6))
    km[:, KM["hgm"]:KM["hgm"] + 128] = np.where((m // 64 == n // 64) & (m <= n), 1, 0).astype(np.uint32).view(f)
    pos = np.arange(512)
    inv = (f(500000.0) ** (-np.arange(0, 16, 2, dtype=f) / f(16))).astype(f)
    ang = pos.astype(f)[:, None] * inv[None]
    cs = np.zeros((128, 2, 512), f)
    cs[:, 0] = 1
    for p in range(128):
        d = p % 64
        if d < 16:
            cs[p, 0] = np.cos(ang[:, d % 8])
            cs[p, 1] = np.sin(ang[:, d % 8]) * (-1 if d < 8 else 1)
    q, s = pos[:, None], pos[None, :]
    df = q - s
    cnt = ((df >= 0) & (df <= 128)).astype(int) + ((df >= 0) & (df % 4 == 0)) + ((df >= 0) & (df % 16 == 0))
    al = np.where(cnt > 0, np.log(np.maximum(cnt, 1)), -1e30).astype(f).reshape(4, 128, 512).transpose(1, 0, 2)
    rst = np.broadcast_to((pos % 64 != 0).astype(f)[None], (128, 512))
    pm = np.zeros((4, 512, 512), f)
    for g, w in enumerate((2, 4, 8, 16)):
        def win(n_):
            a = np.arange(n_)
            lo, hi = np.clip(a - w // 2, 0, n_), np.clip(a - w // 2 + w, 0, n_)
            return ((a[None] >= lo[:, None]) & (a[None] < hi[:, None])) / (hi - lo)[:, None].astype(np.float64)
        pm[g] = (np.kron(win(8), win(64)) - np.eye(512)).T
    pm = pm.reshape(4, 4, 128, 512).transpose(0, 2, 1, 3)
    c = np.ascontiguousarray
    al = np.concatenate([al[:, i, 0:128 * (i + 1)] for i in range(4)], axis=1)
    return {"km": km, "cs": cs, "al": c(al), "rst": c(rst), "pm": c(pm)}


def _lay_out(x):
    a = {k: np.asarray(v) for k, v in x.items()}
    w_in = a["w_in"][0]
    w2 = a["w_in_2"][0]
    pc = [_cols(a["b_ada"][0]), _cols(a["b_gate"][0]),
          a["conv_w"][0].reshape(5, 24, 128).transpose(2, 1, 0).reshape(128, 120), _cols(a["conv_b"][0]),
          _cols(a["ssd_norm_g"][0]), _cols(a["pool_scale"][0]), _cols(a["ln1_g"][0]), _cols(a["ln1_b"][0]),
          _cols(a["ln2_g"][0]), _cols(a["ln2_b"][0]), _cols(a["ffn1_norm_2"][0]), _cols(a["mix_norm_2"][0]),
          _cols(a["ffn2_norm_2"][0]), np.tile(a["q_norm_2"][0], 2)[:, None], np.tile(a["k_norm_2"][0], 2)[:, None],
          _cols(a["hg_lb_logits_2"][0]), _cols(a["hg_lb_logits_2"][1]), a["hg_out_norm_2"][0][:, None],
          np.stack([_cols(a["c"][0]), _cols(a["c_ctx"])], axis=2).reshape(128, 16)]
    pr = np.concatenate([a["dt_bias"].reshape(-1), a["a_log"].reshape(-1), a["d_skip"].reshape(-1),
                         a["b_router_group"].reshape(-1), a["b_router_expert"].reshape(-1)])
    wre = a["w_router_expert"][0].transpose(1, 0, 2).reshape(1024, 32)
    ab = w2
    r = {
        "pc": np.ascontiguousarray(np.concatenate(pc, axis=1)),
        "pr": np.ascontiguousarray(np.broadcast_to(pr[None], (128, NPR))),
        "xT": _rows(np.ascontiguousarray(a["x"][0].T)), "ctxT": _rows(np.ascontiguousarray(a["ctx"][0].T)),
        "wada": _chunks(a["w_ada"][0]), "wdt": _rows(w_in[:, 5120:5184]),
        "wz": _chunks(w_in[:, 0:2048]), "wxbc": _chunks(w_in[:, 2048:5120]),
        "wu": _rows(w_in[:, 5184:6208]), "wg": _chunks(w_in[:, 6208:8256]),
        "pw": _rows(a["pool_w"][0].reshape(1024, 256)),
        "wa": _chunks(a["w_branch_a"][0]), "wb": _chunks(a["w_branch_b"][0]), "wo": _chunks(a["w_out"][0]),
        "wr": _rows(np.concatenate([a["w_router_group"][0], wre], axis=1)),
        "eg": a["w_expert_gate"][0], "eu": a["w_expert_up"][0], "ed": a["w_expert_down"][0],
        "w2in": _chunks(np.concatenate([ab[:, 0:1024], ab[:, 1536:2560], ab[:, 3072:3584]], axis=1)),
        "w2v": _rows(ab[:, 1024:1536]), "w2i": _rows(ab[:, 2560:3072]), "wo2": _chunks(a["w_out_2"][0]),
        "f11": _chunks(a["ffn1_w1_2"][0]), "f13": _chunks(a["ffn1_w3_2"][0]), "f12": _chunks(a["ffn1_w2_2"][0]),
        "f21": _chunks(a["ffn2_w1_2"][0]), "f23": _chunks(a["ffn2_w3_2"][0]), "f22": _chunks(a["ffn2_w2_2"][0]),
    }
    r.update(_constants())
    return r


def kernel(**inputs):
    import concourse.bacc as _bacc
    from concourse.bass_utils import run_bass_kernel_spmd as _run

    arrays = _lay_out(inputs)
    nc = _bacc.Bacc("TRN2", target_bir_lowering=False, num_devices=1)
    plans = program(_bacc.Bacc("TRN2", target_bir_lowering=False, num_devices=1), arrays, None)
    program(nc, arrays, plans)
    r = _run(nc, [{"in_" + k: v for k, v in arrays.items()}], core_ids=[0])
    y = r.results[0]["out_x"]
    return np.ascontiguousarray(y.transpose(2, 1, 0).reshape(1, 512, 1024))
```

```python
from contextlib import ExitStack

import numpy as np

import concourse.bass as bass
from concourse import mybir

F32 = mybir.dt.float32
FR = mybir.dt.float32r
I32 = mybir.dt.int32
U32 = mybir.dt.uint32
ALU = mybir.AluOpType
ACT = mybir.ActivationFunctionType
AX = mybir.AxisListType

ALPHA = 2.0 ** 0.25
CAP = 128
NOV = 7
OVB = 3
NBLK = 32 + NOV
NRAW = 4
NHL = 5
WORDS = 53200
AHEAD = 4

PC = {}
_n = 0
for _name, _w in (("b_ada", 48), ("b_gate", 16), ("conv_w", 120), ("conv_b", 24), ("ssd_g", 16),
                  ("pool_scale", 8), ("ln1_g", 8), ("ln1_b", 8), ("ln2_g", 8), ("ln2_b", 8),
                  ("n1", 8), ("nm", 8), ("n2", 8), ("qn", 1), ("kn", 1), ("lb0", 4), ("lb1", 4),
                  ("hn", 1), ("cc", 16)):
    PC[_name] = _n
    _n += _w
NPC = _n
PR_DTB, PR_ALOG, PR_SKIP, PR_RB = 0, 64, 128, 160
NPR = 196
KM = {}
_n = 0
for _name in ("ident", "ones", "o1024", "o2048", "hb", "o128", "triU", "triL", "sU", "sL", "mF", "mB", "psw",
              "iota"):
    KM[_name] = _n
    _n += 128
KM["iotag"] = _n
_n += 32
KM["tok"] = _n
_n += 8
KM["aid"] = _n
_n += 8
KM["slot"] = _n
_n += 1
KM["hgm"] = _n
_n += 128
KM["eps5"] = _n
KM["eps6"] = _n + 1
_n += 8
NKM = _n


class Eng:

    def __init__(self, e, sem):
        self.e, self.sem, self.n, self.seen = e, sem, 0, {}

    def wait(self, *toks):
        for t in toks:
            if t is None:
                continue
            sem, v = t
            if self.seen.get(id(sem), 0) < v:
                self.e.wait_ge(sem, v)
                self.seen[id(sem)] = v

    def inc(self, ins):
        ins.then_inc(self.sem, 1)
        self.n += 1
        return (self.sem, self.n)

    def now(self):
        return (self.sem, self.n) if self.n else None


class Dma:

    def __init__(self, sem):
        self.sem, self.n = sem, 0

    def inc(self, ins):
        ins.then_inc(self.sem, 16)
        self.n += 16
        return (self.sem, self.n)

    def now(self):
        return (self.sem, self.n) if self.n else None


class Banks:

    def __init__(self, banks):
        self.free = [(b, None) for b in banks]

    def get(self, eng):
        b, t = self.free.pop(0)
        eng.wait(t)
        return b

    def put(self, b, tok):
        self.free.append((b, tok))


def resolve(I, key):
    name, c = key[0], key[1]
    w = I[name]
    if name in ("eg", "eu"):
        return w[c].rearrange("(k p) n -> p k n", p=128)[:, 2 * key[2]:2 * key[2] + 2, :]
    if name == "ed":
        return w[c].rearrange("(k p) n -> p k n", p=128)[:, key[2]:key[2] + 1, :]
    if name == "wada":
        return w[:, 2 * key[2]:2 * key[2] + 2, c * 512:(c + 1) * 512]
    if name in ("wu", "w2v", "w2i"):
        return w[:, 4 * key[2]:4 * key[2] + 4, c * 256:(c + 1) * 256]
    if name == "pm":
        return w[c][:, 2 * key[2]:2 * key[2] + 2, :]
    if name in ("pw", "wdt", "wr"):
        return w[:, c:c + 4, :] if name == "pw" else w[:, :, :]
    k0 = key[2] if len(key) > 2 else 0
    k1 = min(k0 + 1024, w.shape[2])
    if name in ("f12", "f22") and k0 < 1408:
        k1 = min(k1, 1408)
    return w[c][:, k0:k1].rearrange("p (a b) -> p a b", b=128)


class Ring:

    def __init__(self, plan, src, raw, hl, S, A, V, G, dmas, planning):
        self.plan, self.src, self.raw, self.hl = plan, src, raw, hl
        self.S, self.A, self.V, self.G, self.dmas = S, A, V, G, dmas
        self.i = 0
        self.nl = self.ns = 0
        self.slots = [raw[:, i, :] for i in range(NRAW)]
        self.raw_free = [(i, None) for i in range(NRAW)]
        self.hl_free = [(h, None) for h in range(NHL)]
        self.slot = {}
        self.loaded = {}
        self.ready = {}
        self.planning = planning
        self.stop = None
        self.keys = []

    def advance(self, split=True):
        while self.nl < self.limit() and self.raw_free:
            n = self.nl
            r, freed = self.raw_free.pop(0)
            key = self.plan[n][0]
            s = self.src(key)
            self.S.wait(freed)
            a, b = s.shape[1], s.shape[2]
            dst = self.slots[r][:, 0:a * b].rearrange("p (a b) -> p a b", a=a)
            self.loaded[n] = (self.dmas[r].inc(self.S.e.dma_start(dst, s)), a, b, r)
            self.nl += 1
        while split and self.ns < min(self.nl, self.i + AHEAD) and self.split_one():
            pass

    def lend(self, slots, dmas, tok):
        for x, d in zip(slots, dmas):
            self.raw_free.append((len(self.slots), tok))
            self.slots.append(x)
            self.dmas.append(d)

    def take_back(self):
        self.raw_free = [x for x in self.raw_free if x[0] < NRAW]
        assert len(self.raw_free) == NRAW

    def limit(self):
        if self.stop:
            for n, (key, _kind) in enumerate(self.plan):
                if key[0] == self.stop:
                    return n
        return len(self.plan)

    def split_one(self):
        n = self.ns
        key, kind = self.plan[n]
        tok, a, b, r = self.loaded[n]
        w = a * b
        if kind == "raw":
            self.ready[n] = (self.slots[r][:, 0:w].rearrange("p (a b) -> p a b", a=a), None, tok, ("raw", r))
            self.ns += 1
            return True
        if not self.hl_free:
            return False
        h, freed = self.hl_free.pop(0)
        hi, lo = self.hl[:, h, 0, 0:w], self.hl[:, h, 1, 0:w]
        rw = self.slots[r][:, 0:w]
        self.A.wait(tok, freed)
        t = self.A.inc(self.A.e.activation(hi, rw, ACT.Copy))
        self.V.wait(tok, freed, t)
        t = self.V.inc(self.V.e.tensor_tensor(lo, rw, hi.bitcast(F32), ALU.subtract))
        self.raw_free.append((r, t))
        self.ready[n] = (hi.rearrange("p (a b) -> p a b", a=a), lo.rearrange("p (a b) -> p a b", a=a), t, ("hl", h))
        self.ns += 1
        return True

    def get(self, *key, kind="split"):
        if self.planning:
            self.keys.append((key, kind))
            self.plan.append((key, kind))
        assert self.plan[self.i] == (key, kind), (self.plan[self.i], key, kind)
        self.advance()
        n = self.i
        self.i += 1
        assert n in self.ready, ("a slot is held too long", key)
        self.advance()
        return self.ready.pop(n)

    def done(self, e, tok):
        kind, i = e[3]
        if kind == "raw":
            self.raw_free.append((i, tok))
        else:
            self.hl_free.append((i, tok))
        self.advance()


def build(nc, I, outT, plans=None):
    ctx = ExitStack()
    with ctx:
        def sb(name, shape, dt=F32):
            return ctx.enter_context(nc.sbuf_tensor(name, shape, dt))

        def sem(name):
            return ctx.enter_context(nc.semaphore(name))

        banks = Banks([ctx.enter_context(nc.psum_tensor(f"bank{i}", [128, 512], F32)) for i in range(8)])
        T = Eng(nc.tensor, sem("s_pe"))
        V = Eng(nc.vector, sem("s_dve"))
        A = Eng(nc.scalar, sem("s_act"))
        G = Eng(nc.gpsimd, sem("s_pool"))
        S = Eng(nc.sync, sem("s_sp"))
        arena = sb("arena", [128, WORDS])
        base = nc.sbuf_base - 4 * WORDS
        at = [0]

        def place(name, shape, dt=F32, off=None):
            w = 1
            for x in shape[1:]:
                w *= x
            o_ = at[0] if off is None else off
            w = (w + 7) // 8 * 8
            if off is None:
                at[0] += w
            assert o_ + w <= WORDS, (name, o_ + w)
            return nc.alloc_sbuf_tensor_at(name, shape, dt, offset=base + 4 * o_)

        raw = place("raw", [128, NRAW, 1024])
        HLB = place("HLB", [128, NHL, 2, 1024], FR)
        dry = plans is None
        ring = Ring([] if dry else plans[0], lambda k: resolve(I, k), raw, HLB, S, A, V, G,
                    [Dma(sem(f"s_ring{i}")) for i in range(NRAW)], dry)
        d_c = Dma(sem("d_c"))
        d_x = Dma(sem("d_x"))
        d_h = Dma(sem("d_h"))
        d_g = Dma(sem("d_g"))
        d_s = Dma(sem("d_s"))
        d_y = Dma(sem("d_y"))
        d_t = Dma(sem("d_t"))
        d_o = Dma(sem("d_o"))

        ZD = nc.dram_tensor("z_scratch", (16, 128, 512), F32, kind="Internal").ap()
        GD = nc.dram_tensor("g_scratch", (16, 128, 512), F32, kind="Internal").ap()
        UD = nc.dram_tensor("u_scratch", (4, 128, 4, 256), F32, kind="Internal").ap()
        YZD = nc.dram_tensor("yz_scratch", (16, 128, 512), F32, kind="Internal").ap()
        H2 = nc.dram_tensor("h2_scratch", (512, 1024), F32, kind="Internal").ap()
        YD = nc.dram_tensor("y_scratch", (1024, 1024), F32, kind="Internal").ap()

        km = place("km", [128, NKM])
        pc = place("pc", [128, NPC])
        pr = place("pr", [128, NPR])
        HTh = place("HTh", [128, 8, 512], FR)
        HTl = place("HTl", [128, 8, 512], FR)
        mod = place("mod", [128, 48, 2])
        sm = place("sm", [128, 80])
        wk = place("wk", [128, 4, 2])
        gi = place("gi", [128, 4, 8], U32)
        vi = place("vi", [128, 4, 8], U32)
        eidi = place("eidi", [128, NOV + 1], I32)
        ix = place("ix", [128, 2, NBLK], U32)
        SQ = place("SQ", [128, 512])
        RA = place("RA", [128, 512])
        TMP = [place(f"tmp{i}", [128, 512]) for i in range(6)]
        DEC = at[0]
        dec = place("dec", [128, 6, 64])
        acs = place("acs", [128, 4, 64])
        eacs = place("eacs", [128, 4, 64])
        tw = place("tw", [128, 4, 64])
        etot = place("etot", [128, 4, 64])
        cw = place("cw", [128, 2, 64])
        ats = place("ats", [64, 2, 512], FR)
        oneh = place("oneh", [64, 64, 1], FR)
        DEC_END = at[0]
        W0 = at[0]
        XT = place("XT", [128, 8, 512])
        W1 = at[0]
        cur = [0]

        def here(name, shape, dt=F32):
            w = 1
            for x in shape[1:]:
                w *= x
            t_ = place(name, shape, dt, off=cur[0])
            cur[0] += (w + 7) // 8 * 8
            return t_

        def phase(start):
            cur[0] = start

        mm, act = nc.tensor.matmul, nc.scalar.activation

        def K(name, w=128, p=128):
            return km[0:p, KM[name]:KM[name] + w]

        def C(name, i, w=1):
            return pc[:, PC[name] + i:PC[name] + i + w]

        def tt(E, out, a, b, op, *waits):
            E.wait(*waits)
            return E.inc(E.e.tensor_tensor(out, a, b, op))

        def ts(E, out, a, s1, s2, op0, op1, *waits):
            E.wait(*waits)
            if s2 is None:
                return E.inc(E.e.tensor_scalar(out, a, s1, None, op0))
            return E.inc(E.e.tensor_scalar(out, a, s1, s2, op0, op1))

        def stt(out, a, s, b, op0, op1, *waits):
            V.wait(*waits)
            return V.inc(nc.vector.scalar_tensor_tensor(out=out, in0=a, scalar=s, in1=b, op0=op0, op1=op1))

        def recip(out, a, *waits):
            V.wait(*waits)
            return V.inc(nc.vector.reciprocal(out, a))

        def rsqrt(out, a, eps, *waits):
            t0 = av(out, a, ACT.Ln, *waits, bias=K(eps, 1))
            return av(out, out, ACT.Exp, t0, scale=-0.5), t0

        def av(out, a, f, *waits, **kw):
            A.wait(*waits)
            return A.inc(act(out, a, f, **kw))

        def cp(E, out, a, *waits):
            if E is A:
                return av(out, a, ACT.Copy, *waits)
            E.wait(*waits)
            return E.inc(E.e.tensor_copy(out, a))

        def bc(ap, n):
            return ap.unsqueeze(2).to_broadcast([ap.shape[0], ap.shape[1], n])

        def split(hi, lo, src, *waits):
            t1 = cp(A, hi, src, *waits)
            return tt(V, lo, src, hi.bitcast(F32), ALU.subtract, t1, *waits)

        class Splits:

            def __init__(self):
                self.toks, self.pend = [], None

            def flush(self):
                if self.pend:
                    hi, lo, src, t, waits = self.pend
                    self.toks.append(tt(V, lo, src, hi.bitcast(F32), ALU.subtract, t, *waits))
                    self.pend = None
                return self.toks

            def add(self, hi, lo, src, *waits):
                t = cp(A, hi, src, *waits)
                self.flush()
                self.pend = (hi, lo, src, t, waits)

        def prod(bank, parts, *waits, start=True, stop=True, xt=None):
            T.wait(*waits)
            n = len(parts)
            for i, (ah, al, bh, bl) in enumerate(parts):
                if xt:
                    T.wait(xt[i])
                mm(bank, ah, bh, start=(start and i == 0), stop=False)
                mm(bank, ah, bl, start=False, stop=False)
                ins = mm(bank, al, bh, start=False, stop=(stop and i == n - 1))
            return T.inc(ins)

        def feature(bank, e, xh, xl, *waits, k0=0, n=8, **kw):
            return prod(bank, [(e[0][:, k, :], e[1][:, k, :], xh[:, k0 + k, :], xl[:, k0 + k, :]) for k in range(n)],
                        e[2], *waits, **kw)

        def chain(bank, pairs, *waits, m=128, inc=True):
            T.wait(*waits)
            for i, (l, r) in enumerate(pairs):
                ins = mm(bank, l, r, start=(i == 0), stop=(i == len(pairs) - 1))
            return T.inc(ins) if inc else None

        def rows_sum(acc, kname, *waits):
            bank = banks.get(T)
            return bank, chain(bank[:, :], [(K(kname), acc)], *waits)

        t_pc = Dma(sem("d_pc")).inc(nc.sync.dma_start(pc[:, :], I["pc"]))
        tc = d_c.inc(nc.scalar.dma_start(km[:, :], I["km"]))
        tc = d_c.inc(nc.scalar.dma_start(pr[:, :], I["pr"]))
        phase(W1)
        CTX = here("CTX", [128, 8, 256])
        early = here("early", [128, 5, 1024])
        ring.stop = "wz"
        ring.lend([early[:, i, :] for i in range(5)], [Dma(sem(f"s_early{i}")) for i in range(5)], None)
        sc = sm[:, 64:80]
        t_sc = av(sc, C("cc", 0, 16), ACT.Silu, t_pc)
        A.wait(t_sc)
        tx = d_x.inc(nc.scalar.dma_start(XT[:, :, :], I["xT"]))
        tx = d_x.inc(nc.scalar.dma_start(CTX[:, :, :], I["ctxT"]))

        def modulation(blocks, mrow, *free):
            bt = banks.get(T)
            t_out = t_m = None

            def turned(b):
                T.wait(t_m)
                T.wait(tc)
                for c in range(4):
                    o_ = 2 * (4 * b + c)
                    ins = mm(bt[:, o_:o_ + 2], mrow[0:2, c * 128:(c + 1) * 128], K("ident", 2, 2), start=True, stop=True)
                return T.inc(ins)

            for b in blocks:
                bank = banks.get(T)
                T.wait(t_sc)
                for a in range(4):
                    e = ring.get("wada", b, a, kind="raw")
                    T.wait(e[2])
                    for k in range(2):
                        ins = mm(bank[0:2, :], sc[:, 4 * a + 2 * k:4 * a + 2 * k + 2], e[0][:, k, :],
                                 start=(a + k == 0), stop=(a + k == 4))
                    t = T.inc(ins)
                    ring.done(e, t)
                    if a == 1:
                        yield
                if b > blocks[0]:
                    t_out = turned(b - 1)
                t_m = cp(A, mrow[0:2, :], bank[0:2, :], t, t_out, *free)
                banks.put(bank, t_m)
                yield
            t_out = turned(blocks[-1])
            c0, c1 = 4 * blocks[0], 4 * blocks[-1] + 4
            V.wait(t_out)
            t = V.inc(nc.vector.tensor_tensor(mod[:, c0:c1, :],
                                              bt[:, 2 * c0:2 * c1].rearrange("p (c j) -> p c j", j=2),
                                              bc(pc[:, PC["b_ada"] + c0:PC["b_ada"] + c1], 2), ALU.add))
            banks.put(bt, t)
            yield t

        for t in modulation(range(4), TMP[0]):
            pass
        ring.take_back()
        ring.stop = None
        ring.advance(split=False)
        del ring.slots[NRAW:], ring.dmas[NRAW:]
        t_mod01 = ts(V, mod[:, 8:16, :], mod[:, 8:16, :], 1.0, None, ALU.add, None, t)
        phase(W0 + 4096 + 8192)
        HCh = here("HCh", [128, 8, 256], FR)
        HCl = here("HCl", [128, 8, 256], FR)
        s1, s2 = Splits(), Splits()
        for k in range(8):
            t1 = ts(V, XT[:, k, :], XT[:, k, :], mod[:, 8 + k, 0:1], mod[:, k, 0:1], ALU.mult, ALU.add, t_mod01, tx)
            s1.add(HTh[:, k, :], HTl[:, k, :], XT[:, k, :], t1)
        t_hs = s1.flush()
        ring.advance()
        for k in range(8):
            t2 = ts(V, CTX[:, k, :], CTX[:, k, :], mod[:, 8 + k, 1:2], mod[:, k, 1:2], ALU.mult, ALU.add)
            s2.add(HCh[:, k, :], HCl[:, k, :], CTX[:, k, :], t2)
        t_hcs = s2.flush()
        t_h, t_hc = t_hs[7], t_hcs[7]

        phase(W0)
        Y = here("Y", [128, 4, 512])
        SQ3 = here("SQ3", [128, 512])
        XS = here("XS", [128, 4, 512])
        BT = here("BT", [128, 512])
        CTt = here("CTt", [128, 512])
        Bt = here("Bt", [128, 4, 128])
        CBT = here("CBT", [128, 512])
        XC = here("XC", [128, 2, 512])
        Bc = here("Bc", [128, 2, 128])
        ST = [here(f"ST{d}", [128, 512]) for d in range(2)]
        XCW = here("XCW", [128, 2, 512])
        XD = [here(f"XD{i}", [128, 2, 4, 64]) for i in range(2)]
        FB = [here(f"FB{i}", [128, 512]) for i in range(2)]
        assert cur[0] <= W0 + 4096 + 8192
        phase(W0 + 4096 + 8192 + 4096)
        CB = [here(f"CB{i}", [128, 776]) for i in range(2)]
        CA = [here(f"CA{i}", [128, 776]) for i in range(2)]
        YZT = [here(f"YZT{i}", [128, 512]) for i in range(2)]
        SQ2 = here("SQ2", [128, 512])
        E4 = [[TMP[0], TMP[1]], [TMP[2], TMP[3]]]
        V.wait(t_hc)
        for b in CB:
            t_pad = V.inc(nc.vector.memset(b[:, :], 0.0))
        t_sq = V.inc(nc.vector.memset(SQ[:, :], 0.0))
        A.wait(t_pad)
        G.wait(t_sq, t_hc)
        SE = [TMP[2], TMP[3]]
        cb_free = [None, None]
        ca_free = [None, None]
        nconv = 0
        yz_z = [None, None]
        d_z = [Dma(sem(f"d_z{i}")) for i in range(2)]
        d_yz = [Dma(sem(f"d_yz{i}")) for i in range(2)]
        ZB = [SQ2, RA]

        d_fb = [Dma(sem(f"d_fb{i}")) for i in range(2)]
        spilled = {}
        nf = [0]

        def spill(bank, dst, t):
            i = nf[0] % 2
            nf[0] += 1
            w = bank.shape[1]
            t = cp(A, FB[i][:, 0:w], bank, t, d_fb[i].now())
            A.wait(t)
            tok = d_fb[i].inc(nc.scalar.dma_start(dst, FB[i][:, 0:w]))
            return t, tok

        def fill():
            for q in range(16):
                e = ring.get("wz", q)
                bank = banks.get(T)
                t = feature(bank[:, :], e, HTh, HTl, xt=t_hs)
                ring.done(e, t)
                t, spilled[("z", q)] = spill(bank[:, :], ZD[q], t)
                banks.put(bank, t)
                yield
            for q in range(16):
                e = ring.get("wg", q)
                bank = banks.get(T)
                t = feature(bank[:, :], e, HTh, HTl)
                ring.done(e, t)
                t, spilled[("g", q)] = spill(bank[:, :], GD[q], t)
                banks.put(bank, t)
                yield
            for c in range(4):
                es = [ring.get("wu", c, a) for a in range(2)]
                for i in range(4):
                    cs = slice(i * 128, (i + 1) * 128)
                    bank = banks.get(T)
                    t = prod(bank[:, 0:256], [(HTh[:, k, cs], HTl[:, k, cs], es[k // 4][0][:, k % 4, :],
                                               es[k // 4][1][:, k % 4, :]) for k in range(8)], es[0][2], es[1][2])
                    if i == 3:
                        for e in es:
                            ring.done(e, t)
                    t, spilled[("u", c, i)] = spill(bank[:, 0:256], UD[c, :, i, :], t)
                    banks.put(bank, t)
                    yield
            for t in modulation(range(4, 12), FB[0], d_fb[0].now()):
                if t is None:
                    yield
            spilled["mod"] = ts(V, mod[:, 32:40, :], mod[:, 32:40, :], 1.0, None, ALU.add, None, t)

        filler = fill()

        def gap(n=1):
            for _i in range(n):
                next(filler, None)

        aa = TMP[5][:, 0:384].rearrange("p (t h) -> p t h", t=6)
        gap()
        e = ring.get("wdt", 0)
        bank, bank2 = banks.get(T), banks.get(T)
        t = prod(bank[0:64, :], [(e[0][:, k, :], e[1][:, k, :], HTh[:, k, :], HTl[:, k, :]) for k in range(8)],
                 e[2], xt=t_hs)
        t1 = cp(A, CA[0][0:64, 0:512], bank[0:64, :], t)
        banks.put(bank, t1)
        t = prod(bank2[0:64, 0:256], [(e[0][:, k, :], e[1][:, k, :], HCh[:, k, :], HCl[:, k, :]) for k in range(8)],
                 xt=t_hcs)
        ring.done(e, t)
        t1 = cp(A, CA[0][0:64, 512:768], bank2[0:64, 0:256], t)
        banks.put(bank2, t1)
        gap()
        bank = banks.get(T)
        T.wait(t1)
        for i in range(6):
            ins = nc.tensor.transpose(bank[:, i * 64:(i + 1) * 64], CA[0][0:64, i * 128:(i + 1) * 128],
                                      K("ident", 64, 64))
        t = T.inc(ins)
        ca_free[0] = t
        gap(2)
        dtr, ab, e_, u_, l_ = (TMP[i][:, 0:384] for i in range(5))
        b3 = lambda o: pr[:, o:o + 64].unsqueeze(1).to_broadcast([128, 6, 64])
        r3 = lambda a: a.rearrange("p (t h) -> p t h", t=6)
        t = tt(V, r3(dtr), r3(bank[:, 0:384]), b3(PR_DTB), ALU.add, t, tc)
        banks.put(bank, t)
        t = av(ab, dtr, ACT.Abs, t)
        t = av(e_, ab, ACT.Exp, t, scale=-1.0)
        t_u = ts(V, u_, e_, 1.0, None, ALU.add, None, t)
        t_l = av(l_, u_, ACT.Ln, t_u)
        t_d = ts(V, ab, u_, -1.0, None, ALU.add, None, t_u)
        t_z = ts(V, u_, ab, 0.0, None, ALU.is_equal, None, t_d, t_l)
        t = tt(V, ab, ab, u_, ALU.add, t_z)
        t = recip(ab, ab, t)
        t = tt(V, ab, e_, ab, ALU.mult, t)
        t_q = tt(V, l_, l_, ab, ALU.mult, t, t_l)
        t = tt(V, u_, u_, e_, ALU.mult, t_z)
        t = tt(V, l_, l_, u_, ALU.add, t, t_q)
        dt2 = dec[:, :, :].rearrange("p t h -> p (t h)")
        t_dt = stt(dt2, dtr, 0.0, l_, ALU.max, ALU.add, t)
        t = av(sm[:, 0:64], pr[:, PR_ALOG:PR_ALOG + 64], ACT.Exp, t_dt)
        t = tt(V, aa, dec[:, :, :], sm[:, 0:64].unsqueeze(1).to_broadcast([128, 6, 64]), ALU.mult, t)
        t = ts(V, aa, aa, -1.0, None, ALU.mult, None, t)
        t_a = t
        gap(2)
        b1, b2 = banks.get(T), banks.get(T)
        T.wait(t_a)
        v1 = b1[:, 0:256].rearrange("p (t h) -> p t h", t=4)
        v2 = b2[:, 0:256].rearrange("p (t h) -> p t h", t=4)
        for i in range(4):
            mm(v1[:, i, 0:32], K("triU"), aa[:, i, 0:32], start=True, stop=True)
            mm(v1[:, i, 32:64], K("triL"), aa[:, i, 32:64], start=True, stop=True)
            mm(v2[:, i, :], K("ones"), aa[:, i, :], start=True, stop=True)
        v3 = b2[:, 256:384].rearrange("p (t h) -> p t h", t=2)
        mm(v3[:, 0, 0:32], K("sL"), aa[:, 4, 0:32], start=True, stop=False)
        mm(v3[:, 0, 0:32], K("ones"), aa[:, 5, 0:32], start=False, stop=True)
        mm(v3[:, 1, 0:32], K("sL"), aa[:, 5, 0:32], start=True, stop=True)
        mm(v3[:, 0, 32:64], K("sU"), aa[:, 4, 32:64], start=True, stop=True)
        mm(v3[:, 1, 32:64], K("sU"), aa[:, 5, 32:64], start=True, stop=False)
        t = T.inc(mm(v3[:, 1, 32:64], K("ones"), aa[:, 4, 32:64], start=False, stop=True))
        t_acs = cp(V, acs[:, :, :], v1, t)
        banks.put(b1, t_acs)
        t_tl = tt(V, tw[:, :, :], v2, acs[:, :, :], ALU.subtract, t_acs)
        t_e1 = av(etot[:, :, :], v2, ACT.Exp, t_tl)
        t_e2 = av(cw[:, :, :], v3, ACT.Exp, t)
        banks.put(b2, t_e2)
        t_e3 = av(tw[:, :, :], tw[:, :, :], ACT.Exp, t_tl)
        t_e4 = av(eacs[:, :, :], acs[:, :, :], ACT.Exp, t_acs)
        tt(V, tw[:, :, :], tw[:, :, :], dec[:, 0:4, :], ALU.mult, t_e3)
        t_co = tt(V, cw[:, :, :], cw[:, :, :], dec[:, 4:6, :], ALU.mult, t_e4)
        gap()
        bank = banks.get(T)
        T.wait(t_acs)
        for i in range(4):
            ins = nc.tensor.transpose(bank[0:64, i * 128:(i + 1) * 128], acs[:, i, :], K("ident"))
        t = T.inc(ins)
        t_ats = split(ats[:, 0, :], ats[:, 1, :], bank[0:64, :], t)
        banks.put(bank, t_ats)
        cp(A, oneh[:, :, 0], K("ident", 64, 64))
        t_ats2 = A.now()

        def conv_chunk(xc, e, ctx_too):
            nonlocal nconv
            i = nconv % 2
            nconv += 1
            bank = banks.get(T)
            t = feature(bank[:, :], e, HTh, HTl, t_h)
            t1 = cp(A, CB[i][:, 2:514], bank[:, :], t, cb_free[i])
            banks.put(bank, t1)
            n = 512
            if ctx_too:
                bank = banks.get(T)
                t = feature(bank[:, 0:256], e, HCh, HCl, t_hc)
                t1 = cp(A, CB[i][:, 516:772], bank[:, 0:256], t)
                banks.put(bank, t1)
                n = 770
            t_pe = t
            t = ts(V, CA[i][:, 0:n], CB[i][:, 0:n], C("conv_w", xc * 5), C("conv_b", xc), ALU.mult, ALU.add,
                   t1, ca_free[i])
            for j in range(1, 5):
                t = stt(CA[i][:, 0:n], CB[i][:, j:j + n], C("conv_w", xc * 5 + j), CA[i][:, 0:n], ALU.mult, ALU.add, t)
            cb_free[i] = t
            t = av(CA[i][:, 0:n], CA[i][:, 0:n], ACT.Silu, t)
            return i, t, t_pe

        def turn(E, dst, srcs, *waits):
            bank = banks.get(T)
            T.wait(*waits)
            n = len(srcs)
            for j, src in enumerate(srcs):
                ins = nc.tensor.transpose(bank[:, j * 128:(j + 1) * 128], src, K("ident"))
            t = T.inc(ins)
            v = bank[:, 0:n * 128]
            if len(dst.shape) == 3:
                v = v.rearrange("p (t n) -> p t n", t=n)
            t2 = cp(E, dst, v, t)
            banks.put(bank, t2)
            return t, t2

        t_yzd = {}

        def gate(g, t_y):
            nonlocal t_sq, t_yg
            for j in range(4):
                q = 4 * g + j
                A.wait(spilled[("z", q)], yz_z[j % 2])
                t = d_z[j % 2].inc(nc.scalar.dma_start(ZB[j % 2][:, :], ZD[q]))
                by = banks.get(T)
                T.wait(t_y)
                for c in range(4):
                    ins = nc.tensor.transpose(by[:, c * 128:(c + 1) * 128], Y[:, c, j * 128:(j + 1) * 128], K("ident"))
                t_yg = T.inc(ins)
                yield
                t_s = av(ZB[j % 2][:, :], ZB[j % 2][:, :], ACT.Silu, t)
                yz = YZT[j % 2]
                t_yz = tt(V, yz[:, :], ZB[j % 2][:, :], by[:, :], ALU.mult, t_yg, t_s, d_yz[j % 2].now())
                yz_z[j % 2] = t_yz
                banks.put(by, t_yz)
                t = tt(G, SQ3[:, :], yz[:, :], yz[:, :], ALU.mult, t_yz, t_sq)
                t_sq = tt(G, SQ[:, :], SQ[:, :], SQ3[:, :], ALU.add, t)
                t = av(yz[:, :], yz[:, :], ACT.Copy, t, scale=C("ssd_g", q))
                A.wait(t)
                t_yzd[q] = d_yz[j % 2].inc(nc.scalar.dma_start(YZD[q], yz[:, :]))

        t_yg = None
        gating = None
        pe_end = v_end = g_end = None
        for g in range(4):
            order = [("b", 16 + g), ("c", 20 + g)] + [("x", 4 * g + j) for j in range(4)]

            def place_chunk(kind, xc, i, t):
                nonlocal t_xs, t_B, t_bt, t_ct
                ca = CA[i]
                blocks = [ca[:, c * 128:(c + 1) * 128] for c in range(4)]
                cblocks = [ca[:, 514 + c * 128:514 + (c + 1) * 128] for c in range(2)]
                A.wait(pe_end, v_end, g_end)
                V.wait(pe_end)
                if kind == "x":
                    q = xc - 4 * g
                    _a, ta = turn(A, XS[:, :, q * 128:(q + 1) * 128], blocks, t)
                    ca_free[i], tb = turn(V, XC[:, :, q * 128:(q + 1) * 128], cblocks)
                    t_xs = [ta, tb]
                elif kind == "b":
                    _a, ta = turn(A, Bt[:, :, :], blocks, t)
                    _b, tb = turn(V, Bc[:, :, :], cblocks)
                    t_B = [ta, tb]
                    t_bt = ca_free[i] = cp(G, BT[:, :], ca[:, 0:512], t, pe_end)
                    V.wait(_b)
                else:
                    t_ct = ca_free[i] = cp(G, CTt[:, :], ca[:, 0:512], t, pe_end)

            t_xs = t_B = t_bt = t_ct = None
            made = None
            for kind, xc in order:
                e = ring.get("wxbc", xc)
                i, t, t_pe = conv_chunk(xc, e, kind != "c")
                ring.done(e, t_pe)
                if gating:
                    next(gating, None)
                if made:
                    place_chunk(*made)
                made = (kind, xc, i, t)
            if gating:
                for _g in gating:
                    pass
            bank = banks.get(T)
            T.wait(t_bt, t_ct)
            for c in range(4):
                sl_ = slice(c * 128, (c + 1) * 128)
                ins = mm(bank[:, sl_], BT[:, sl_], CTt[:, sl_], start=True, stop=True)
            t = T.inc(ins)
            t_cb = cp(A, CBT[:, :], bank[:, :], t)
            banks.put(bank, t_cb)
            gap()
            place_chunk(*made)

            def heads(ap, d):
                return ap[:, 32 * d + 8 * g:32 * d + 8 * g + 8]

            def r8(ap):
                return ap.rearrange("p (h n) -> p h n", h=8)

            t_st, t_xw = [None, None], [None, None]
            xcw = [[XCW[:, i, :] for i in range(2)], [TMP[i][:, :] for i in range(2)]]
            for d in range(2):
                for i in range(2):
                    t_xw[d] = tt(V, r8(xcw[d][i]), r8(XC[:, i, :]), bc(heads(cw[:, i, :], d), 64), ALU.mult,
                                 t_xs[1], t_co, pe_end)
            gap()
            for d in range(2):
                bank = banks.get(T)
                t = chain(bank[:, :], [(Bc[:, i, :], xcw[d][i]) for i in range(2)], t_xw[d], t_B[1])
                t_st[d] = cp(A, ST[d][:, :], bank[:, :], t)
                banks.put(bank, t_st[d])
            t_ctx = t
            for c in range(4):
                t_y = tt(V, r8(Y[:, c, :]), r8(XS[:, c, :]), bc(pr[:, PR_SKIP + 8 * g:PR_SKIP + 8 * g + 8], 64),
                         ALU.mult, t_xs[0], t_yg)

            def decayed(h):
                out = []
                for d in range(2):
                    hh = 32 * d + 8 * g + h
                    E_ = E4[h % 2][d]
                    bank = banks.get(T)
                    t = chain(bank[:, :], [(oneh[:, hh, :].to_broadcast([64, 128]), ats[0:64, i, :]) for i in range(2)],
                              t_ats, t_ats2)
                    for c in range(4):
                        cs = slice(c * 128, (c + 1) * 128)
                        t2 = stt(E_[:, cs], bank[:, cs], acs[:, c, hh:hh + 1], K("mF" if d == 0 else "mB"),
                                 ALU.subtract, ALU.min, t, e_free[h % 2])
                    banks.put(bank, t2)
                    t = av(E_[:, :], E_[:, :], ACT.Exp, t2)
                    t3 = tt(G, XD[h % 2][:, d, :, :], XS[:, :, h * 64:(h + 1) * 64],
                            dec[:, 0:4, hh:hh + 1].to_broadcast([128, 4, 64]), ALU.mult, e_free[h % 2], t_xs[0])
                    out.append((t, t3))
                return out

            t_ty = [None, None]
            tq = [TMP[4], TMP[5]]
            t_up = [None, None]
            e_free = [t_ctx, None]
            for step in range(4):
                cs_ = (step, 3 - step)
                t_se, b_o, b_u, t_o = [None] * 2, [None] * 2, [None] * 2, [None] * 2
                for d in range(2):
                    if step < 3:
                        t_se[d] = tt(V, r8(SE[d][:, :]), r8(XS[:, cs_[d], :]), bc(heads(tw[:, cs_[d], :], d), 64),
                                     ALU.mult, t_up[d], t_xs[0], pe_end)
                for d in range(2):
                    b_o[d] = banks.get(T)
                    t_o[d] = chain(b_o[d][:, :], [(CTt[:, cs_[d] * 128:(cs_[d] + 1) * 128], ST[d][:, :])], t_st[d])
                if step < 3:
                    for d in range(2):
                        b_u[d] = banks.get(T)
                        t_up[d] = chain(b_u[d][:, :], [(Bt[:, cs_[d], :], SE[d][:, :])], t_se[d], t_B[0])
                else:
                    next_e = decayed(0)
                for d in range(2):
                    c = cs_[d]
                    if step < 3:
                        t = tt(V, r8(ST[d][:, :]), r8(ST[d][:, :]), bc(heads(etot[:, c, :], d), 64), ALU.mult,
                               t_o[d], t_st[d])
                        t_st[d] = tt(V, ST[d][:, :], ST[d][:, :], b_u[d][:, :], ALU.add, t, t_up[d])
                        banks.put(b_u[d], t_st[d])
                for d in range(2):
                    c = cs_[d]
                    t = tt(V, r8(tq[d][:, :]), r8(b_o[d][:, :]), bc(heads(eacs[:, c, :], d), 64), ALU.mult,
                           t_o[d], t_ty[d])
                    banks.put(b_o[d], t)
                    t_ty[d] = tt(G, Y[:, c, :], Y[:, c, :], tq[d][:, :], ALU.add, t, t_y, *t_ty)
                gap()
            e_free[1] = t_up[1]
            late = None

            def add_y(h, bank, t):
                t_y = tt(V, Y[:, :, h * 64:(h + 1) * 64], Y[:, :, h * 64:(h + 1) * 64],
                         bank[:, 0:256].rearrange("p (t n) -> p t n", t=4), ALU.add, t, *t_ty)
                banks.put(bank, t_y)
                return t_y

            for h in range(8):
                this = next_e
                ts_ = []
                for d in range(2):
                    E_ = E4[h % 2][d]
                    ts_.append(tt(V, E_[:, :], E_[:, :], CBT[:, :], ALU.mult, this[d][0], t_cb))
                if h < 7:
                    next_e = decayed(h + 1)
                if late:
                    add_y(*late)
                gap()
                bank = banks.get(T)
                T.wait(*ts_, this[0][1], this[1][1])
                for c in range(4):
                    for d in range(2):
                        ins = mm(bank[:, c * 64:(c + 1) * 64], E4[h % 2][d][:, c * 128:(c + 1) * 128],
                                 XD[h % 2][:, d, c, :], start=(d == 0), stop=(d == 1))
                t = e_free[h % 2] = T.inc(ins)
                late = (h, bank, t)
            t_y = add_y(*late)
            pe_end, v_end, g_end = T.now(), V.now(), G.now()
            gating = gate(g, t_y)
        for _f in filler:
            pass

        t_mod = spilled["mod"]
        for E_ in (A, V, G):
            E_.wait(pe_end, v_end, g_end, T.now(), d_fb[0].now(), d_fb[1].now())
        d_ld = [Dma(sem(f"d_ld{i}")) for i in range(4)]
        phase(W1)
        ACC = here("ACC", [128, 8, 512])
        at_ = cur[0]
        YL_ = here("YL_", [128, 8, 512], FR)
        YH = here("YH", [128, 8, 512], FR)
        n_ld = [0]
        ld_free = [(V.now(), A.now())] * 4

        def fetch(src, *waits, w=512):
            i = n_ld[0] % 4
            n_ld[0] += 1
            f = ld_free[i]
            G.wait(*(f if isinstance(f[0], tuple) else (f,)), *waits)
            v = TMP[i][:, 0:w]
            return i, d_ld[i].inc(nc.gpsimd.dma_start(v if len(src.shape) == 2 else
                                                      v.rearrange("p (a b) -> p a b", a=src.shape[1]), src))

        t_a = [None] * 8
        half_done = None
        t_us, t_dp = {}, {}

        def load_u(g):
            U = UU[g % 2]
            for m in range(2):
                i, t = fetch(UD[g, :, 2 * m:2 * m + 2, :])
                t_us[g] = ld_free[i] = split(U[0][:, 2 * m:2 * m + 2, :], U[1][:, 2 * m:2 * m + 2, :],
                                             TMP[i][:, :].rearrange("p (a b) -> p a b", a=2), t, t_dp.get(g - 2))

        for n in range(2):
            ty = Splits()
            if n:
                phase(W0)
                UU = [[here(f"U{i}{p}", [128, 4, 256], FR) for p in "hl"] for i in range(2)]
                A.wait(T.now())
                V.wait(T.now())
            for k in range(8):
                i, t = fetch(YZD[8 * n + k], t_yzd[8 * n + k])
                ty.add(YH[:, k, :], YL_[:, k, :], TMP[i][:, :], t, half_done)
                ty.flush()
                ld_free[i] = ty.toks[-1]
            for c in range(8):
                e = ring.get("wa", c, 1024 * n)
                bank = banks.get(T)
                t = feature(bank[:, :], e, YH, YL_, xt=ty.toks)
                ring.done(e, t)
                half_done = t
                if n == 0:
                    t_a[c] = cp(A, ACC[:, c, :], bank[:, :], t)
                    next(gating, None)
                else:
                    t = tt(V, ACC[:, c, :], bank[:, :], ACC[:, c, :], ALU.add, t, t_a[c])
                    t_a[c] = tt(G, ACC[:, c, :], ACC[:, c, :], RA[:, :], ALU.mult, t, t_ra)
                    if c in (3, 5):
                        load_u(c // 5)
                banks.put(bank, t_a[c] if n == 0 else t)
            if n == 0:
                for _g in gating:
                    pass
                bank, t = rows_sum(SQ[:, :], "o2048", t_sq)
                t_ra, t = rsqrt(RA[:, :], bank[:, :], "eps5", t, V.now())
                banks.put(bank, t)

        phase(at_)
        YPh = here("YPh", [128, 8, 512], FR)
        YPl = here("YPl", [128, 8, 512], FR)
        DD = [[here(f"D{i}{p}", [128, 2, 512], FR) for p in "hl"] for i in range(2)]
        V.wait(half_done)
        A.wait(half_done)
        t_dd, t_p, t_yps = {}, {}, []
        ew = None
        for s_ in range(5):
            if s_ < 4:
                g = s_
                U, D = UU[g % 2], DD[g % 2]
                es = [ring.get("pm", g, a) for a in range(2)]
                for j in range(2):
                    bank = banks.get(T)
                    cs = slice(j * 128, (j + 1) * 128)
                    t = prod(bank[:, :], [(U[0][:, i, cs], U[1][:, i, cs], es[i // 2][0][:, i % 2, :],
                                           es[i // 2][1][:, i % 2, :]) for i in range(4)], es[0][2], es[1][2], t_us[g])
                    t_dd[g] = split(D[0][:, j, :], D[1][:, j, :], bank[:, :], t, t_p.get(g - 2))
                    banks.put(bank, t_dd[g])
                t_dp[g] = t
                for e in es:
                    ring.done(e, t)
                if g < 2:
                    load_u(g + 2)
            if s_:
                g = s_ - 1
                D = DD[g % 2]
                if g % 2 == 0:
                    ew = ring.get("pw", 2 * g)
                for m in range(2):
                    bank = banks.get(T)
                    ms_ = slice(m * 128, (m + 1) * 128)
                    kk = 2 * (g % 2)
                    t = prod(bank[:, :], [(ew[0][:, kk + k, ms_], ew[1][:, kk + k, ms_], D[0][:, k, :], D[1][:, k, :])
                                          for k in range(2)], ew[2], t_dd[g])
                    t1 = av(TMP[4 + m][:, :], bank[:, :], ACT.Copy, t, *t_yps[-2:-1], scale=C("pool_scale", 2 * g + m))
                    banks.put(bank, t1)
                    t_yp = split(YPh[:, 2 * g + m, :], YPl[:, 2 * g + m, :], TMP[4 + m][:, :], t1)
                    t_yps.append(t_yp)
                t_p[g] = t
                if g % 2:
                    ring.done(ew, t)
        G.wait(t_dp[3])
        tx = Dma(sem("d_x2")).inc(nc.gpsimd.dma_start(XT[:, :, :], I["xT"]))
        for c in range(8):
            ia, t1 = fetch(GD[c])
            ip, t2 = fetch(GD[8 + c])
            t1 = av(TMP[ia][:, :], TMP[ia][:, :], ACT.Sigmoid, t1, bias=C("b_gate", c))
            t2 = av(TMP[ip][:, :], TMP[ip][:, :], ACT.Sigmoid, t2, bias=C("b_gate", 8 + c))
            t3 = tt(G, ACC[:, c, :], ACC[:, c, :], TMP[ia][:, :], ALU.mult, t1, t_a[c])
            ld_free[ia] = t3
            e = ring.get("wb", c)
            bank = banks.get(T)
            t = feature(bank[:, :], e, YPh, YPl, xt=t_yps)
            ring.done(e, t)
            t = tt(V, TMP[ip][:, :], TMP[ip][:, :], bank[:, :], ALU.mult, t, t2)
            banks.put(bank, t)
            t_mg = tt(V, ACC[:, c, :], ACC[:, c, :], TMP[ip][:, :], ALU.add, t, t3)
            ld_free[ip] = t_mg
        phase(at_)
        MGh = here("MGh", [128, 8, 512], FR)
        MGl = here("MGl", [128, 8, 512], FR)
        V.wait(T.now())
        A.wait(T.now())
        sp = Splits()
        for c in range(8):
            sp.add(MGh[:, c, :], MGl[:, c, :], ACC[:, c, :], t_mg)
        t_mgs = sp.flush()

        class Squares:

            def __init__(self):
                self.bank = banks.get(T)
                self.free = [None, None]
                self.pend = None
                self.v = V.now()

            def flush(self):
                if self.pend is not None:
                    i, t = self.pend
                    T.wait(t)
                    self.t = self.free[i % 2] = T.inc(mm(self.bank[:, :], K("o1024"), TMP[2 + i % 2][:, :],
                                                         start=(i == 0), stop=(i == 3)))
                    self.pend = None

            def add(self, k, t):
                x, i = XT[:, k, :], k // 2
                if k % 2 == 0:
                    self.a = av(TMP[2 + i % 2][:, :], x, ACT.Square, t, self.free[i % 2])
                else:
                    t = tt(V, SQ[:, :], x, x, ALU.mult, t, self.v)
                    t = self.v = tt(V, TMP[2 + i % 2][:, :], TMP[2 + i % 2][:, :], SQ[:, :], ALU.add, t, self.a)
                    self.flush()
                    self.pend = (i, t)

            def rsqrt(self, eps):
                self.flush()
                t, t0 = rsqrt(RA[:, :], self.bank[:, :], eps, self.t)
                banks.put(self.bank, t0)
                return t

        def layer_norm(gname, bname, sums, also=None):
            bank, t = sums
            sq = Squares()
            for k in range(8):
                t_c = tt(V, XT[:, k, :], XT[:, k, :], bank[:, :], ALU.subtract, t)
                sq.add(k, t_c)
            banks.put(bank, t_c)
            t = sq.rsqrt("eps5")
            out, t2 = [], [None] * 8
            if also:
                for k in range(8):
                    t2[k] = also(k, tt(V, XT[:, k, :], XT[:, k, :], RA[:, :], ALU.mult, t))
            for k in range(8):
                if not also:
                    t2[k] = tt(V, XT[:, k, :], XT[:, k, :], RA[:, :], ALU.mult, t)
                out.append(av(XT[:, k, :], XT[:, k, :], ACT.Identity, t2[k], scale=C(gname, k), bias=C(bname, k)))
            return out

        class Mean:

            def add(self, k, t):
                if k == 0:
                    self.first = t
                else:
                    self.t = tt(V, SQ[:, :], XT[:, 0, :] if k == 1 else SQ[:, :], XT[:, k, :], ALU.add,
                                t, self.first if k == 1 else self.t)

            def sums(self):
                return rows_sum(SQ[:, :], "o1024", self.t)

        V.wait(G.now(), T.now())
        mean = Mean()
        t_al = [ts(V, XT[:, c, :], XT[:, c, :], ALPHA, None, ALU.mult, None, tx) for c in range(8)]
        for c in range(8):
            e = ring.get("wo", c)
            bank = banks.get(T)
            t = feature(bank[:, :], e, MGh, MGl, xt=t_mgs)
            ring.done(e, t)
            t_r = stt(XT[:, c, :], bank[:, :], mod[:, 16 + c, 0:1], XT[:, c, :], ALU.mult, ALU.add, t, t_al[c], t_mod)
            banks.put(bank, t_r)
            mean.add(c, t_r)
        phase(at_ + 8192)
        HF = here("HF", [128, 8, 512])
        HF_END = cur[0]
        hg_, hb_ = sm[:, 0:8], sm[:, 8:16]
        t = tt(V, hg_, C("ln1_g", 0, 8), mod[:, 32:40, 0], ALU.mult, t_mod, V.now())
        t = tt(V, hb_, C("ln1_b", 0, 8), mod[:, 32:40, 0], ALU.mult, t_mod, t)
        t_hb = tt(V, hb_, hb_, mod[:, 24:32, 0], ALU.add, t)
        sp = Splits()

        def to_h2(k, t):
            t = ts(V, HF[:, k, :], XT[:, k, :], hg_[:, k:k + 1], hb_[:, k:k + 1], ALU.mult, ALU.add, t, t_hb)
            sp.add(HTh[:, k, :], HTl[:, k, :], HF[:, k, :], t)
            return t

        t_xs = layer_norm("ln1_g", "ln1_b", mean.sums(), to_h2)
        t_h2s = sp.flush()
        t_h2 = t_h2s[7]

        phase(W1)
        HR = here("HR", [128, 4, 1024])
        rt = here("rt", [128, 4900])
        LGT = here("LGT", [36, 512])
        assert cur[0] <= at_ + 8192
        ro = [0]

        def rc(*shape):
            w = 1
            for x in shape:
                w *= x
            v = rt[:, ro[0]:ro[0] + w]
            ro[0] += w
            assert ro[0] <= 4900
            if len(shape) == 2:
                return v.rearrange("p (a b) -> p a b", a=shape[0])
            if len(shape) == 3:
                return v.rearrange("p (a b c) -> p a b c", a=shape[0], b=shape[1])
            return v

        lg, g8, gm, m32, lm, vm = rc(4, 36), rc(4, 8), rc(4, 8), rc(4, 32), rc(4, 32), rc(4, 8)
        OH, ohs, ga, ex, wt = rc(4, 2, 32), rc(4, 32), rc(4, 1), rc(4, 2), rc(4, 8)
        cnt, ove, send, sst, t32, eid, rk = rc(32), rc(32), rc(32), rc(32), rc(32), rc(NOV + 1), rc(4, 32)
        X, Y_, Q, R1, BL = rc(4, 2), rc(4, 2), rc(4, 2), rc(4, 2), rc(4, 2)
        PRD = rc(4, 2, 32)
        LE = rc(NOV, 32)
        SBA = rc(8, 128)
        SBB = rc(8, 2, NBLK)
        fl = rc(2, NBLK)
        em = rc(2, NBLK)

        def vi_(ins):
            return V.inc(ins)

        def reduce(out, a, op, *waits):
            V.wait(*waits)
            return V.inc(nc.vector.tensor_reduce(out, a, AX.X, op))

        V.wait(T.now(), A.now())
        V.inc(nc.vector.memset(g8, -1e30))
        t0 = V.inc(nc.vector.memset(t32, 0.0))
        e = ring.get("wr", 0)
        bank = banks.get(T)
        t = prod(bank[0:36, :], [(e[0][:, k, :], e[1][:, k, :], HTh[:, k, :], HTl[:, k, :]) for k in range(8)],
                 e[2], xt=t_h2s)
        ring.done(e, t)
        t = cp(A, LGT[:, :], bank[0:36, :], t)
        banks.put(bank, t)
        bank = banks.get(T)
        T.wait(t)
        for i in range(4):
            ins = nc.tensor.transpose(bank[:, i * 36:(i + 1) * 36], LGT[:, i * 128:(i + 1) * 128], K("ident", 36, 36))
        t = T.inc(ins)
        t_lg = tt(V, lg, bank[:, 0:144].rearrange("p (t n) -> p t n", t=4),
                  pr[:, PR_RB:PR_RB + 36].unsqueeze(1).to_broadcast([128, 4, 36]), ALU.add, t, t0)
        banks.put(bank, t_lg)

        def rows_of_h(i, q):
            _t, t = turn(A, HR[:, i, q * 512:(q + 1) * 512].rearrange("p (t n) -> p t n", t=4),
                         [HF[:, 4 * q + k, i * 128:(i + 1) * 128] for k in range(4)], t_h2)
            return t

        for i in range(4):
            for q in range(2):
                t = rows_of_h(i, q)
            A.wait(t)
            t_hd = d_h.inc(nc.scalar.dma_start(H2[i * 128:(i + 1) * 128, :], HR[:, i, :]))
        t = cp(V, g8[:, :, 0:4], lg[:, :, 0:4], t_lg)
        V.wait(t)
        for i in range(4):
            t = vi_(nc.vector.max(gm[:, i, :], g8[:, i, :]))
        V.wait(t)
        for i in range(4):
            t = vi_(nc.vector.max_index(gi[:, i, :], gm[:, i, :], g8[:, i, :]))
        t = cp(V, ga, gi[:, :, 0:1], t)
        t = tt(V, m32, K("iotag", 32).unsqueeze(1).to_broadcast([128, 4, 32]), ga.to_broadcast([128, 4, 32]),
               ALU.is_equal, t)
        t1 = tt(V, lm, lg[:, :, 4:36], m32, ALU.mult, t)
        t2 = ts(V, m32, m32, 1e30, -1e30, ALU.mult, ALU.add, t1)
        t = tt(V, lm, lm, m32, ALU.add, t2)
        V.wait(t)
        for i in range(4):
            t = vi_(nc.vector.max(vm[:, i, :], lm[:, i, :]))
        V.wait(t)
        for i in range(4):
            t = vi_(nc.vector.max_index(vi[:, i, :], vm[:, i, :], lm[:, i, :]))
        t = cp(V, ex, vi[:, :, 0:2], t)
        for k in range(2):
            t1 = tt(V, OH[:, :, k, :], K("iota", 32).unsqueeze(1).to_broadcast([128, 4, 32]),
                    ex[:, :, k:k + 1].to_broadcast([128, 4, 32]), ALU.is_equal, t)
        t = tt(V, ohs, OH[:, :, 0, :], OH[:, :, 1, :], ALU.add, t1)
        bank = banks.get(T)
        T.wait(t)
        for i in range(4):
            for j in range(i + 1):
                mm(bank[:, i * 32:(i + 1) * 32], K("sU") if j == i else K("ones"), ohs[:, j, :],
                   start=(j == 0), stop=(j == i))
        for j in range(4):
            ins = mm(bank[:, 128:160], K("ones"), ohs[:, j, :], start=(j == 0), stop=(j == 3))
        t_cnt = T.inc(ins)
        t = tt(V, wt[:, :, 0:4], lg[:, :, 0:4], gm[:, :, 0:1].to_broadcast([128, 4, 4]), ALU.subtract)
        t = tt(V, wt[:, :, 4:5], vm[:, :, 1:2], vm[:, :, 0:1], ALU.subtract, t)
        t_w = av(wt[:, :, 0:5], wt[:, :, 0:5], ACT.Exp, t)
        t0 = cp(V, cnt, bank[:, 128:160], t_cnt)
        t1 = cp(V, rk, bank[:, 0:128].rearrange("p (t n) -> p t n", t=4), t_cnt)
        banks.put(bank, t1)
        t = ts(V, ove, cnt, float(CAP), None, ALU.is_gt, None, t1)
        for b in range(2, OVB + 1):
            t = stt(ove, cnt, float(CAP * b), ove, ALU.is_gt, ALU.add, t)
        V.wait(t)
        t = vi_(nc.vector.tensor_tensor_scan(send, ove, t32, 0.0, ALU.add, ALU.add))
        t_ss = tt(V, sst, send, ove, ALU.subtract, t)
        for k in range(2):
            t = tt(V, PRD[:, :, k, :], rk, OH[:, :, k, :], ALU.mult, t_ss)
        t = reduce(X, PRD, ALU.add, t)
        for k in range(2):
            t = tt(V, PRD[:, :, k, :], sst.unsqueeze(1).to_broadcast([128, 4, 32]), OH[:, :, k, :], ALU.mult, t)
        t = reduce(Y_, PRD, ALU.add, t)
        t = ts(V, Q, X, float(CAP), None, ALU.is_ge, None, t)
        for b in range(2, OVB + 1):
            t = stt(Q, X, float(CAP * b), Q, ALU.is_ge, ALU.add, t)
        t_r1 = stt(R1, Q, -float(CAP), X, ALU.mult, ALU.add, t)
        t = stt(Y_, Y_, 31.0, Q, ALU.add, ALU.add, t)
        t = tt(V, Y_, Y_, ex, ALU.subtract, t)
        t = ts(V, X, Q, 0.0, None, ALU.is_gt, None, t, t_r1)
        t = tt(V, Y_, Y_, X, ALU.mult, t)
        t = tt(V, BL, Y_, ex, ALU.add, t)
        flat = lambda a: a.rearrange("p a b -> p (a b)")
        t1 = tt(V, SBA, K("iota").unsqueeze(1).to_broadcast([128, 8, 128]), bc(flat(R1), 128), ALU.is_equal, t_r1)
        t = tt(V, SBB[:, :, 0, :], K("iota", NBLK).unsqueeze(1).to_broadcast([128, 8, NBLK]), bc(flat(BL), NBLK),
               ALU.is_equal, t)
        t = tt(V, SBB[:, :, 1, :], SBB[:, :, 0, :], bc(K("aid", 8), NBLK), ALU.mult, t)
        t = tt(V, SBB[:, :, 0, :], SBB[:, :, 0, :], bc(K("tok", 8), NBLK), ALU.mult, t)
        bank = banks.get(T)
        T.wait(t)
        for n in range(8):
            ins = mm(bank[:, 0:2 * NBLK], SBA[:, n, :], SBB[:, n, :, :].rearrange("p a b -> p (a b)"), start=(n == 0),
                     stop=(n == 7))
        t = T.inc(ins)
        v = bank[:, 0:2 * NBLK].rearrange("p (a n) -> p a n", a=2)
        t = ts(V, em, v, 0.0, K("slot", 1), ALU.is_equal, ALU.mult, t)
        t = stt(fl, v, -1.0, em, ALU.add, ALU.add, t)
        banks.put(bank, t)
        t_ix = cp(V, ix[:, :, :], fl, t)
        t = tt(V, LE, send.unsqueeze(1).to_broadcast([128, NOV, 32]), bc(K("iota", NOV), 32), ALU.is_le, t_ss)
        t = reduce(eid[:, 0:NOV], LE, ALU.add, t)
        t = ts(V, eid[:, 0:NOV], eid[:, 0:NOV], 31.0, None, ALU.min, None, t)
        t = cp(V, eid[:, NOV:NOV + 1], send[:, 31:32], t)
        t_eid = cp(V, eidi[:, :], eid, t)
        t = reduce(wt[:, :, 5:6], wt[:, :, 0:4], ALU.add, t_w)
        t1 = ts(V, wt[:, :, 6:7], wt[:, :, 4:5], 1.0, None, ALU.add, None, t_w)
        t = tt(V, wt[:, :, 6:7], wt[:, :, 6:7], wt[:, :, 5:6], ALU.mult, t, t1)
        t = recip(wk[:, :, 0:1], wt[:, :, 6:7], t)
        t = tt(V, wk[:, :, 1:2], wk[:, :, 0:1], wt[:, :, 4:5], ALU.mult, t)
        t_free = (T.now(), A.now())
        V.wait(t_ix)

        phase(W1)
        XG = [here(f"XG{i}", [128, 1024]) for i in range(2)]
        XGh = [here(f"XGh{i}", [128, 8, 128], FR) for i in range(2)]
        XGl = [here(f"XGl{i}", [128, 8, 128], FR) for i in range(2)]
        YO = [here(f"YO{i}", [128, 1024]) for i in range(2)]
        GT = [here(f"GT{i}", [128, 512]) for i in range(2)]
        GTh = [here(f"GTh{i}", [128, 4, 128], FR) for i in range(2)]
        GTl = [here(f"GTl{i}", [128, 4, 128], FR) for i in range(2)]
        d_gg = [Dma(sem(f"d_gg{i}")) for i in range(2)]

        def experts(T, V, A, G, ring, banks, d_gg, d_s, blocks, before):
            free, got, xt, act_ = {}, {}, {}, {}

            def w(name, i):
                return free.get((name, i))

            def gather(b):
                i = b % 2
                G.wait(w("xg", i), *before)
                got[b] = d_gg[i].inc(nc.gpsimd.indirect_dma_start(
                    XG[i][:, :], None, H2, bass.IndirectOffsetOnAxis(ap=ix[:, 0, b:b + 1], axis=0),
                    bounds_check=511, oob_is_err=False))

            def turn_in(b):
                i = b % 2
                for q in range(2):
                    bank = banks.get(T)
                    T.wait(got[b])
                    for k in range(4):
                        ins = nc.tensor.transpose(bank[:, k * 128:(k + 1) * 128],
                                                  XG[i][:, (4 * q + k) * 128:(4 * q + k + 1) * 128], K("ident"))
                    t = T.inc(ins)
                    v = bank[:, :].rearrange("p (k n) -> p k n", k=4)
                    h_, l_ = XGh[i][:, 4 * q:4 * q + 4, :], XGl[i][:, 4 * q:4 * q + 4, :]
                    A.wait(t, w("xgt", i))
                    t1 = A.inc(act(h_, v, ACT.Copy))
                    V.wait(t1)
                    t2 = V.inc(nc.vector.tensor_tensor(l_, v, h_.bitcast(F32), ALU.subtract))
                    banks.put(bank, t2)
                free[("xg", i)] = t
                xt[b] = t2

            def first(b, e):
                i = b % 2
                bk = []
                T.wait(xt[b])
                for name in ("eg", "eu"):
                    bank = banks.get(T)
                    for a in range(4):
                        en = ring.get(name, e, a)
                        T.wait(en[2])
                        for kk in range(2):
                            k = 2 * a + kk
                            mm(bank[:, :], XGh[i][:, k, :], en[0][:, kk, :], start=(k == 0), stop=False)
                            mm(bank[:, :], XGl[i][:, k, :], en[0][:, kk, :], start=False, stop=False)
                            ins = mm(bank[:, :], XGh[i][:, k, :], en[1][:, kk, :], start=False, stop=(k == 7))
                        t = T.inc(ins)
                        ring.done(en, t)
                    bk.append((bank, t))
                free[("xgt", i)] = t
                A.wait(bk[0][1], w("gt", i))
                t = A.inc(act(GT[i][:, :], bk[0][0][:, :], ACT.Silu))
                banks.put(bk[0][0], t)
                V.wait(t, bk[1][1])
                act_[b] = V.inc(nc.vector.tensor_tensor(GT[i][:, :], GT[i][:, :], bk[1][0][:, :], ALU.mult))
                banks.put(bk[1][0], act_[b])

            def turn_mid(b):
                i = b % 2
                bank = banks.get(T)
                T.wait(act_[b])
                for k in range(4):
                    ins = nc.tensor.transpose(bank[:, k * 128:(k + 1) * 128], GT[i][:, k * 128:(k + 1) * 128],
                                              K("ident"))
                t = T.inc(ins)
                free[("gt", i)] = t
                v = bank[:, :].rearrange("p (k n) -> p k n", k=4)
                A.wait(t, w("gtt", i))
                t = A.inc(act(GTh[i][:, :, :], v, ACT.Copy))
                V.wait(t)
                t = V.inc(nc.vector.tensor_tensor(GTl[i][:, :, :], v, GTh[i][:, :, :].bitcast(F32), ALU.subtract))
                banks.put(bank, t)
                act_[b] = t

            def last(b, e):
                i = b % 2
                T.wait(act_[b])
                bs = [banks.get(T), banks.get(T)]
                for k in range(4):
                    en = ring.get("ed", e, k)
                    T.wait(en[2])
                    for n in range(2):
                        ns = slice(n * 512, (n + 1) * 512)
                        mm(bs[n][:, :], GTh[i][:, k, :], en[0][:, 0, ns], start=(k == 0), stop=False)
                        mm(bs[n][:, :], GTl[i][:, k, :], en[0][:, 0, ns], start=False, stop=False)
                        ins = mm(bs[n][:, :], GTh[i][:, k, :], en[1][:, 0, ns], start=False, stop=(k == 3))
                    t = T.inc(ins)
                    ring.done(en, t)
                free[("gtt", i)] = t
                for n in range(2):
                    A.wait(t, w("yo", i))
                    t3 = A.inc(act(YO[i][:, n * 512:(n + 1) * 512], bs[n][:, :], ACT.Copy))
                    banks.put(bs[n], t3)
                G.wait(t3, d_s.now())
                free[("yo", i)] = d_s.inc(nc.gpsimd.indirect_dma_start(
                    YD, bass.IndirectOffsetOnAxis(ap=ix[:, 1, b:b + 1], axis=0), YO[i][:, :], None,
                    bounds_check=1023, oob_is_err=False))

            n = len(blocks)
            gather(blocks[0][0])
            if n > 1:
                gather(blocks[1][0])
            turn_in(blocks[0][0])
            for j, (b, e) in enumerate(blocks):
                first(b, e)
                if j + 1 < n:
                    turn_in(blocks[j + 1][0])
                if j + 2 < n:
                    gather(blocks[j + 2][0])
                if j:
                    last(*blocks[j - 1])
                turn_mid(b)
            last(*blocks[-1])

        A.wait(V.now(), G.now())
        V.wait(A.now(), G.now(), T.now(), t_hd)
        for x in XG:
            t_z = V.inc(nc.vector.memset(x[:, :], 0.0))
        for k in range(8):
            ts(V, XT[:, k, :], XT[:, k, :], ALPHA, None, ALU.mult, None, t_xs[7])
        for E_ in (T, V, A, G, S):
            E_.wait(t_eid)
        nov = nc.values_load(eidi[0:1, NOV:NOV + 1], min_val=0, max_val=NOV)
        ring.stop = "f11"
        more = here("more", [128, 5, 1024])
        S.wait(T.now(), V.now(), A.now(), t_hd)
        ring.lend([more[:, i, :] for i in range(5)], [Dma(sem(f"s_more{i}")) for i in range(5)], None)
        experts(T, V, A, G, ring, banks, d_gg, d_s, [(e, e) for e in range(32)], (t_ix, t_hd, *t_free, t_z))

        everything = (T.now(), V.now(), A.now(), G.now(), d_s.now(), t_eid)
        with nc.If(nov > 0):
            T2, V2, A2, G2, S2 = (Eng(e_.e, sem(f"o_{n}")) for n, e_ in enumerate((T, V, A, G, S)))
            for E_ in (T2, V2, A2, G2, S2):
                E_.wait(*everything)
            loaded = {}

            def theirs(key):
                j = key[1]
                if j not in loaded:
                    loaded[j] = nc.sync.value_load(eidi[0:1, j:j + 1], min_val=0, max_val=31)
                v = I[key[0]].rearrange("e (k p) n -> e p k n", p=128)[bass.ds(loaded[j], 1)]
                v = v.rearrange("e p k n -> p (e k) n")
                if key[0] == "ed":
                    return v[:, key[2]:key[2] + 1, :]
                return v[:, 2 * key[2]:2 * key[2] + 2, :]

            ring2 = Ring([] if dry else plans[1], theirs, raw, HLB, S2, A2, V2, G2,
                         [Dma(sem(f"o_r{i}")) for i in range(NRAW)], dry)
            banks2 = Banks([b for b, _t in banks.free])
            ds2 = Dma(sem("o_s"))
            experts(T2, V2, A2, G2, ring2, banks2, [Dma(sem(f"o_g{i}")) for i in range(2)], ds2,
                    [(32 + j, j) for j in range(NOV)], ())
            for E_ in (T2, V2, A2, G2, S2):
                E_.wait(T2.now(), V2.now(), A2.now(), G2.now(), ds2.now())
        nc.end_ifs()
        ring.take_back()
        ring.stop = None
        ring.advance()

        YV = YD.rearrange("(t p k) n -> t p k n", p=128, k=2)
        phase(W1)
        YI = here("YI", [128, 4, 2, 1024])
        YL = here("YL", [128, 4, 1024])
        V.wait(A.now(), G.now(), T.now())
        G.wait(d_s.now())
        G.wait(T.now(), V.now(), A.now())
        A.wait(T.now(), G.now(), t_hd)
        t_ld = [Dma(sem(f"d_yy{i}")).inc(nc.gpsimd.dma_start(YI[:, i, :, :], YV[i])) for i in range(4)]
        for i in range(4):
            t1 = av(YL[:, i, :], YI[:, i, 0, :], ACT.Copy, t_ld[i], V.now() if i == 0 else None, scale=wk[:, i, 0:1])
            t_yl = stt(YL[:, i, :], YI[:, i, 1, :], wk[:, i, 1:2], YL[:, i, :], ALU.mult, ALU.add, t1)
        for k in range(8):
            bank = banks.get(T)
            T.wait(t_yl)
            for i in range(4):
                ins = nc.tensor.transpose(bank[:, i * 128:(i + 1) * 128], YL[:, i, k * 128:(k + 1) * 128], K("ident"))
            t = T.inc(ins)
            t_r = stt(XT[:, k, :], bank[:, :], mod[:, 40 + k, 0:1], XT[:, k, :], ALU.mult, ALU.add, t)
            banks.put(bank, t_r)
            mean.add(k, t_r)
        t_xs = layer_norm("ln2_g", "ln2_b", mean.sums())

        def rms_norm(name, sq):
            t = sq.rsqrt("eps6")
            V.wait(T.now())
            A.wait(T.now())
            sp = Splits()
            for k in range(8):
                t2 = stt(TMP[4 + k % 2][:, :], XT[:, k, :], C(name, k), RA[:, :], ALU.mult, ALU.mult, t,
                         sp.toks[k - 2] if k > 1 else None)
                sp.add(HTh[:, k, :], HTl[:, k, :], TMP[4 + k % 2][:, :], t2)
            return sp.flush()

        def ffn(name, w1, w3, w2, sq, last=None):
            t_n = rms_norm(name, sq)
            phase(W1)
            FAh = here(name + "FAh", [128, 11, 512], FR)
            FAl = here(name + "FAl", [128, 11, 512], FR)
            tfree = [None, None]
            V.wait(A.now(), T.now(), G.now())
            A.wait(T.now(), G.now())
            for half in range(2):
                t_d = T.now() if half else None
                t_f = []
                for f in range(11):
                    bk = []
                    for w in (w1, w3):
                        e = ring.get(w, 11 * half + f)
                        bank = banks.get(T)
                        t = feature(bank[:, :], e, HTh, HTl, xt=t_n)
                        ring.done(e, t)
                        bk.append((bank, t))
                    i = f % 2
                    t = av(TMP[i][:, :], bk[0][0][:, :], ACT.Silu, bk[0][1], tfree[i])
                    banks.put(bk[0][0], t)
                    t = tt(V, TMP[i][:, :], TMP[i][:, :], bk[1][0][:, :], ALU.mult, t, bk[1][1])
                    banks.put(bk[1][0], t)
                    tfree[i] = split(FAh[:, f, :], FAl[:, f, :], TMP[i][:, :], t, t_d)
                    t_f.append(tfree[i])
                if half and last is None:
                    sq = Squares()
                for c in range(8):
                    bank = banks.get(T)
                    e = ring.get(w2, c, 1408 * half)
                    t = feature(bank[:, :], e, FAh, FAl, xt=t_f, n=8, stop=False)
                    ring.done(e, t)
                    e = ring.get(w2, c, 1408 * half + 1024)
                    t = feature(bank[:, :], e, FAh, FAl, xt=t_f[8:], k0=8, n=3, start=False)
                    ring.done(e, t)
                    t_o = stt(XT[:, c, :], bank[:, :], 0.5, XT[:, c, :], ALU.mult, ALU.add, t)
                    banks.put(bank, t_o)
                    if half and last is None:
                        sq.add(c, t_o)
                    elif half:
                        last(c, t_o)
            return sq

        sq = Squares()
        for k in range(8):
            sq.add(k, t_xs[k])
        sq = ffn("n1", "f11", "f13", "f12", sq)
        t_n = rms_norm("nm", sq)
        fr = (T.now(), V.now(), G.now(), A.now())
        V.wait(T.now())
        A.wait(T.now())
        G.wait(*fr)
        phase(W1)
        HV = here("HV", [128, 4, 512])
        MX = here("MX", [128, 8, 512])
        RST = here("RST", [128, 512])
        at_ = cur[0]
        QT = here("QT", [128, 4, 512])
        KT = here("KT", [128, 4, 512])
        VV = here("VV", [128, 4, 512])
        AL = here("AL", [128, 1280])
        CS = here("CS", [128, 2, 512])
        PT = [here(f"PT{i}", [128, 4, 128]) for i in range(2)]
        ms_ = [here(f"ms{i}", [128, 8]) for i in range(3)]
        PB = [TMP[0], TMP[1], here("PB2", [128, 512])]
        al_at = [0, 128, 384, 768]
        t_tab = d_t.inc(nc.gpsimd.dma_start(CS[:, :, :], I["cs"]))
        t_tab = d_t.inc(nc.gpsimd.dma_start(AL[:, :], I["al"]))
        t_tab = d_t.inc(nc.gpsimd.dma_start(RST[:, :], I["rst"]))

        def qk():
            f_n = [None] * 2
            st = {}
            for n in range(10):
                if n < 8:
                    e = ring.get("w2in", n)
                    bank = banks.get(T)
                    t = feature(bank[:, :], e, HTh, HTl, xt=t_n)
                    ring.done(e, t)
                    t_s = av(TMP[n % 2][:, :], bank[:, :], ACT.Square, t, st[n - 2][2] if n > 1 else None)
                    st[n] = [bank, t_s, None, None]
                if 0 <= n - 1 < 8:
                    m = n - 1
                    b2, t = rows_sum(TMP[m % 2][:, :], "hb", st[m][1])
                    st[m][2] = t
                    t, t0 = rsqrt(RA[:, :], b2[:, :], "eps6", t, V.now())
                    banks.put(b2, t0)
                    t = stt(TMP[2 + m % 2][:, :], st[m][0][:, :], C("qn" if m < 4 else "kn", 0), RA[:, :], ALU.mult,
                            ALU.mult, t, f_n[m % 2])
                    banks.put(st[m][0], t)
                    st[m][3] = t
                if 0 <= n - 2 < 8:
                    m = n - 2
                    b3_, t = rows_sum(TMP[2 + m % 2][:, :], "psw", st[m][3])
                    nm_ = TMP[2 + m % 2][:, :]
                    t1 = tt(G, TMP[4][:, :], nm_, CS[:, 0, :], ALU.mult, st[m][3], t_tab, G.now())
                    t2 = tt(V, nm_, b3_[:, :], CS[:, 1, :], ALU.mult, t, t1, t_tab)
                    banks.put(b3_, t2)
                    f_n[m % 2] = tt(G, (QT if m < 4 else KT)[:, m % 4, :], TMP[4][:, :], nm_, ALU.add, t1, t2)
                yield f_n[1]

        def vi():
            for nm, dst in (("w2v", VV), ("w2i", HV)):
                for c in range(2):
                    es = [ring.get(nm, c, a) for a in range(2)]
                    for i in range(4):
                        cs = slice(i * 128, (i + 1) * 128)
                        bank = banks.get(T)
                        t = prod(bank[:, 0:256], [(HTh[:, k, cs], HTl[:, k, cs], es[k // 4][0][:, k % 4, :],
                                                   es[k // 4][1][:, k % 4, :]) for k in range(8)], es[0][2], es[1][2])
                        if i == 3:
                            for e in es:
                                ring.done(e, t)
                        t_v = cp(A, dst[:, i, c * 256:(c + 1) * 256], bank[:, 0:256], t)
                        banks.put(bank, t_v)
                        if i % 2:
                            yield t_v

        turns = [qk(), vi()]
        t_qk = t_v = None
        for i in range(10):
            t_qk = next(turns[0])
            if i in (2, 5):
                t_v = next(turns[1])
                t_v = next(turns[1])
        t_v = [t_v] + list(turns[1])
        t_v = t_v[-1]

        lw = sm[:, 16:40]
        t = tt(V, lw[:, 0:4], C("lb0", 0, 4), C("lb1", 0, 4), ALU.max)
        tt(V, lw[:, 4:8], C("lb0", 0, 4), lw[:, 0:4], ALU.subtract, t)
        t = tt(V, lw[:, 8:12], C("lb1", 0, 4), lw[:, 0:4], ALU.subtract, t)
        t = av(lw[:, 4:12], lw[:, 4:12], ACT.Exp, t)
        t = tt(V, lw[:, 0:4], lw[:, 4:8], lw[:, 8:12], ALU.add, t)
        t = recip(lw[:, 0:4], lw[:, 0:4], t)
        t = tt(V, lw[:, 12:16], lw[:, 4:8], lw[:, 0:4], ALU.mult, t)
        t_lb = ts(V, lw[:, 16:20], lw[:, 12:16], -1.0, 1.0, ALU.mult, ALU.add, t)
        phase(DEC)
        GG, EX, ATT, HGB = (here("hg" + n_, [128, 512])[:, :] for n_ in "abcd")
        assert cur[0] <= DEC_END
        QD, KD, KW, FF = TMP[2][:, :], TMP[3][:, :], TMP[4][:, :], TMP[5][:, :]
        KWT = RA[:, :].rearrange("p (t n) -> p t n", t=4)
        REC = SQ[:, :]
        SS = [CS[:, i // 4, (i % 4) * 128:(i % 4 + 1) * 128] for i in range(8)]
        V.wait(t_qk, t_v)
        A.wait(V.now(), t_qk)
        V.inc(nc.vector.memset(ATT, 0.0))
        t_at0 = V.inc(nc.vector.memset(SS[0], 0.0))
        V.wait(t_at0)
        hgm = K("hgm").bitcast(U32)
        t_mx2 = None

        def recurrence():
            nonlocal t_mx2
            t_o = t_s = t_mm = None
            for h in range(4):
                bks = []
                e = ring.get("w2in", 12 + h)
                bf = banks.get(T)
                t_bf = feature(bf[:, :], e, HTh, HTl)
                ring.done(e, t_bf)
                t = av(FF, bf[:, :], ACT.Sigmoid, t_bf, V.now())
                banks.put(bf, t)
                t_f = ts(V, FF, FF, lw[:, 16 + h:17 + h], lw[:, 12 + h:13 + h], ALU.mult, ALU.add, t, t_lb)
                yield
                t = av(GG, FF, ACT.Ln, t_f)
                t_k = ts(V, FF, FF, -1.0, 1.0, ALU.mult, ALU.add, t)
                V.wait(t, t_tab, t_k)
                t_g = V.inc(nc.vector.tensor_tensor_scan(GG, RST[:, :], GG, 0.0, ALU.mult, ALU.add))
                t_ex = av(EX, GG, ACT.Exp, t_g, t_mx2)
                e = ring.get("w2in", 8 + h)
                bq = banks.get(T)
                t_bq = feature(bq[:, :], e, HTh, HTl)
                ring.done(e, t_bq)
                yield
                t_qd = tt(V, QD, bq[:, :], EX, ALU.mult, t_ex, t_bq, t_o)
                banks.put(bq, t_qd)
                ev = EX.rearrange("p (c n) -> p c n", c=8)
                dc = sm[:, 40:48]
                t_dc = cp(V, dc, ev[:, :, 63], t_ex, t_s)
                t = av(KD, GG, ACT.Exp, t_g, t_mm, scale=-1.0)
                t_kd = tt(V, KD, KD, FF, ALU.mult, t, t_k)
                gv = GG.rearrange("p (c n) -> p c n", c=8)
                t = tt(V, KW.rearrange("p (c n) -> p c n", c=8), gv[:, :, 63:64].to_broadcast([128, 8, 64]), gv,
                       ALU.subtract, t_kd)
                t = av(KW, KW, ACT.Exp, t)
                t_kw = tt(V, KW, KW, FF, ALU.mult, t)
                e = ring.get("w2in", 16 + h)
                bg = banks.get(T)
                t_bg = feature(bg[:, :], e, HTh, HTl)
                ring.done(e, t_bg)
                t_hg = av(HGB, bg[:, :], ACT.Silu, t_bg, t_mx2)
                banks.put(bg, t_hg)
                yield
                bank = banks.get(T)
                T.wait(t_qd, t_kd)
                for c in range(4):
                    cs = slice(c * 128, (c + 1) * 128)
                    ins = mm(bank[:, cs], KD[:, cs], QD[:, cs], start=True, stop=True)
                t_mm = T.inc(ins)
                V.wait(t_mm, t_o)
                t_att = V.inc(nc.vector.copy_predicated(ATT.rearrange("p (c n) -> p c n", c=4),
                                                        hgm.unsqueeze(1).to_broadcast([128, 4, 128]),
                                                        bank[:, :].rearrange("p (c n) -> p c n", c=4)))
                banks.put(bank, t_att)
                _t, t_kwt = turn(A, KWT, [KW[:, c * 128:(c + 1) * 128] for c in range(4)], t_kw)
                t_mm = _t
                yield
                T.wait(t_kwt)
                b4 = [banks.get(T), banks.get(T)]
                for c in range(8):
                    pp = slice(64 * (c % 2), 64 * (c % 2) + 64)
                    t_u = T.inc(mm(b4[c % 2][:, (c // 2) * 128:(c // 2 + 1) * 128], KWT[pp, c // 2, :],
                                   HV[pp, c // 2, h * 128:(h + 1) * 128], start=True, stop=True))
                t_s = t_at0
                tss = [t_at0]
                for c in range(7):
                    t_s = stt(SS[c + 1], SS[c], dc[:, c:c + 1], b4[c % 2][:, (c // 2) * 128:(c // 2 + 1) * 128],
                              ALU.mult, ALU.add, t_u, t_s, t_dc)
                    tss.append(t_s)
                for b_ in b4:
                    banks.put(b_, t_s)
                yield
                bo = banks.get(T)
                T.wait(t_att)
                for c in range(4):
                    for j in range(2):
                        cj = 2 * c + j
                        cs = slice(cj * 64, (cj + 1) * 64)
                        T.wait(tss[cj])
                        mm(bo[:, cs], HV[:, c, h * 128:(h + 1) * 128], ATT[:, cs], start=True, stop=False)
                        ins = mm(bo[:, cs], SS[cj], QD[:, cs], start=False, stop=True)
                t_o = T.inc(ins)
                t = av(REC, bo[:, :], ACT.Square, t_o)
                yield
                b5, t = rows_sum(REC, "o128", t)
                t, t0 = rsqrt(EX, b5[:, :], "eps6", t, V.now())
                banks.put(b5, t0)
                t = stt(EX, bo[:, :], C("hn", 0), EX, ALU.mult, ALU.mult, t)
                banks.put(bo, t)
                t_mx2 = tt(V, MX[:, 4 + h, :], EX, HGB, ALU.mult, t, t_hg)
                yield

        rec = recurrence()
        f_pb, f_pt = [None] * 3, [None] * 2
        st = {}
        t_mx = None
        for n in range(34):
            if n < 32:
                h, qt, i = n // 4, n % 4, n % 3
                ps = slice(64 * (h % 2), 64 * (h % 2) + 64)
                nk = (qt + 1) * 128
                bank = banks.get(T)
                t = chain(bank[:, 0:nk], [(QT[ps, h // 2, qt * 128:(qt + 1) * 128], KT[ps, h // 2, 0:nk])], t_qk)
                t = stt(PB[i][:, 0:nk], bank[:, 0:nk], 0.125, AL[:, al_at[qt]:al_at[qt] + nk], ALU.mult, ALU.add, t,
                        f_pb[i], t_tab)
                banks.put(bank, t)
                V.wait(t)
                t = V.inc(nc.vector.tensor_reduce(ms_[i][:, 0:1], PB[i][:, 0:nk], AX.X, ALU.max))
                t = ts(V, ms_[i][:, 1:2], ms_[i][:, 0:1], -1.0, None, ALU.mult, None, t)
                A.wait(t)
                t_e = A.inc(act(PB[i][:, 0:nk], PB[i][:, 0:nk], ACT.Exp, bias=ms_[i][:, 1:2], accum_out=ms_[i][:, 2:3]))
                st[n] = [t_e, None]
            if 0 <= n - 1 < 32:
                m = n - 1
                qt, i, j = m % 4, m % 3, m % 2
                nk = (qt + 1) * 128
                V.wait(st[m][0])
                t = V.inc(nc.vector.reciprocal(ms_[i][:, 3:4], ms_[i][:, 2:3]))
                t = ts(V, PB[i][:, 0:nk], PB[i][:, 0:nk], ms_[i][:, 3:4], None, ALU.mult, None, t)
                next(rec, None)
                bank = banks.get(T)
                T.wait(t)
                for k in range(qt + 1):
                    ins = nc.tensor.transpose(bank[:, k * 128:(k + 1) * 128], PB[i][:, k * 128:(k + 1) * 128],
                                              K("ident"))
                t = T.inc(ins)
                f_pb[i] = t
                t = cp(A, PT[j][:, 0:qt + 1, :], bank[:, 0:nk].rearrange("p (k n) -> p k n", k=qt + 1), t, f_pt[j])
                banks.put(bank, t)
                st[m][1] = t
            if 0 <= n - 2:
                m = n - 2
                h, qt, j = m // 4, m % 4, m % 2
                ps = slice(64 * (h % 2), 64 * (h % 2) + 64)
                if qt == 0:
                    bo = banks.get(T)
                T.wait(st[m][1], t_v)
                for k in range(qt + 1):
                    ins = mm(bo[ps, qt * 128:(qt + 1) * 128], VV[:, k, h * 64:(h + 1) * 64], PT[j][:, k, :],
                             start=(k == 0), stop=(k == qt))
                t = T.inc(ins)
                f_pt[j] = t
                if qt == 3:
                    t_mx = cp(V, MX[ps, h // 2, :], bo[ps, :], t)
                    banks.put(bo, t_mx)
        for _r in rec:
            pass
        phase(at_)
        MXh = here("MXh", [128, 8, 512], FR)
        MXl = here("MXl", [128, 8, 512], FR)
        A.wait(T.now())
        V.wait(T.now())
        sp = Splits()
        for c in range(8):
            sp.add(MXh[:, c, :], MXl[:, c, :], MX[:, c, :], t_mx if c < 4 else t_mx2)
        t_m = sp.flush()
        sq = Squares()
        for c in range(8):
            e = ring.get("wo2", c)
            bank = banks.get(T)
            t = feature(bank[:, :], e, MXh, MXl, xt=t_m)
            ring.done(e, t)
            t_x = tt(V, XT[:, c, :], bank[:, :], XT[:, c, :], ALU.add, t)
            banks.put(bank, t_x)
            sq.add(c, t_x)

        def store(c, t):
            S.wait(t)
            d_o.inc(nc.sync.dma_start(outT[:, c, :], XT[:, c, :]))

        ffn("n2", "f21", "f23", "f22", sq, store)
        S.wait(d_o.now())
        return ring.keys, ring2.keys


def program(nc, arrays, plans):
    aps = {n: nc.dram_tensor("in_" + n, a.shape, F32, kind="ExternalInput").ap() for n, a in arrays.items()}
    out = nc.dram_tensor("out_x", (128, 8, 512), F32, kind="ExternalOutput").ap()
    return build(nc, aps, out, plans)


def _chunks(w):
    k, n = w.shape
    return np.ascontiguousarray(w.reshape(k // 128, 128, n // 128, 128).transpose(2, 1, 0, 3)).reshape(
        n // 128, 128, k)


def _rows(w):
    k, n = w.shape
    return np.ascontiguousarray(w.reshape(k // 128, 128, n).transpose(1, 0, 2))


def _cols(v):
    return v.reshape(-1, 128).T


def _constants():
    f = np.float32
    i = np.arange(128)
    m, n = i[:, None], i[None, :]
    km = np.zeros((128, NKM), f)

    def put(name, a):
        a = np.asarray(a, f)
        km[:, KM[name]:KM[name] + a.shape[1]] = a

    put("ident", m == n)
    put("ones", np.ones((128, 128)))
    put("o1024", np.full((128, 128), 1 / 1024))
    put("o2048", np.full((128, 128), 1 / 2048))
    put("hb", (m // 64 == n // 64) / 64)
    put("o128", np.full((128, 128), 1 / 128))
    put("triU", m <= n)
    put("triL", m >= n)
    put("sU", m < n)
    put("sL", m > n)
    put("mF", np.where(n >= m, 0, -1e30))
    put("mB", np.where(n <= m, 0, -1e30))
    md = n % 64
    put("psw", ((md < 8) & (m == n + 8)) | ((md >= 8) & (md < 16) & (m == n - 8)))
    put("iota", np.broadcast_to(n, (128, 128)))
    put("iotag", np.broadcast_to(np.arange(32)[None] // 8, (128, 32)))
    t, k = np.arange(8)[None] // 2, np.arange(8)[None] % 2
    put("tok", t * 128 + m + 1)
    put("aid", (t * 128 + m) * 2 + k + 1)
    put("slot", 1025.0 + m)
    put("eps5", np.full((128, 1), 1e-5))
    put("eps6", np.full((128, 1), 1e-6))
    km[:, KM["hgm"]:KM["hgm"] + 128] = np.where((m // 64 == n // 64) & (m <= n), 1, 0).astype(np.uint32).view(f)
    pos = np.arange(512)
    inv = (f(500000.0) ** (-np.arange(0, 16, 2, dtype=f) / f(16))).astype(f)
    ang = pos.astype(f)[:, None] * inv[None]
    cs = np.zeros((128, 2, 512), f)
    cs[:, 0] = 1
    for p in range(128):
        d = p % 64
        if d < 16:
            cs[p, 0] = np.cos(ang[:, d % 8])
            cs[p, 1] = np.sin(ang[:, d % 8]) * (-1 if d < 8 else 1)
    q, s = pos[:, None], pos[None, :]
    df = q - s
    cnt = ((df >= 0) & (df <= 128)).astype(int) + ((df >= 0) & (df % 4 == 0)) + ((df >= 0) & (df % 16 == 0))
    al = np.where(cnt > 0, np.log(np.maximum(cnt, 1)), -1e30).astype(f).reshape(4, 128, 512).transpose(1, 0, 2)
    rst = np.broadcast_to((pos % 64 != 0).astype(f)[None], (128, 512))
    pm = np.zeros((4, 512, 512), f)
    for g, w in enumerate((2, 4, 8, 16)):
        def win(n_):
            a = np.arange(n_)
            lo, hi = np.clip(a - w // 2, 0, n_), np.clip(a - w // 2 + w, 0, n_)
            return ((a[None] >= lo[:, None]) & (a[None] < hi[:, None])) / (hi - lo)[:, None].astype(np.float64)
        pm[g] = (np.kron(win(8), win(64)) - np.eye(512)).T
    pm = pm.reshape(4, 4, 128, 512).transpose(0, 2, 1, 3)
    c = np.ascontiguousarray
    al = np.concatenate([al[:, i, 0:128 * (i + 1)] for i in range(4)], axis=1)
    return {"km": km, "cs": cs, "al": c(al), "rst": c(rst), "pm": c(pm)}


def _lay_out(x):
    a = {k: np.asarray(v) for k, v in x.items()}
    w_in = a["w_in"][0]
    w2 = a["w_in_2"][0]
    pc = [_cols(a["b_ada"][0]), _cols(a["b_gate"][0]),
          a["conv_w"][0].reshape(5, 24, 128).transpose(2, 1, 0).reshape(128, 120), _cols(a["conv_b"][0]),
          _cols(a["ssd_norm_g"][0]), _cols(a["pool_scale"][0]), _cols(a["ln1_g"][0]), _cols(a["ln1_b"][0]),
          _cols(a["ln2_g"][0]), _cols(a["ln2_b"][0]), _cols(a["ffn1_norm_2"][0]), _cols(a["mix_norm_2"][0]),
          _cols(a["ffn2_norm_2"][0]), np.tile(a["q_norm_2"][0], 2)[:, None], np.tile(a["k_norm_2"][0], 2)[:, None],
          _cols(a["hg_lb_logits_2"][0]), _cols(a["hg_lb_logits_2"][1]), a["hg_out_norm_2"][0][:, None],
          np.stack([_cols(a["c"][0]), _cols(a["c_ctx"])], axis=2).reshape(128, 16)]
    pr = np.concatenate([a["dt_bias"].reshape(-1), a["a_log"].reshape(-1), a["d_skip"].reshape(-1),
                         a["b_router_group"].reshape(-1), a["b_router_expert"].reshape(-1)])
    wre = a["w_router_expert"][0].transpose(1, 0, 2).reshape(1024, 32)
    ab = w2
    r = {
        "pc": np.ascontiguousarray(np.concatenate(pc, axis=1)),
        "pr": np.ascontiguousarray(np.broadcast_to(pr[None], (128, NPR))),
        "xT": _rows(np.ascontiguousarray(a["x"][0].T)), "ctxT": _rows(np.ascontiguousarray(a["ctx"][0].T)),
        "wada": _rows(a["w_ada"][0]), "wdt": _rows(w_in[:, 5120:5184]),
        "wz": _chunks(w_in[:, 0:2048]), "wxbc": _chunks(w_in[:, 2048:5120]),
        "wu": _rows(w_in[:, 5184:6208]), "wg": _chunks(w_in[:, 6208:8256]),
        "pw": _rows(a["pool_w"][0].reshape(1024, 256)),
        "wa": _chunks(a["w_branch_a"][0]), "wb": _chunks(a["w_branch_b"][0]), "wo": _chunks(a["w_out"][0]),
        "wr": _rows(np.concatenate([a["w_router_group"][0], wre], axis=1)),
        "eg": a["w_expert_gate"][0], "eu": a["w_expert_up"][0], "ed": a["w_expert_down"][0],
        "w2in": _chunks(np.concatenate([ab[:, 0:1024], ab[:, 1536:2560], ab[:, 3072:3584]], axis=1)),
        "w2v": _rows(ab[:, 1024:1536]), "w2i": _rows(ab[:, 2560:3072]), "wo2": _chunks(a["w_out_2"][0]),
        "f11": _chunks(a["ffn1_w1_2"][0]), "f13": _chunks(a["ffn1_w3_2"][0]), "f12": _chunks(a["ffn1_w2_2"][0]),
        "f21": _chunks(a["ffn2_w1_2"][0]), "f23": _chunks(a["ffn2_w3_2"][0]), "f22": _chunks(a["ffn2_w2_2"][0]),
    }
    r.update(_constants())
    return r


def kernel(**inputs):
    import concourse.bacc as _bacc
    from concourse.bass_utils import run_bass_kernel_spmd as _run

    arrays = _lay_out(inputs)
    nc = _bacc.Bacc("TRN2", target_bir_lowering=False, num_devices=1)
    plans = program(_bacc.Bacc("TRN2", target_bir_lowering=False, num_devices=1), arrays, None)
    program(nc, arrays, plans)
    r = _run(nc, [{"in_" + k: v for k, v in arrays.items()}], core_ids=[0])
    y = r.results[0]["out_x"]
    return np.ascontiguousarray(y.transpose(2, 1, 0).reshape(1, 512, 1024))
```
